# Optimizing a Trainium2 kernel written in Bass

```python
import jax, jax.numpy as jnp
from jax import lax
import numpy as np

D_MODEL = 1024
BATCH = 1
SEQ = 1024
DEPTH = 1

GRID_W = 64
CTX_LEN = 256

FOURIER_GROUPS = 4
FOURIER_GROUP_DIM = 128
FOURIER_WIDTH = FOURIER_GROUPS * FOURIER_GROUP_DIM
LRU_WIDTH = D_MODEL
LRU_HEADS = 8
LRU_HEAD_DIM = LRU_WIDTH // LRU_HEADS
CONV_WIDTH = 4
CONV_PAD_LEFT = 1
LRU_C = 8.0
IN_WIDTH = FOURIER_WIDTH + 2 * LRU_WIDTH + 2 * D_MODEL
PEER_HEADS = 8
PEER_KEY_DIM = 256
PEER_HALF_DIM = PEER_KEY_DIM // 2
N_KEYS = 128
N_EXPERTS = N_KEYS * N_KEYS
PEER_TOPK = 16
TOKEN_BLOCK = 128
NORM_EPS = 1e-6
POS_BASE = 10000.0

kernel_name = "hybrid_fourier_rglru_peer_dit_block"

def rmsnorm(x, g):
    xf = x.astype(jnp.float32)
    y = xf * lax.rsqrt(jnp.mean(xf * xf, axis=-1, keepdims=True) + NORM_EPS)
    return y.astype(x.dtype) * g

def modulate(h, shift, scale):
    return h * (1.0 + scale) + shift

def adaln(cond, w_mod, b_mod):
    return jnp.split(jax.nn.silu(cond) @ w_mod + b_mod, 6, axis=-1)

def sincos_2d(num_tokens, dim):
    rows = num_tokens // GRID_W
    row = jnp.repeat(jnp.arange(rows, dtype=jnp.float32), GRID_W)
    col = jnp.tile(jnp.arange(GRID_W, dtype=jnp.float32), rows)
    nf = dim // 4
    omega = 1.0 / (POS_BASE ** (jnp.arange(nf, dtype=jnp.float32) / nf))
    er = row[:, None] * omega[None]
    ec = col[:, None] * omega[None]
    return jnp.concatenate([jnp.sin(er), jnp.cos(er), jnp.sin(ec), jnp.cos(ec)], axis=-1)

def fourier_mix(z):
    B, T, _ = z.shape
    zg = z.astype(jnp.float32).reshape(B, T, FOURIER_GROUPS, FOURIER_GROUP_DIM)
    y = jnp.fft.fft2(zg, axes=(1, 3), norm="ortho").real
    return y.reshape(B, T, FOURIER_WIDTH).astype(z.dtype)

def centred_dwconv(z, w, b):
    T = z.shape[1]
    zp = jnp.pad(z, ((0, 0), (CONV_PAD_LEFT, CONV_WIDTH - 1 - CONV_PAD_LEFT), (0, 0)))
    y = b
    for k in range(CONV_WIDTH):
        y = y + zp[:, k:k + T] * w[k]
    return y

def block_diag(z, w):
    B, T, _ = z.shape
    zh = z.reshape(B, T, LRU_HEADS, LRU_HEAD_DIM)
    return jnp.einsum('bthi,hij->bthj', zh, w).reshape(B, T, LRU_WIDTH)

def linear_scan(a, b, h0, reverse):
    def step(h, ab):
        a_t, b_t = ab
        h = a_t * h + b_t
        return h, h
    h_final, hs = lax.scan(step, h0, (jnp.swapaxes(a, 0, 1), jnp.swapaxes(b, 0, 1)), reverse=reverse)
    return jnp.swapaxes(hs, 0, 1), h_final

def rglru_dir(xc, wa, ba, wx, bx, lam, h0, reverse):
    r = jax.nn.sigmoid((block_diag(xc, wa) + ba).astype(jnp.float32))
    i = jax.nn.sigmoid((block_diag(xc, wx) + bx).astype(jnp.float32))
    log_a = -LRU_C * r * jax.nn.softplus(-lam.astype(jnp.float32))
    a = jnp.exp(log_a)
    b = jnp.sqrt(-jnp.expm1(2.0 * log_a)) * (i * xc.astype(jnp.float32))
    return linear_scan(a, b, h0, reverse)

def rglru_bidir(xc, lp, h0_f, h0_b):
    hf, hTf = rglru_dir(xc, lp['lru_wa'][0], lp['lru_ba'][0], lp['lru_wx'][0], lp['lru_bx'][0],
                        lp['lru_lambda'][0], h0_f, False)
    hb, hTb = rglru_dir(xc, lp['lru_wa'][1], lp['lru_ba'][1], lp['lru_wx'][1], lp['lru_bx'][1],
                        lp['lru_lambda'][1], h0_b, True)
    return hf, hb, hTf, hTb

def mixer(h, lp, h0_f, h0_b):
    F, R, D = FOURIER_WIDTH, LRU_WIDTH, D_MODEL
    z = h @ lp['w_in']
    zf, zx, zy, zga, zgb = jnp.split(z, [F, F + R, F + 2 * R, F + 2 * R + D], axis=-1)
    y_a = fourier_mix(zf) @ lp['w_fourier']
    xc = centred_dwconv(zx, lp['conv_w'], lp['conv_b'])
    hf, hb, hTf, hTb = rglru_bidir(xc, lp, h0_f, h0_b)
    y_b = ((hf + hb).astype(h.dtype) * jax.nn.gelu(zy)) @ lp['w_lru_out']
    merged = jax.nn.sigmoid(zga) * y_a + jax.nn.sigmoid(zgb) * y_b
    return merged @ lp['w_out'] + lp['b_out'], hTf, hTb

def context_scan_states(h_c, lp, h0):
    F, R = FOURIER_WIDTH, LRU_WIDTH
    zx = h_c @ lp['w_in'][:, F:F + R]
    xc = centred_dwconv(zx, lp['conv_w'], lp['conv_b'])
    _, _, hTf, hTb = rglru_bidir(xc, lp, h0, h0)
    return hTf, hTb

def peer_block(xb, wq, keys, u_tab, v_tab):
    T = xb.shape[0]
    q = (xb @ wq).reshape(T, PEER_HEADS, 2, PEER_HALF_DIM).astype(jnp.float32)
    s = jnp.einsum('thpd,hpkd->thpk', q, keys.astype(jnp.float32))
    sv, si = lax.top_k(s, PEER_TOPK)
    cand = (sv[:, :, 0, :, None] + sv[:, :, 1, None, :]).reshape(T, PEER_HEADS, PEER_TOPK * PEER_TOPK)
    cidx = (si[:, :, 0, :, None] * N_KEYS + si[:, :, 1, None, :]).reshape(T, PEER_HEADS, PEER_TOPK * PEER_TOPK)
    top_s, pos = lax.top_k(cand, PEER_TOPK)
    eidx = jnp.take_along_axis(cidx, pos, axis=-1)
    g = jax.nn.softmax(top_s, axis=-1)
    u = jnp.take(u_tab, eidx, axis=0)
    act = jax.nn.gelu(jnp.einsum('thkd,td->thk', u, xb).astype(jnp.float32))
    v = jnp.take(v_tab, eidx, axis=0)
    return jnp.einsum('thk,thkd->td', (g * act).astype(xb.dtype), v)

def peer(h, wq, keys, u_tab, v_tab):
    B, T, D = h.shape
    blocks = h.reshape(-1, TOKEN_BLOCK, D)
    out = lax.map(lambda xb: peer_block(xb, wq, keys, u_tab, v_tab), blocks)
    return out.reshape(B, T, D)

def setup_inputs(seed: int = 0) -> dict:
    key = jax.random.key(seed)
    ks = jax.random.split(key, 26)
    D, F, R, L = D_MODEL, FOURIER_WIDTH, LRU_WIDTH, DEPTH
    nrm = lambda k, shape, s: jax.random.normal(k, shape, jnp.float32) * s
    a0 = jax.random.uniform(ks[16], (L, 2, R), jnp.float32, 0.9, 0.999)
    return {
        'x': nrm(ks[0], (BATCH, SEQ, D), 1.0),
        'c': nrm(ks[1], (BATCH, D), 1.0),
        'ctx': nrm(ks[2], (BATCH, CTX_LEN, D), 1.0),
        'c_ctx': nrm(ks[3], (D,), 1.0),
        'w_mod': nrm(ks[4], (L, D, 6 * D), D ** -0.5),
        'b_mod': nrm(ks[5], (L, 6 * D), 0.01),
        'norm1_g': 1.0 + nrm(ks[6], (L, D), 0.05),
        'norm2_g': 1.0 + nrm(ks[7], (L, D), 0.05),
        'w_in': nrm(ks[8], (L, D, IN_WIDTH), D ** -0.5),
        'w_fourier': nrm(ks[9], (L, F, D), F ** -0.5),
        'conv_w': nrm(ks[10], (L, CONV_WIDTH, R), CONV_WIDTH ** -0.5),
        'conv_b': nrm(ks[11], (L, R), 0.01),
        'lru_wa': nrm(ks[12], (L, 2, LRU_HEADS, LRU_HEAD_DIM, LRU_HEAD_DIM), LRU_HEAD_DIM ** -0.5),
        'lru_ba': nrm(ks[13], (L, 2, R), 0.01),
        'lru_wx': nrm(ks[14], (L, 2, LRU_HEADS, LRU_HEAD_DIM, LRU_HEAD_DIM), LRU_HEAD_DIM ** -0.5),
        'lru_bx': nrm(ks[15], (L, 2, R), 0.01),
        'lru_lambda': jnp.log(a0) - jnp.log1p(-a0),
        'w_lru_out': nrm(ks[17], (L, R, D), R ** -0.5),
        'w_out': nrm(ks[18], (L, D, D), D ** -0.5),
        'b_out': nrm(ks[19], (L, D), 0.01),
        'peer_wq': nrm(ks[20], (L, D, PEER_HEADS * PEER_KEY_DIM), D ** -0.5),
        'peer_keys': nrm(ks[21], (L, PEER_HEADS, 2, N_KEYS, PEER_HALF_DIM), PEER_HALF_DIM ** -0.5),
        'peer_u': nrm(ks[22], (L, N_EXPERTS, D), D ** -0.5),
        'peer_v': nrm(ks[23], (L, N_EXPERTS, D), 1.0),
        'final_g': 1.0 + nrm(ks[24], (D,), 0.05),
    }

def reference(x, c, ctx, c_ctx, w_mod, b_mod, norm1_g, norm2_g, w_in, w_fourier, conv_w, conv_b,
              lru_wa, lru_ba, lru_wx, lru_bx, lru_lambda, w_lru_out, w_out, b_out,
              peer_wq, peer_keys, peer_u, peer_v, final_g):
    B, S, D = x.shape
    x = x + sincos_2d(S, D).astype(x.dtype)[None]
    zeros = jnp.zeros((B, LRU_WIDTH), jnp.float32)
    for layer in range(DEPTH):
        is_last = layer == DEPTH - 1
        lp = {
            'w_in': w_in[layer], 'w_fourier': w_fourier[layer],
            'conv_w': conv_w[layer], 'conv_b': conv_b[layer],
            'lru_wa': lru_wa[layer], 'lru_ba': lru_ba[layer],
            'lru_wx': lru_wx[layer], 'lru_bx': lru_bx[layer], 'lru_lambda': lru_lambda[layer],
            'w_lru_out': w_lru_out[layer], 'w_out': w_out[layer], 'b_out': b_out[layer],
        }
        sh1, sc1, g1, sh2, sc2, g2 = adaln(c, w_mod[layer], b_mod[layer])
        csh1, csc1, cg1, csh2, csc2, cg2 = adaln(c_ctx, w_mod[layer], b_mod[layer])

        h_c = modulate(rmsnorm(ctx, norm1_g[layer]), csh1, csc1)
        if is_last:
            hTf, hTb = context_scan_states(h_c, lp, zeros)
        else:
            ctx_mix, hTf, hTb = mixer(h_c, lp, zeros, zeros)
            ctx = ctx + cg1 * ctx_mix
            h2c = modulate(rmsnorm(ctx, norm2_g[layer]), csh2, csc2)
            ctx = ctx + cg2 * peer(h2c, peer_wq[layer], peer_keys[layer], peer_u[layer], peer_v[layer])

        h = modulate(rmsnorm(x, norm1_g[layer]), sh1[:, None], sc1[:, None])
        mix, _, _ = mixer(h, lp, hTf, hTb)
        x = x + g1[:, None] * mix
        h2 = modulate(rmsnorm(x, norm2_g[layer]), sh2[:, None], sc2[:, None])
        x = x + g2[:, None] * peer(h2, peer_wq[layer], peer_keys[layer], peer_u[layer], peer_v[layer])
    return rmsnorm(x, final_g)


_drawn_inputs = setup_inputs


def setup_inputs(seed=0):
    import zlib

    import numpy as np

    out = dict(_drawn_inputs(seed))
    spreads = {}
    factors = {'lru_ba': 6.913, 'lru_bx': 5.173, 'b_out': 3.459}
    for name, (base, spread) in spreads.items():
        noise = np.random.default_rng([zlib.crc32(name.encode()), seed]).standard_normal(out[name].shape)
        drawn = base * np.exp(spread * noise) if base else spread * noise
        out[name] = __import__('jax').numpy.asarray(drawn.astype(out[name].dtype))
    for name, factor in factors.items():
        out[name] = (out[name] * factor).astype(out[name].dtype)
    return out
```

```python
import concourse.bass as bass
from concourse import mybir
from contextlib import ExitStack


def build_block(nc, t_in, mod_dram, x1_dram, out):
    f32, bf16, u32 = mybir.dt.float32, mybir.dt.bfloat16, mybir.dt.uint32
    ALU, ACT, AXX = mybir.AluOpType, mybir.ActivationFunctionType, mybir.AxisListType.X
    ds = bass.ds

    P = 128
    T, D = out.shape
    TC = t_in["ctx"].shape[0]
    KD = D // P
    NT = T // P
    NTC = TC // P
    G = t_in["wf"].shape[2]
    R = t_in["lru_gates"].shape[0]
    TA = TC + T
    H = 512
    NH = T // H
    MC = t_in["w_mod"].shape[0]
    PH = t_in["keys"].shape[1] // 2
    NK = t_in["keys"].shape[2]
    TOPK = 16
    RING = 8
    BATCH = 4
    NB = TOPK // BATCH
    EPS = 1e-6
    LRU_C = 8.0
    NEG = -3.0e38
    WSLOT = 3584
    ZX0, ZY0, ZGA0, ZGB0 = G, G + R, G + 2 * R, G + 2 * R + KD

    ctx = ExitStack()
    with ctx:
        def sb(name, shape, dt=f32):
            return ctx.enter_context(nc.sbuf_tensor(name, shape, dt))

        def sem(name):
            return ctx.enter_context(nc.semaphore(name))

        xs = sb("xs", [P, NT, D])
        lru = sb("lru", [P, 9 * 1288])
        hT = sb("hT", [P, KD, TA])
        ybT = sb("ybT", [P, KD, T])
        yT = sb("yT", [P, G, T])
        wgt = sb("wgt", [P, 2 * WSLOT])

        consts = sb("consts", [P, P + 2 * P + TOPK])
        ident, dft_chan, iota = consts[:, 0:P], consts[:, P:3 * P], consts[:, 3 * P:3 * P + TOPK]
        head_vecs = sb("head_vecs", [P, 12, R])
        c_cols = sb("c_cols", [P, KD, 2])
        c_silu = sb("c_silu", [P, KD, 2])
        mod_cols = sb("mod_cols", [P, 4, KD])
        gain1 = sb("gain1", [P, 2, KD])
        lam = sb("lam", [P, 8, 2 * R])
        ssq = sb("ssq", [P, NT + NTC])
        rstd = sb("rstd", [P, NT + NTC])
        zero = sb("zero", [P, P])
        small = sb("small", [P, 8])
        s_sb = sb("s_sb", [P, 2, NK])
        s_rep = sb("s_rep", [P, NK])
        cand = sb("cand", [P, TOPK, TOPK])
        cand_rep = sb("cand_rep", [P, TOPK, TOPK])
        q_sb = sb("q_sb", [P, 2 * P])
        qT_sb = sb("qT_sb", [P, 2, P])
        key_val = sb("key_val", [P, 2, TOPK])
        key_idx = sb("key_idx", [P, 2, TOPK], u32)
        key_idxf = sb("key_idxf", [P, 2, TOPK])
        top_val = sb("top_val", [P, TOPK])
        top_pos = sb("top_pos", [P, TOPK], u32)
        top_ab = sb("top_ab", [P, 2, TOPK], u32)
        top_abf = sb("top_abf", [P, 2, TOPK])
        picked = sb("picked", [P, 2, TOPK])
        top_exp = sb("top_exp", [P, TOPK])
        soft = sb("soft", [P, 4])
        dots = sb("dots", [P, TOPK])
        gact = sb("gact", [P, BATCH])
        wrow = sb("wrow", [P, BATCH])
        diag = sb("diag", [P, BATCH, P])
        idx_stage = sb("idx_stage", [P, TOPK], u32)
        sq_junk = sb("sq_junk", [P, D], bf16)

        pos_row = lru[:, 0:NT * H].rearrange("p (i n) -> p i n", i=NT)
        pos_col = lru[:, 4096:4608]
        mod_stage = lru[:, 4608:5632].rearrange("p (b n) -> p b n", b=2)
        w_mod_ring = ybT[:, :, :].rearrange("p a n -> p (a n)").rearrange("p (b k n) -> p b k n", b=2, k=KD)
        b_mod = hT[:, :, :].rearrange("p a n -> p (a n)")[0:2, 0:MC * H]
        xhat = yT[:, 0:2, :]
        ctx_raw = yT[:, 2:2 + NTC, :]
        zfT = yT[:, 0, :]
        PQ = lru[:, 0:NT * G * 2 * P].rearrange("p (t g n) -> p t g n", t=NT, g=G)

        def wview(u, at, k):
            return wgt[:, u * WSLOT + at:u * WSLOT + at + k * P].rearrange("p (k n) -> p k n", k=k)

        w_a = [wview(u, 0, KD) for u in range(2)]
        w_b = [wview(u, 1024, KD) for u in range(2)]
        w_g = [wview(u, 2048, 4) for u in range(2)]
        w_l = [wview(u, 2048, KD) for u in range(2)]
        w_f = [wview(u, 3072, G) for u in range(2)]
        dft_t = [wgt[:, u * WSLOT + 1024:u * WSLOT + 3072].rearrange("p (c n) -> p c n", c=2) for u in range(2)]

        def larr(i):
            return lru[:, i * 1288:i * 1288 + TA]
        zpad = lru[:, 8 * 1288:8 * 1288 + TA + 6]
        ZL = TC + 3
        xc, tmp = larr(0), larr(1)
        rg, ig, ag = [larr(2), larr(3)], [larr(4), larr(5)], [larr(6), larr(7)]
        merged = lru[:, 0:KD * T].rearrange("p (k n) -> p k n", k=KD)
        sig_a, sig_b = lru[:, 8192:9216], lru[:, 9216:10240]
        merged_tile = [lru[:, 8192 + 1024 * u:9216 + 1024 * u].rearrange("p (k n) -> p k n", k=KD) for u in range(2)]
        mix_tmp = lru[:, 10240:11264]
        w_out_k = [yT[:, k, :] for k in range(4)] + [wgt[:, k * D:(k + 1) * D] for k in range(4)]
        gate1_row, bout_row = wgt[:, 4096:5120], wgt[:, 5120:6144]

        hT_flat = hT[:, :, :].rearrange("p a n -> p (a n)")
        ybT_flat = ybT[:, :, :].rearrange("p a n -> p (a n)")
        wq_k = [hT_flat[:, k * 2048:(k + 1) * 2048] for k in range(5)] + \
               [ybT_flat[:, k * 2048:(k + 1) * 2048] for k in range(3)]
        keys_T = ybT_flat[:, 6144:8192].rearrange("p (m n) -> p m n", m=2 * PH)
        ring = [xs[:, 2 * s:2 * s + 2, :].rearrange("p a n -> p (a n)") for s in range(4)] + \
               [lru[:, s * 2 * D:(s + 1) * 2 * D] for s in range(4)]
        dot_junk = lru[:, 8192:9216].bitcast(bf16).rearrange("p (b n) -> p b n", b=2)
        eidx = lru[:, 9216:10240].bitcast(u32)
        gates = lru[:, 10240:11264]
        gain2_row, shift2_row, gate2_row, final_row = (yT[:, j, :] for j in range(4))
        h2T = wgt[:, 0:1024].rearrange("p (k n) -> p k n", k=KD)
        h2_next, h2_cur, x1_front, x1_end, acc_sb, norm2_row = (wgt[:, j * D:(j + 1) * D] for j in range(1, 7))

        bank = [ctx.enter_context(nc.psum_tensor(f"bank{i}", [P, H], f32)) for i in range(8)]

        setup_loaded = sem("setup_loaded")
        x_loaded = sem("x_loaded")
        silu_done = sem("silu_done")
        w_mod_loaded = [sem("w_mod_loaded0"), sem("w_mod_loaded1")]
        mod_matmul = sem("mod_matmul")
        mod_rows = sem("mod_rows")
        mod_stored = [sem("mod_stored0"), sem("mod_stored1")]
        mod_cols_loaded = sem("mod_cols_loaded")
        pos_added = sem("pos_added")
        squares = sem("squares")
        means = sem("means")
        roots = sem("roots")
        lam_dve = sem("lam_dve")
        lam_act = sem("lam_act")
        xhat_ready = sem("xhat_ready")
        x_transposed = sem("x_transposed")
        h_act = sem("h_act")
        h_dve = sem("h_dve")
        w_loaded = [sem("w_loaded0"), sem("w_loaded1")]
        w_used = sem("w_used")
        dft_loaded = [sem("dft_loaded0"), sem("dft_loaded1")]
        dft_used = sem("dft_used")
        zf_done = sem("zf_done")
        zf_copied = sem("zf_copied")
        pq_done = sem("pq_done")
        pq_copied = sem("pq_copied")
        y_done = sem("y_done")
        y_copied = sem("y_copied")
        zx_done = sem("zx_done")
        zx_copied = sem("zx_copied")
        zy_done = sem("zy_done")
        zy_read = sem("zy_read")
        conv_started = sem("conv_started")
        conv_done = sem("conv_done")
        gate_done = sem("gate_done")
        gate_read = sem("gate_read")
        gx_done = sem("gx_done")
        decay_done = sem("decay_done")
        norm_ready = sem("norm_ready")
        norm_root = sem("norm_root")
        yb_ready = sem("yb_ready")
        ga_done, ya_done, gb_done, yb_done = sem("ga_done"), sem("ya_done"), sem("gb_done"), sem("yb_done")
        ga_read, gb_read = sem("ga_read"), sem("gb_read")
        ya_read, yb_read = sem("ya_read"), sem("yb_read")
        merge_done = sem("merge_done")
        w_out_loaded = sem("w_out_loaded")
        bout_gated = sem("bout_gated")
        tile_staged = sem("tile_staged")
        bias_added = sem("bias_added")
        mix_done = sem("mix_done")
        x1_ready = sem("x1_ready")
        x1_stored = sem("x1_stored")
        wq_loaded = sem("wq_loaded")
        rows_loaded = sem("rows_loaded")
        x1_front_loaded = sem("x1_front_loaded")
        x1_end_loaded = sem("x1_end_loaded")
        sq2_done = sem("sq2_done")
        mean2_done = sem("mean2_done")
        root2_done = sem("root2_done")
        h2_ready = sem("h2_ready")
        h2_transposed = sem("h2_transposed")
        h2T_ready = sem("h2T_ready")
        q_done = sem("q_done")
        q_copied = sem("q_copied")
        qT_done = sem("qT_done")
        qT_copied = sem("qT_copied")
        score_done = sem("score_done")
        score_copied = sem("score_copied")
        max_ready = sem("max_ready")
        exp_done = sem("exp_done")
        picks_done = sem("picks_done")
        landed = [sem(f"landed{s}") for s in range(RING)]
        ring_free = sem("ring_free")
        idx_staged = sem("idx_staged")
        dots_done = sem("dots_done")
        diag_done = sem("diag_done")
        acc_done = sem("acc_done")
        acc_copied = sem("acc_copied")
        y_squared = sem("y_squared")
        mean3_done = sem("mean3_done")
        root3_done = sem("root3_done")
        out_ready = sem("out_ready")
        out_stored = sem("out_stored")

        SETUP = 5

        block = ctx.enter_context(nc.Block())

        @block.sync
        def _(sp):
            sp.dma_start(consts[:, :], t_in["consts"]).then_inc(setup_loaded, 16)
            sp.dma_start(c_cols[:, :, :], t_in["c_cols"]).then_inc(setup_loaded, 16)
            sp.dma_start(head_vecs[:, :, :], t_in["head_vecs"]).then_inc(setup_loaded, 16)
            for r in range(2):
                sp.dma_start(b_mod[r:r + 1, :], t_in["b_mod"]).then_inc(setup_loaded, 16)
            for u in range(2):
                sp.dma_start(w_mod_ring[:, u], t_in["w_mod"][u]).then_inc(w_mod_loaded[u], 16)
            xv = t_in["x"].rearrange("(i p) n -> p i n", p=P)
            for j in range(2):
                sp.dma_start(xs[:, 4 * j:4 * j + 4, :], xv[:, 4 * j:4 * j + 4, :]).then_inc(x_loaded, 16)
            sp.dma_start(pos_row, t_in["pos_row"].rearrange("(i p) n -> p i n", p=P)).then_inc(x_loaded, 16)
            sp.dma_start(pos_col, t_in["pos_col"]).then_inc(x_loaded, 16)
            sp.dma_start(ctx_raw, t_in["ctx"].rearrange("(i p) n -> p i n", p=P)).then_inc(x_loaded, 16)
            with sp.Fori(0, MC // 2 - 1) as n:
                for u in range(2):
                    sp.wait_ge(mod_rows, 2 * n + u + 1)
                    sp.dma_start(mod_dram[:, ds((2 * n + u) * H, H)], mod_stage[0:2, u, :]).then_inc(mod_stored[u], 16)
                    sp.wait_ge(mod_matmul, 2 * n + u + 1)
                    sp.dma_start(w_mod_ring[:, u], t_in["w_mod"][ds(2 * n + u + 2, 1)].rearrange("a p k n -> (a p) k n"))\
                        .then_inc(w_mod_loaded[u], 16)
            for u in range(2):
                sp.wait_ge(mod_rows, MC - 2 + u + 1)
                sp.dma_start(mod_dram[:, (MC - 2 + u) * H:(MC - 1 + u) * H], mod_stage[0:2, u, :])\
                    .then_inc(mod_stored[u], 16)
            for u in range(2):
                sp.dma_start(w_a[u], t_in["w_in"][u]).then_inc(w_loaded[u], 16)
                sp.dma_start(dft_t[u], t_in["dft_time"][u]).then_inc(dft_loaded[u], 16)
            for u in range(2):
                sp.wait_ge(mod_stored[u], 16 * (MC // 2))
            for j in range(2):
                for r in range(2):
                    sp.dma_start(mod_cols[:, 2 * j + r, :],
                                 mod_dram[r:r + 1, j * D:(j + 1) * D].rearrange("a (k p) -> p (a k)", p=P),
                                 allow_slow_non_contiguous=True)\
                        .then_inc(mod_cols_loaded, 16)
            for g in range(2, G):
                sp.wait_ge(w_used, g - 1)
                sp.dma_start(w_a[g % 2], t_in["w_in"][g]).then_inc(w_loaded[g % 2], 16)
            for t in range(2, NT):
                sp.wait_ge(dft_used, t - 1)
                sp.dma_start(dft_t[t % 2], t_in["dft_time"][t]).then_inc(dft_loaded[t % 2], 16)
            sp.wait_ge(dft_used, NT)
            with sp.Fori(0, R // 2) as n:
                for u in range(2):
                    sp.wait_ge(w_used, G + 2 * n + u - 1)
                    r = 2 * n + u
                    for dst, src, at in ((w_a[u], "w_in", ZX0), (w_b[u], "w_in", ZY0), (w_g[u], "lru_gates", 0)):
                        sp.dma_start(dst, t_in[src][ds(r + at, 1)].rearrange("a p k n -> (a p) k n"))\
                            .then_inc(w_loaded[u], 16)
            with sp.Fori(0, KD // 2) as n:
                for u in range(2):
                    sp.wait_ge(w_used, G + R + 2 * n + u - 1)
                    d = 2 * n + u
                    for dst, src, at in ((w_a[u], "w_in", ZGA0), (w_b[u], "w_in", ZGB0), (w_l[u], "wl", 0), (w_f[u], "wf", 0)):
                        sp.dma_start(dst, t_in[src][ds(d + at, 1)].rearrange("a p k n -> (a p) k n"))\
                            .then_inc(w_loaded[u], 16)
            sp.wait_ge(w_used, G + R + KD)
            for k in range(KD):
                sp.dma_start(w_out_k[k], t_in["w_out"][k * P:(k + 1) * P, :]).then_inc(w_out_loaded, 16)
            sp.dma_start(gate1_row, mod_dram[0:1, 2 * D:3 * D].to_broadcast([P, D])).then_inc(w_out_loaded, 16)
            sp.dma_start(bout_row, t_in["b_out"].to_broadcast([P, D])).then_inc(w_out_loaded, 16)
            for k in range(KD):
                sp.dma_start(wq_k[k], t_in["wq"][k * P:(k + 1) * P, :]).then_inc(wq_loaded, 16)
            sp.dma_start(keys_T, t_in["keys"]).then_inc(wq_loaded, 16)
            with sp.Fori(0, NT) as i:
                sp.wait_ge(x1_ready, i + 1)
                sp.dma_start(x1_dram[ds(i * P, P), :], xs[:, ds(i, 1), :].rearrange("p a n -> p (a n)"))\
                    .then_inc(x1_stored, 16)
            sp.wait_ge(mix_done, NT + 2)
            for dst, src in ((gain2_row, mod_dram[0:1, 4 * D:5 * D]), (shift2_row, mod_dram[0:1, 3 * D:4 * D]),
                             (gate2_row, mod_dram[0:1, 5 * D:6 * D]), (final_row, t_in["final_g"]),
                             (norm2_row, t_in["norm2_g"])):
                sp.dma_start(dst, src.to_broadcast([P, D])).then_inc(rows_loaded, 16)
            sp.wait_ge(x1_stored, 16 * NT)
            sp.dma_start(x1_front, x1_dram[0:P, :]).then_inc(x1_front_loaded, 16)
            sp.wait_ge(h2_ready, 1)
            sp.dma_start(x1_front, x1_dram[P:2 * P, :]).then_inc(x1_front_loaded, 16)

            def tile_io(i, first, fetch):
                if not first:
                    sp.wait_ge(out_ready, i)
                    sp.dma_start(out[ds((i - 1) * P, P), :], x1_end).then_inc(out_stored, 16)
                    sp.wait_ge(out_stored, 16 * i)
                sp.dma_start(x1_end, x1_dram[ds(i * P, P), :]).then_inc(x1_end_loaded, 16)
                if fetch:
                    sp.wait_ge(h2_ready, i + 2)
                    sp.dma_start(x1_front, x1_dram[ds((i + 2) * P, P), :]).then_inc(x1_front_loaded, 16)

            tile_io(0, True, True)
            with sp.Fori(1, NT - 2) as i:
                tile_io(i, False, True)
            tile_io(NT - 2, False, False)
            tile_io(NT - 1, False, False)
            sp.wait_ge(out_ready, NT)
            sp.dma_start(out[(NT - 1) * P:NT * P, :], x1_end).then_inc(out_stored, 16)
            sp.wait_ge(out_stored, 16 * NT)

        @block.gpsimd
        def _(pool):
            pool.sem_inc(zx_copied, 1)
            pool.sem_inc(zy_read, 1)
            pool.sem_inc(gate_read, 3)
            pool.sem_inc(conv_done, 1)
            pool.sem_inc(gx_done, 1)
            pool.sem_inc(ga_read, 1)
            pool.sem_inc(gb_read, 1)
            pool.sem_inc(ya_read, 1)
            pool.sem_inc(yb_read, 1)
            pool.sem_inc(merge_done, 1)
            pool.sem_inc(mix_done, 2)
            pool.sem_inc(h2_transposed, 1)
            pool.sem_inc(h2T_ready, 1)
            pool.sem_inc(q_copied, 1)
            pool.sem_inc(qT_copied, 1)
            pool.sem_inc(score_copied, 1)
            pool.sem_inc(acc_copied, 1)
            pool.sem_inc(ring_free, RING)
            pool.wait_ge(x_loaded, 16 * 5)
            with pool.Fori(0, NT) as i:
                xt = xs[:, ds(i, 1), :].rearrange("p a n -> p (a n)")
                pr = pos_row[:, ds(i, 1), :].rearrange("p a n -> p (a n)")
                nc.gpsimd.tensor_tensor(xt[:, 0:H], xt[:, 0:H], pr, ALU.add)
                nc.gpsimd.tensor_tensor(xt[:, H:D], xt[:, H:D], pos_col, ALU.add).then_inc(pos_added, 1)
            pool.wait_ge(merge_done, KD + 1)
            pool.wait_ge(bout_gated, 1)
            with pool.Fori(0, NT // 2) as n:
                for u in range(2):
                    i = 2 * n + u
                    pool.wait_ge(mix_done, i + 1)
                    pool.nop(nofuse=True)
                    nc.gpsimd.tensor_copy(merged_tile[u], merged[:, :, ds(i * P, P)]).then_inc(tile_staged, 1)
                    xt = xs[:, ds(i, 1), :].rearrange("p a n -> p (a n)")
                    nc.gpsimd.tensor_tensor(xt, xt, bout_row, ALU.add).then_inc(bias_added, 1)
            pool.wait_ge(x1_stored, 16 * NT)
            pool.wait_ge(mix_done, NT + 2)
            with pool.Fori(0, NT * PH) as j:
                pool.wait_ge(picks_done, j + 1)
                pool.nop(nofuse=True)
                for k in range(TOPK):
                    if k % RING == 0:
                        nc.gpsimd.tensor_copy(idx_stage[:, k:k + RING], eidx[:, ds(j * TOPK + k, RING)])\
                            .then_inc(idx_staged, 1)
                        pool.wait_ge(idx_staged, 2 * j + k // RING + 1)
                        pool.nop(nofuse=True)
                    pool.wait_ge(ring_free, j * TOPK + k + 1)
                    pool.nop(nofuse=True)
                    pool.indirect_dma_start(
                        out=ring[k % RING], out_offset=None, in_=t_in["uv"],
                        in_offset=bass.IndirectOffsetOnAxis(ap=idx_stage[:, k:k + 1], axis=0))\
                        .then_inc(landed[k % RING], 16)

        @block.scalar
        def _(act):
            act.wait_ge(setup_loaded, 16 * SETUP)
            nc.scalar.activation(c_silu[:, :, :], c_cols[:, :, :], ACT.Silu).then_inc(silu_done, 1)
            act.wait_ge(lam_dve, 1)
            nc.scalar.activation(lam[:, 1, :], lam[:, 0, :], ACT.Exp, scale=-1.0).then_inc(lam_act, 1)
            act.wait_ge(lam_dve, 2)
            nc.scalar.activation(lam[:, 3, :], lam[:, 2, :], ACT.Ln).then_inc(lam_act, 1)
            with act.Fori(0, NT) as i:
                act.wait_ge(pos_added, i + 1)
                act.nop(nofuse=True)
                nc.scalar.activation(sq_junk[:, :], xs[:, ds(i, 1), :].rearrange("p a n -> p (a n)"), ACT.Square,
                                     accum_out=ssq[:, ds(i, 1)])
                act.drain()
            for i in range(NTC):
                last = nc.scalar.activation(sq_junk[:, :], ctx_raw[:, i, :], ACT.Square,
                                            accum_out=ssq[:, NT + i:NT + i + 1])
                act.drain()
            nc.scalar.activation(small[:, 7:8], ident[:, 0:1], ACT.Copy).then_inc(squares, 1)
            act.wait_ge(means, 1)
            nc.scalar.activation(rstd[:, :], ssq[:, :], ACT.Sqrt).then_inc(roots, 1)
            act.wait_ge(lam_dve, 4)

            def modulate(t, u, which, col):
                act.wait_ge(x_transposed, t + 1)
                act.nop(nofuse=True)
                for k in range(4):
                    last = nc.scalar.activation(hT[:, k, col], bank[2 * u][:, k * P:(k + 1) * P], ACT.Identity,
                                                scale=gain1[:, which, k:k + 1], bias=mod_cols[:, which, k:k + 1])
                last.then_inc(h_act, 1)

            for i in range(NTC):
                modulate(i, i, 1, slice(i * P, (i + 1) * P))
            with act.Fori(0, NT // 2) as n:
                for u in range(2):
                    modulate(NTC + 2 * n + u, u, 0, ds(TC + (2 * n + u) * P, P))
            with act.Fori(0, G) as g:
                act.wait_ge(zf_done, g + 1)
                nc.scalar.activation(zfT[:, 0:H], bank[0][:, :], ACT.Copy).then_inc(zf_copied, 1)
                act.wait_ge(pq_done, g + 1)
                act.nop(nofuse=True)
                for j in range(2):
                    last = nc.scalar.activation(PQ[:, 2 * j:2 * j + 2, ds(g, 1), :].rearrange("p t a n -> p t (a n)"),
                                                bank[4 + j][:, :].rearrange("p (t n) -> p t n", t=2), ACT.Copy)
                last.then_inc(pq_copied, 1)
            act.wait_ge(y_done, 1)
            for g in range(G):
                last = nc.scalar.activation(yT[:, g, 0:H], bank[2 * g][:, :], ACT.Copy)
            last.then_inc(y_copied, 1)
            act.wait_ge(lam_dve, 5)
            with act.Fori(0, R) as r:
                act.wait_ge(zx_done, r + 1)
                act.wait_ge(conv_done, r + 1)
                nc.scalar.activation(zpad[:, 1:1 + TC], bank[2][:, 0:TC], ACT.Copy)
                for j in range(NH):
                    last = nc.scalar.activation(zpad[:, ZL + 1 + j * H:ZL + 1 + (j + 1) * H], bank[j][:, :], ACT.Copy)
                last.then_inc(zx_copied, 1)
                act.drain()
                act.wait_ge(gx_done, r + 1)
                act.nop(nofuse=True)
                w0, cb = head_vecs[:, 0, ds(r, 1)], head_vecs[:, 4, ds(r, 1)]
                nc.scalar.activation(xc[:, 0:TC], zpad[:, 0:TC], ACT.Identity, scale=w0, bias=cb)
                nc.scalar.activation(xc[:, TC:TA], zpad[:, ZL:ZL + T], ACT.Identity, scale=w0, bias=cb)\
                    .then_inc(conv_started, 1)
                act.wait_ge(zy_done, r + 1)
                act.nop(nofuse=True)
                yb_r = ybT[:, ds(r, 1), :].rearrange("p a n -> p (a n)")
                for j in range(NH):
                    last = nc.scalar.activation(yb_r[:, j * H:(j + 1) * H], bank[3 + j][:, :], ACT.Gelu_apprx_tanh)
                last.then_inc(zy_read, 1)
                pieces = [(0, TC), (TC, TC + H), (TC + H, TA)]
                for m, dst in enumerate((rg[0], ig[0], rg[1], ig[1])):
                    for p, (a, b) in enumerate(pieces):
                        act.wait_ge(gate_done, 12 * r + 3 * m + p + 1)
                        act.nop(nofuse=True)
                        nc.scalar.activation(dst[:, a:b], bank[5 + p][:, 0:b - a], ACT.Sigmoid,
                                             bias=head_vecs[:, 5 + m, ds(r, 1)]).then_inc(gate_read, 1)
                act.drain()
                for v in range(2):
                    nc.scalar.activation(ag[v], rg[v], ACT.Exp, scale=lam[:, 6, ds(v * R + r, 1)])
                act.drain()
                for v in range(2):
                    nc.scalar.activation(rg[v], rg[v], ACT.Tanh, scale=lam[:, 7, ds(v * R + r, 1)]).then_inc(decay_done, 1)
                for v in range(2):
                    act.wait_ge(norm_ready, 2 * r + v + 1)
                    nc.scalar.activation(rg[v], rg[v], ACT.Sqrt).then_inc(norm_root, 1)
            act.wait_ge(yb_ready, R)
            with act.Fori(0, KD) as d:
                for done, read, dst, b0 in ((ga_done, ga_read, sig_a, 0), (gb_done, gb_read, sig_b, 4)):
                    act.wait_ge(done, d + 1)
                    act.wait_ge(merge_done, d + 1)
                    for j in range(NH):
                        last = nc.scalar.activation(dst[:, j * H:(j + 1) * H], bank[b0 + j][:, :], ACT.Sigmoid)
                    last.then_inc(read, 1)

            def square_front(i):
                act.wait_ge(x1_front_loaded, 16 * (i + 1))
                nc.scalar.activation(sq_junk[:, :], x1_front, ACT.Square, accum_out=small[:, 0:1]).then_inc(sq2_done, 1)
                act.wait_ge(mean2_done, i + 1)
                nc.scalar.activation(small[:, 1:2], small[:, 1:2], ACT.Sqrt).then_inc(root2_done, 1)

            def copy_h2T(i):
                act.wait_ge(h2_transposed, i + 2)
                for j in range(2):
                    last = nc.scalar.activation(h2T[:, 4 * j:4 * j + 4, :].rearrange("p k n -> p (k n)"), bank[2 + j][:, :],
                                                ACT.Copy)
                last.then_inc(h2T_ready, 1)

            def copy_q(f):
                act.wait_ge(q_done, f + 1)
                nc.scalar.activation(q_sb[:, :], bank[4][:, 0:2 * P], ACT.Copy).then_inc(q_copied, 1)

            def copy_qT(f):
                act.wait_ge(qT_done, f + 1)
                nc.scalar.activation(qT_sb[:, :, :].rearrange("p a n -> p (a n)"), bank[5][:, 0:2 * P], ACT.Copy)\
                    .then_inc(qT_copied, 1)

            def soft_exp(f):
                act.wait_ge(max_ready, f + 1)
                nc.scalar.activation(top_exp[:, :], top_val[:, :], ACT.Exp, bias=soft[:, 0:1],
                                     accum_out=soft[:, 1:2]).then_inc(exp_done, 1)

            def weigh(j, b):
                act.wait_ge(dots_done, NB * j + b + 1)
                nc.scalar.activation(gact[:, :], dots[:, b * BATCH:(b + 1) * BATCH], ACT.Gelu_apprx_tanh)
                act.drain()
                for k in range(BATCH):
                    nc.scalar.activation(wrow[:, k:k + 1], gact[:, k:k + 1], ACT.Copy,
                                         scale=gates[:, ds(j * TOPK + b * BATCH + k, 1)])
                act.drain()
                for k in range(BATCH):
                    act.wait_ge(ring_free, j * TOPK + b * BATCH + k + 1 + RING - BATCH)
                    nc.scalar.activation(diag[:, k, :], ident, ACT.Copy, scale=wrow[:, k:k + 1]).then_inc(diag_done, 1)

            def copy_acc(i):
                act.wait_ge(acc_done, i + 1)
                for h in range(2):
                    last = nc.scalar.activation(acc_sb[:, h * H:(h + 1) * H], bank[h][:, :], ACT.Copy)
                last.then_inc(acc_copied, 1)

            def root_end(i):
                act.wait_ge(mean3_done, i + 1)
                nc.scalar.activation(small[:, 4:5], small[:, 4:5], ACT.Sqrt).then_inc(root3_done, 1)

            def tile_body(i, first, last):
                if not last:
                    square_front(i + 1)
                if not first:
                    copy_acc(i - 1)
                if not last:
                    copy_h2T(i + 1)
                if not first:
                    root_end(i - 1)
                with act.Fori(0, PH) as h:
                    j = i * PH + h
                    f = j + PH
                    weigh(j, 0)
                    if not last:
                        copy_q(f)
                    weigh(j, 1)
                    if not last:
                        copy_qT(f)
                    weigh(j, 2)
                    weigh(j, 3)
                    if not last:
                        soft_exp(f)

            square_front(0)
            copy_h2T(0)
            with act.Fori(0, PH) as f:
                copy_q(f)
                copy_qT(f)
                soft_exp(f)
            tile_body(0, True, False)
            with act.Fori(1, NT - 1) as i:
                tile_body(i, False, False)
            tile_body(NT - 1, False, True)
            copy_acc(NT - 1)
            root_end(NT - 1)

        @block.vector
        def _(dve):
            TT, TS, STT = nc.vector.tensor_tensor, nc.vector.tensor_scalar, nc.vector.scalar_tensor_tensor
            dve.wait_ge(setup_loaded, 16 * SETUP)
            nc.vector.memset(zero[:, :], 0.0)
            lam_in = head_vecs[:, 9:11, :].rearrange("p a r -> p (a r)")
            STT(lam[:, 0, :], lam_in, -1.0, lam_in, ALU.mult, ALU.max).then_inc(lam_dve, 1)
            dve.wait_ge(lam_act, 1)
            TS(lam[:, 2, :], lam[:, 1, :], 1.0, None, ALU.add).then_inc(lam_dve, 1)
            dve.wait_ge(lam_act, 2)
            TS(lam[:, 4, :], lam[:, 2, :], -1.0, None, ALU.add)
            dve.drain()
            TS(lam[:, 5, :], lam[:, 4, :], 0.0, None, ALU.is_equal)
            dve.drain()
            TT(lam[:, 4, :], lam[:, 4, :], lam[:, 5, :], ALU.add)
            TT(lam[:, 3, :], lam[:, 3, :], lam[:, 1, :], ALU.mult)
            TT(lam[:, 5, :], lam[:, 5, :], lam[:, 1, :], ALU.mult)
            dve.drain()
            nc.vector.reciprocal(lam[:, 4, :], lam[:, 4, :])
            dve.drain()
            TT(lam[:, 3, :], lam[:, 3, :], lam[:, 4, :], ALU.mult)
            TS(lam[:, 2, :], lam_in, -1.0, 0.0, ALU.mult, ALU.max)
            dve.drain()
            TT(lam[:, 3, :], lam[:, 3, :], lam[:, 5, :], ALU.add)
            dve.drain()
            TT(lam[:, 3, :], lam[:, 3, :], lam[:, 2, :], ALU.add)
            dve.drain()
            TS(lam[:, 6, :], lam[:, 3, :], -LRU_C, None, ALU.mult)
            TS(lam[:, 7, :], lam[:, 3, :], LRU_C, None, ALU.mult).then_inc(lam_dve, 1)
            for c in range(2):
                dve.wait_ge(mod_matmul, c + 1)
                TT(mod_stage[0:2, c, :], bank[c][0:2, :], b_mod[:, c * H:(c + 1) * H], ALU.add).then_inc(mod_rows, 1)
            with dve.Fori(1, MC // 2) as n:
                for u in range(2):
                    c = 2 * n + u
                    dve.wait_ge(mod_matmul, c + 1)
                    dve.wait_ge(mod_stored[u], 16 * n)
                    TT(mod_stage[0:2, u, :], bank[u][0:2, :], b_mod[:, ds(c * H, H)], ALU.add).then_inc(mod_rows, 1)
            dve.wait_ge(squares, 1)
            TS(ssq[:, :], ssq[:, :], 1.0 / D, EPS, ALU.mult, ALU.add).then_inc(means, 1)
            dve.wait_ge(roots, 1)
            nc.vector.reciprocal(rstd[:, :], rstd[:, :])
            dve.wait_ge(mod_cols_loaded, 16 * 4)
            for which in range(2):
                STT(gain1[:, which, :], mod_cols[:, 2 + which, :], 1.0, head_vecs[:, 11, :], ALU.add, ALU.mult)
            dve.drain()
            nc.vector.memset(small[:, 6:7], 0.0).then_inc(lam_dve, 1)

            def modulate(t, u, which, col, xin, row):
                TS(xhat[:, u, :], xin, row, None, ALU.mult).then_inc(xhat_ready, 1)
                dve.wait_ge(x_transposed, t + 1)
                for k in range(4, KD):
                    last = TS(hT[:, k, col], bank[2 * u + 1][:, (k - 4) * P:(k - 3) * P], gain1[:, which, k:k + 1],
                              mod_cols[:, which, k:k + 1], ALU.mult, ALU.add)
                last.then_inc(h_dve, 1)

            for i in range(NTC):
                modulate(i, i, 1, slice(i * P, (i + 1) * P), ctx_raw[:, i, :], rstd[:, NT + i:NT + i + 1])
            with dve.Fori(0, NT // 2) as n:
                for u in range(2):
                    i = 2 * n + u
                    modulate(NTC + i, u, 0, ds(TC + i * P, P), xs[:, ds(i, 1), :].rearrange("p a n -> p (a n)"),
                             rstd[:, ds(i, 1)])
            with dve.Fori(0, G) as g:
                dve.wait_ge(zf_done, g + 1)
                nc.vector.tensor_copy(zfT[:, H:T], bank[1][:, :]).then_inc(zf_copied, 1)
                dve.wait_ge(pq_done, g + 1)
                for j in range(2, 4):
                    last = nc.vector.tensor_copy(PQ[:, 2 * j:2 * j + 2, ds(g, 1), :].rearrange("p t a n -> p t (a n)"),
                                                 bank[4 + j][:, :].rearrange("p (t n) -> p t n", t=2))
                last.then_inc(pq_copied, 1)
            dve.wait_ge(y_done, 1)
            for g in range(G):
                last = nc.vector.tensor_copy(yT[:, g, H:T], bank[2 * g + 1][:, :])
            last.then_inc(y_copied, 1)
            for a, b in ((0, 1), (1 + TC, ZL + 1), (ZL + 1 + T, ZL + T + 3)):
                last = nc.vector.memset(zpad[:, a:b], 0.0)
            last.then_inc(lam_dve, 1)
            with dve.Fori(0, R) as r:
                dve.wait_ge(conv_started, r + 1)
                for k in range(1, 4):
                    wk = head_vecs[:, k, ds(r, 1)]
                    STT(xc[:, 0:TC], zpad[:, k:k + TC], wk, xc[:, 0:TC], ALU.mult, ALU.add)
                    last = STT(xc[:, TC:TA], zpad[:, ZL + k:ZL + k + T], wk, xc[:, TC:TA], ALU.mult, ALU.add)
                    if k < 3:
                        dve.drain()
                last.then_inc(conv_done, 1)
                dve.drain()
                for v in range(2):
                    dve.wait_ge(gate_read, 3 + 12 * r + 6 * (v + 1))
                    last = TT(ig[v], ig[v], xc, ALU.mult)
                last.then_inc(gx_done, 1)
                for v in range(2):
                    dve.wait_ge(decay_done, 2 * r + v + 1)
                    TS(tmp, rg[v], 1.0, None, ALU.add)
                    dve.drain()
                    nc.vector.reciprocal(tmp, tmp)
                    dve.drain()
                    STT(rg[v], rg[v], 2.0, tmp, ALU.mult, ALU.mult).then_inc(norm_ready, 1)
                    dve.drain()
                dve.wait_ge(norm_root, 2 * r + 1)
                TT(rg[0], rg[0], ig[0], ALU.mult)
                dve.wait_ge(norm_root, 2 * r + 2)
                TT(rg[1], rg[1], ig[1], ALU.mult)
                dve.drain()
                nc.vector.tensor_tensor_scan(out=ig[0], data0=ag[0], data1=rg[0], initial=0.0, op0=ALU.mult, op1=ALU.add)
                nc.vector.tensor_tensor_scan(out=ig[1][:, TC - 1::-1], data0=ag[1][:, TC - 1::-1],
                                             data1=rg[1][:, TC - 1::-1], initial=0.0, op0=ALU.mult, op1=ALU.add)
                dve.drain()
                nc.vector.tensor_tensor_scan(out=ig[1][:, TA - 1:TC - 1:-1], data0=ag[1][:, TA - 1:TC - 1:-1],
                                             data1=rg[1][:, TA - 1:TC - 1:-1], initial=ig[1][:, 0:1],
                                             op0=ALU.mult, op1=ALU.add)
                dve.drain()
                TT(tmp[:, 0:T], ig[0][:, TC:TA], ig[1][:, TC:TA], ALU.add)
                dve.drain()
                yb_r = ybT[:, ds(r, 1), :].rearrange("p a n -> p (a n)")
                TT(yb_r, yb_r, tmp[:, 0:T], ALU.mult).then_inc(yb_ready, 1)
                dve.drain()
            with dve.Fori(0, KD) as d:
                for sig, prod, read, dst, b0 in ((ga_read, ya_done, ya_read, sig_a, 2), (gb_read, yb_done, yb_read, sig_b, 6)):
                    dve.wait_ge(sig, d + 2)
                    dve.wait_ge(prod, d + 1)
                    for j in range(NH):
                        last = TT(dst[:, j * H:(j + 1) * H], dst[:, j * H:(j + 1) * H], bank[b0 + j][:, :], ALU.mult)
                    last.then_inc(read, 1)
                dve.drain()
                TT(merged[:, ds(d, 1), :].rearrange("p a n -> p (a n)"), sig_a, sig_b, ALU.add).then_inc(merge_done, 1)
            dve.wait_ge(w_out_loaded, 16 * (KD + 2))
            TT(bout_row, bout_row, gate1_row, ALU.mult).then_inc(bout_gated, 1)
            with dve.Fori(0, NT // 2) as n:
                for u in range(2):
                    i = 2 * n + u
                    dve.wait_ge(mix_done, i + 3)
                    for j in range(2):
                        TT(mix_tmp[:, j * H:(j + 1) * H], bank[2 * u + j][:, :], gate1_row[:, j * H:(j + 1) * H], ALU.mult)
                    dve.drain()
                    dve.wait_ge(bias_added, i + 1)
                    xt = xs[:, ds(i, 1), :].rearrange("p a n -> p (a n)")
                    TT(xt, xt, mix_tmp, ALU.add).then_inc(x1_ready, 1)
                    dve.drain()

            dve.wait_ge(rows_loaded, 16 * 5)
            STT(gain2_row, gain2_row, 1.0, norm2_row, ALU.add, ALU.mult)
            dve.drain()

            def front_norm(i):
                dve.wait_ge(sq2_done, i + 1)
                TS(small[:, 1:2], small[:, 0:1], 1.0 / D, EPS, ALU.mult, ALU.add).then_inc(mean2_done, 1)
                dve.wait_ge(root2_done, i + 1)
                nc.vector.reciprocal(small[:, 2:3], small[:, 1:2])
                dve.drain()
                dve.wait_ge(h2_transposed, i + 1)
                STT(h2_next, x1_front, small[:, 2:3], gain2_row, ALU.mult, ALU.mult)
                dve.drain()
                TT(h2_next, h2_next, shift2_row, ALU.add).then_inc(h2_ready, 1)

            def top16(vals, rep, val_out, idx_out):
                nc.vector.max(val_out[:, 0:8], vals)
                dve.drain()
                nc.vector.max_index(idx_out[:, 0:8], val_out[:, 0:8], vals)
                nc.vector.match_replace(out=rep, in_to_replace=val_out[:, 0:8], in_values=vals, imm_value=NEG)
                dve.drain()
                nc.vector.max(val_out[:, 8:16], rep)
                dve.drain()
                nc.vector.max_index(idx_out[:, 8:16], val_out[:, 8:16], rep)

            def pick_keys(f):
                dve.wait_ge(score_done, f + 1)
                nc.vector.tensor_copy(s_sb[:, :, :].rearrange("p a n -> p (a n)"), bank[6][:, 0:2 * NK])\
                    .then_inc(score_copied, 1)
                dve.drain()
                for p in range(2):
                    top16(s_sb[:, p, :], s_rep[:, :], key_val[:, p, :], key_idx[:, p, :])
                dve.drain()

            def pick_experts(f):
                nc.vector.tensor_copy(key_idxf[:, :, :], key_idx[:, :, :])
                TT(cand[:, :, :], key_val[:, 0, :].unsqueeze(2).to_broadcast([P, TOPK, TOPK]),
                   key_val[:, 1, :].unsqueeze(1).to_broadcast([P, TOPK, TOPK]), ALU.add)
                dve.drain()
                top16(cand[:, :, :].rearrange("p a b -> p (a b)"), cand_rep[:, :, :].rearrange("p a b -> p (a b)"),
                      top_val[:, :], top_pos[:, :])
                TS(soft[:, 0:1], top_val[:, 0:1], -1.0, None, ALU.mult).then_inc(max_ready, 1)
                dve.drain()
                TS(top_ab[:, 0, :], top_pos[:, :], 4, None, ALU.logical_shift_right)
                TS(top_ab[:, 1, :], top_pos[:, :], 15, None, ALU.bitwise_and)
                dve.drain()
                nc.vector.tensor_copy(top_abf[:, :, :], top_ab[:, :, :])
                dve.drain()
                for p in range(2):
                    TT(cand_rep[:, :, :], top_abf[:, p, :].unsqueeze(2).to_broadcast([P, TOPK, TOPK]),
                       iota.unsqueeze(1).to_broadcast([P, TOPK, TOPK]), ALU.is_equal)
                    dve.drain()
                    TT(cand_rep[:, :, :], cand_rep[:, :, :], key_idxf[:, p, :].unsqueeze(1).to_broadcast([P, TOPK, TOPK]),
                       ALU.mult)
                    dve.drain()
                    nc.vector.tensor_reduce(picked[:, p, :], cand_rep[:, :, :], AXX, ALU.add)
                    dve.drain()
                STT(eidx[:, ds(f * TOPK, TOPK)], picked[:, 0, :], float(NK), picked[:, 1, :], ALU.mult, ALU.add)
                dve.wait_ge(exp_done, f + 1)
                nc.vector.reciprocal(soft[:, 2:3], soft[:, 1:2])
                dve.drain()
                TS(gates[:, ds(f * TOPK, TOPK)], top_exp[:, :], soft[:, 2:3], None, ALU.mult).then_inc(picks_done, 1)
                dve.drain()

            def dot_batch(j, b):
                for k in range(b * BATCH, (b + 1) * BATCH):
                    dve.wait_ge(landed[k % RING], 16 * (TOPK // RING * j + k // RING + 1))
                    last = STT(dot_junk[:, k % 2, :], ring[k % RING][:, 0:D], 1.0, h2_cur, ALU.mult, ALU.mult,
                               accum_out=dots[:, k:k + 1])
                    if k % BATCH == BATCH - 1:
                        last.then_inc(dots_done, 1)
                    if k % 2:
                        dve.drain()

            def finish(i):
                dve.wait_ge(acc_copied, i + 2)
                TT(acc_sb, acc_sb, gate2_row, ALU.mult)
                dve.drain()
                dve.wait_ge(x1_end_loaded, 16 * (i + 1))
                TT(acc_sb, acc_sb, x1_end, ALU.add)
                dve.drain()
                STT(dot_junk[:, 0, :], acc_sb, 1.0, acc_sb, ALU.mult, ALU.mult, accum_out=small[:, 3:4])
                dve.drain()
                TS(small[:, 4:5], small[:, 3:4], 1.0 / D, EPS, ALU.mult, ALU.add).then_inc(mean3_done, 1)
                dve.wait_ge(root3_done, i + 1)
                nc.vector.reciprocal(small[:, 5:6], small[:, 4:5])
                dve.drain()
                STT(x1_end, acc_sb, small[:, 5:6], final_row, ALU.mult, ALU.mult).then_inc(out_ready, 1)
                dve.drain()

            def tile_body(i, first, last):
                nc.vector.tensor_copy(h2_cur, h2_next)
                dve.drain()
                if not last:
                    front_norm(i + 1)
                if not first:
                    finish(i - 1)
                with dve.Fori(0, PH) as h:
                    j = i * PH + h
                    for b in range(NB - 1):
                        dot_batch(j, b)
                    if not last:
                        pick_keys(j + PH)
                    dot_batch(j, NB - 1)
                    if not last:
                        pick_experts(j + PH)

            front_norm(0)
            with dve.Fori(0, PH) as f:
                pick_keys(f)
                pick_experts(f)
            tile_body(0, True, False)
            with dve.Fori(1, NT - 1) as i:
                tile_body(i, False, False)
            tile_body(NT - 1, False, True)
            finish(NT - 1)

        @block.tensor
        def _(pe):
            mm = nc.tensor.matmul
            pe.wait_ge(silu_done, 1)

            def mod_chunk(c, u, n):
                pe.wait_ge(w_mod_loaded[u], 16 * (n + 1))
                for k in range(KD):
                    last = mm(bank[u][0:2, :], c_silu[:, k, :], w_mod_ring[:, u, k, :], start=(k == 0), stop=(k == KD - 1))
                last.then_inc(mod_matmul, 1)

            for u in range(2):
                mod_chunk(u, u, 0)
            with pe.Fori(1, MC // 2) as n:
                for u in range(2):
                    pe.wait_ge(mod_rows, 2 * n + u - 1)
                    mod_chunk(2 * n + u, u, n)
            pe.wait_ge(mod_rows, MC)

            def transpose_tile(t, u):
                pe.wait_ge(xhat_ready, t + 1)
                for k in range(KD):
                    last = nc.tensor.transpose(bank[2 * u + k // 4][:, (k % 4) * P:(k % 4 + 1) * P],
                                               xhat[:, u, k * P:(k + 1) * P], ident)
                last.then_inc(x_transposed, 1)

            for u in range(2):
                transpose_tile(u, u)
            with pe.Fori(1, (NT + NTC) // 2) as n:
                for u in range(2):
                    t = 2 * n + u
                    pe.wait_ge(h_act, t - 1)
                    pe.wait_ge(h_dve, t - 1)
                    transpose_tile(t, u)
            pe.wait_ge(h_act, NT + NTC)
            pe.wait_ge(h_dve, NT + NTC)

            def project(dst, w, cols, k_n=KD, src=hT):
                for k in range(k_n):
                    last = mm(dst, w[:, k, :], src[:, k, cols], start=(k == 0), stop=(k == k_n - 1))
                return last

            with pe.Fori(0, G // 2) as n:
                for u in range(2):
                    g = 2 * n + u
                    pe.wait_ge(w_loaded[u], 16 * (n + 1))
                    for j in range(NH):
                        last = project(bank[j][:, :], w_a[u], slice(TC + j * H, TC + (j + 1) * H))
                    last.then_inc(zf_done, 1)
                    pe.wait_ge(zf_copied, 2 * g + 2)
                    for t in range(NT):
                        last = mm(bank[4 + t // 2][:, (t % 2) * 2 * P:(t % 2 + 1) * 2 * P], zfT[:, t * P:(t + 1) * P],
                                  dft_chan, start=True, stop=True)
                    last.then_inc(pq_done, 1)
                    pe.wait_ge(pq_copied, 2 * g + 2)
                    pe.sem_inc(w_used, 1)
            for t in range(NT):
                pe.wait_ge(dft_loaded[t % 2], 16 * (t // 2 + 1))
                for g in range(G):
                    for c in range(2):
                        for j in range(NH):
                            last = mm(bank[2 * g + j][:, :], PQ[:, t, g, c * P:(c + 1) * P], dft_t[t % 2][:, c, j * H:(j + 1) * H],
                                      start=(t == 0 and c == 0), stop=(t == NT - 1 and c == 1))
                last.then_inc(dft_used, 1)
            pe.drain()
            pe.sem_inc(y_done, 1)
            pe.wait_ge(y_copied, 2)
            with pe.Fori(0, R // 2) as n:
                for u in range(2):
                    r = 2 * n + u
                    pe.wait_ge(w_loaded[u], 16 * (G // 2) + 48 * (n + 1))
                    pe.wait_ge(zx_copied, r + 1)
                    project(bank[2][:, 0:TC], w_a[u], slice(0, TC))
                    for j in range(NH):
                        last = project(bank[j][:, :], w_a[u], slice(TC + j * H, TC + (j + 1) * H))
                    last.then_inc(zx_done, 1)
                    pe.wait_ge(zy_read, r + 1)
                    for j in range(NH):
                        last = project(bank[3 + j][:, :], w_b[u], slice(TC + j * H, TC + (j + 1) * H))
                    last.then_inc(zy_done, 1)
                    pe.wait_ge(conv_done, r + 2)
                    for m in range(4):
                        for p, (a, b) in enumerate([(0, TC), (TC, TC + H), (TC + H, TA)]):
                            pe.wait_ge(gate_read, 12 * r + 3 * m + p + 1)
                            mm(bank[5 + p][:, 0:b - a], w_g[u][:, m, :], xc[:, a:b], start=True, stop=True)\
                                .then_inc(gate_done, 1)
                    pe.wait_ge(gate_done, 12 * r + 12)
                    pe.sem_inc(w_used, 1)
            pe.wait_ge(zx_copied, R + 1)
            pe.wait_ge(zy_read, R + 1)
            pe.wait_ge(gate_read, 12 * R + 3)
            with pe.Fori(0, KD // 2) as n:
                for u in range(2):
                    d = 2 * n + u
                    pe.wait_ge(w_loaded[u], 16 * (G // 2) + 48 * (R // 2) + 64 * (n + 1))
                    pe.wait_ge(ga_read, d + 1)
                    for j in range(NH):
                        last = project(bank[j][:, :], w_a[u], slice(TC + j * H, TC + (j + 1) * H))
                    last.then_inc(ga_done, 1)
                    pe.wait_ge(ya_read, d + 1)
                    for j in range(NH):
                        last = project(bank[2 + j][:, :], w_f[u], slice(j * H, (j + 1) * H), G, yT)
                    last.then_inc(ya_done, 1)
                    pe.wait_ge(gb_read, d + 1)
                    for j in range(NH):
                        last = project(bank[4 + j][:, :], w_b[u], slice(TC + j * H, TC + (j + 1) * H))
                    last.then_inc(gb_done, 1)
                    pe.wait_ge(yb_read, d + 1)
                    pe.wait_ge(yb_ready, R)
                    for j in range(NH):
                        last = project(bank[6 + j][:, :], w_l[u], slice(j * H, (j + 1) * H), R, ybT)
                    last.then_inc(yb_done, 1)
                    pe.wait_ge(yb_done, d + 1)
                    pe.sem_inc(w_used, 1)
            pe.wait_ge(w_out_loaded, 16 * (KD + 2))
            pe.wait_ge(ga_read, KD + 1)
            pe.wait_ge(ya_read, KD + 1)
            for u in range(2):
                pe.wait_ge(tile_staged, u + 1)
                for j in range(2):
                    for k in range(KD):
                        last = mm(bank[2 * u + j][:, :], merged_tile[u][:, k, :], w_out_k[k][:, j * H:(j + 1) * H],
                                  start=(k == 0), stop=(k == KD - 1))
                last.then_inc(mix_done, 1)
            with pe.Fori(1, NT // 2) as n:
                for u in range(2):
                    i = 2 * n + u
                    pe.wait_ge(tile_staged, i + 1)
                    pe.wait_ge(x1_ready, i - 1)
                    for j in range(2):
                        for k in range(KD):
                            last = mm(bank[2 * u + j][:, :], merged_tile[u][:, k, :], w_out_k[k][:, j * H:(j + 1) * H],
                                      start=(k == 0), stop=(k == KD - 1))
                    last.then_inc(mix_done, 1)
            pe.wait_ge(x1_ready, NT)

            pe.wait_ge(wq_loaded, 16 * (KD + 1))

            def transpose_h2(i):
                pe.wait_ge(h2_ready, i + 1)
                pe.wait_ge(h2T_ready, i + 1)
                for k in range(KD):
                    last = nc.tensor.transpose(bank[2 + k // 4][:, (k % 4) * P:(k % 4 + 1) * P],
                                               h2_next[:, k * P:(k + 1) * P], ident)
                last.then_inc(h2_transposed, 1)

            def query(f, h):
                pe.wait_ge(q_copied, f + 1)
                for k in range(KD):
                    last = mm(bank[4][:, 0:2 * P], h2T[:, k, :], wq_k[k][:, ds(h * 2 * P, 2 * P)],
                              start=(k == 0), stop=(k == KD - 1))
                last.then_inc(q_done, 1)

            def query_T(f):
                pe.wait_ge(q_copied, f + 2)
                pe.wait_ge(qT_copied, f + 1)
                for p in range(2):
                    last = nc.tensor.transpose(bank[5][:, p * P:(p + 1) * P], q_sb[:, p * P:(p + 1) * P], ident)
                last.then_inc(qT_done, 1)

            def scores(f, h):
                pe.wait_ge(qT_copied, f + 2)
                pe.wait_ge(score_copied, f + 1)
                for p in range(2):
                    last = mm(bank[6][:, p * NK:(p + 1) * NK], qT_sb[:, p, :],
                              keys_T[:, ds(2 * h + p, 1), :].rearrange("p a n -> p (a n)"), start=True, stop=True)
                last.then_inc(score_done, 1)

            def acc_edge(start):
                for c in range(2):
                    last = mm(bank[c][:, :], zero[:, :], final_row[:, c * H:(c + 1) * H], start=start, stop=not start,
                              skip_group_check=True)
                return last

            def add_rows(j, b):
                for k in range(b * BATCH, (b + 1) * BATCH):
                    pe.wait_ge(diag_done, TOPK * j + k + 1)
                    for c in range(2):
                        last = mm(bank[c][:, :], diag[:, k % BATCH, :], ring[k % RING][:, D + c * H:D + (c + 1) * H],
                                  start=False, stop=False, skip_group_check=True)
                    last.then_inc(ring_free, 1)

            def tile_body(i, last):
                if not last:
                    transpose_h2(i + 1)
                    pe.wait_ge(h2T_ready, i + 3)
                pe.wait_ge(acc_copied, i + 1)
                acc_edge(True)
                with pe.Fori(0, PH) as h:
                    j = i * PH + h
                    f = j + PH
                    if not last:
                        query(f, h)
                    add_rows(j, 0)
                    if not last:
                        query_T(f)
                    add_rows(j, 1)
                    if not last:
                        scores(f, h)
                    add_rows(j, 2)
                    add_rows(j, 3)
                acc_edge(False).then_inc(acc_done, 1)

            transpose_h2(0)
            pe.wait_ge(h2T_ready, 2)
            with pe.Fori(0, PH) as h:
                query(h, h)
                query_T(h)
                scores(h, h)
            tile_body(0, False)
            with pe.Fori(1, NT - 1) as i:
                tile_body(i, False)
            tile_body(NT - 1, True)


def kernel(**inputs):
    import numpy as np
    import concourse.bacc as bacc
    from concourse import mybir as my
    from concourse.bass_utils import run_bass_kernel_spmd as run

    P, GRID_W, TOPK = 128, 64, 16
    x = inputs["x"][0]
    T, D = x.shape
    KD = D // P
    cc = np.ascontiguousarray

    def cols(a):
        a = np.asarray(a)
        return np.moveaxis(a.reshape(a.shape[:-1] + (a.shape[-1] // P, P)), -1, 0)

    def chunks(w, width):
        k, n = w.shape
        return cc(w.reshape(k // P, P, n // width, width).transpose(2, 1, 0, 3))

    nf = D // 4
    omega = 1.0 / (10000.0 ** (np.arange(nf, dtype=np.float64) / nf))
    er = np.repeat(np.arange(T // GRID_W), GRID_W)[:, None] * omega[None]
    ec = np.tile(np.arange(GRID_W), P // GRID_W)[:, None] * omega[None]
    ang = 2 * np.pi * (np.outer(np.arange(P), np.arange(P)) % P) / P
    dft_c = np.concatenate([np.cos(ang), np.sin(ang)], axis=1) / np.sqrt(P)
    ang = 2 * np.pi * (np.outer(np.arange(T), np.arange(T)) % T) / T
    dft_t = np.stack([np.cos(ang), -np.sin(ang)], axis=1) / np.sqrt(T)
    iota = np.tile(np.arange(TOPK), (P, 1))

    wa, wx = inputs["lru_wa"][0], inputs["lru_wx"][0]
    ba, bx, lm = inputs["lru_ba"][0], inputs["lru_bx"][0], inputs["lru_lambda"][0]
    cw, cb = inputs["conv_w"][0], inputs["conv_b"][0]
    A = {
        "x": x, "ctx": inputs["ctx"][0],
        "pos_row": np.concatenate([np.sin(er), np.cos(er)], axis=1).astype(np.float32),
        "pos_col": np.concatenate([np.sin(ec), np.cos(ec)], axis=1).astype(np.float32),
        "consts": np.concatenate([np.eye(P), dft_c, iota], axis=1).astype(np.float32),
        "dft_time": dft_t.reshape(T // P, P, 2, T).astype(np.float32),
        "c_cols": np.stack([cols(inputs["c"][0]), cols(inputs["c_ctx"])], axis=2),
        "w_mod": chunks(inputs["w_mod"][0], 512), "b_mod": inputs["b_mod"],
        "head_vecs": cols(np.stack([cw[0], cw[1], cw[2], cw[3], cb, ba[0], bx[0], ba[1], bx[1], lm[0], lm[1],
                                    inputs["norm1_g"][0]])),
        "w_in": chunks(inputs["w_in"][0], P),
        "wf": chunks(inputs["w_fourier"][0], P), "wl": chunks(inputs["w_lru_out"][0], P),
        "lru_gates": np.stack([wa[0], wx[0], wa[1], wx[1]]).transpose(1, 2, 0, 3),
        "w_out": inputs["w_out"][0], "b_out": inputs["b_out"], "norm2_g": inputs["norm2_g"],
        "final_g": np.asarray(inputs["final_g"])[None],
        "wq": inputs["peer_wq"][0],
        "keys": np.moveaxis(np.asarray(inputs["peer_keys"][0]).reshape(-1, inputs["peer_keys"].shape[3], P), 2, 0),
        "uv": np.concatenate([inputs["peer_u"][0], inputs["peer_v"][0]], axis=1),
    }
    A = {k: cc(v) for k, v in A.items()}
    nc = bacc.Bacc("TRN2", target_bir_lowering=False, num_devices=1)
    t_in = {k: nc.dram_tensor("in_" + k, v.shape, my.dt.from_np(v.dtype), kind="ExternalInput").ap() for k, v in A.items()}
    out = nc.dram_tensor("out_tokens", (T, D), my.dt.float32, kind="ExternalOutput").ap()
    mod_dram = nc.dram_tensor("modulation_rows", (2, 6 * D), my.dt.float32, kind="Internal").ap()
    x1_dram = nc.dram_tensor("x1_tokens", (T, D), my.dt.float32, kind="Internal").ap()
    build_block(nc, t_in, mod_dram, x1_dram, out)
    r = run(nc, [{"in_" + k: v for k, v in A.items()}], core_ids=[0])
    return r.results[0]["out_tokens"].reshape(1, T, D)
```

```python
import concourse.bass as bass
from concourse import mybir
from contextlib import ExitStack


def build_block(nc, t_in, mod_dram, x1_dram, out):
    f32, bf16, u32 = mybir.dt.float32, mybir.dt.bfloat16, mybir.dt.uint32
    ALU, ACT, AXX = mybir.AluOpType, mybir.ActivationFunctionType, mybir.AxisListType.X
    ds = bass.ds

    P = 128
    T, D = out.shape
    TC = t_in["ctx"].shape[0]
    KD = D // P
    NT = T // P
    NTC = TC // P
    G = t_in["wf"].shape[2]
    R = t_in["lru_gates"].shape[0]
    TA = TC + T
    H = 512
    NH = T // H
    MC = t_in["w_mod"].shape[0]
    PH = t_in["keys"].shape[1] // 2
    NK = t_in["keys"].shape[2]
    TOPK = 16
    RING = 8
    BATCH = 4
    NB = TOPK // BATCH
    AHEAD = 2
    NF = NT // 2
    ME = 4
    EPS = 1e-6
    LRU_C = 8.0
    NEG = -3.0e38
    WSLOT = 3584
    ZX0, ZY0, ZGA0, ZGB0 = G, G + R, G + 2 * R, G + 2 * R + KD

    ctx = ExitStack()
    with ctx:
        def sb(name, shape, dt=f32):
            return ctx.enter_context(nc.sbuf_tensor(name, shape, dt))

        def sem(name):
            return ctx.enter_context(nc.semaphore(name))

        xs = sb("xs", [P, NT, D])
        lru = sb("lru", [P, 9 * 1288])
        hT = sb("hT", [P, KD, TA])
        ybT = sb("ybT", [P, KD, T])
        yT = sb("yT", [P, G, T])
        wgt = sb("wgt", [P, 2 * WSLOT])

        consts = sb("consts", [P, P + TOPK + 1])
        ident, iota, ones = consts[:, 0:P], consts[:, P:P + TOPK], consts[:, P + TOPK:P + TOPK + 1]
        head_vecs = sb("head_vecs", [P, 12, R])
        c_cols = sb("c_cols", [P, KD, 2])
        c_silu = sb("c_silu", [P, KD, 2])
        mod_cols = sb("mod_cols", [P, 4, KD])
        gain1 = sb("gain1", [P, 2, KD])
        lam = sb("lam", [P, 8, 2 * R])
        ssq = sb("ssq", [P, NT + NTC])
        rstd = sb("rstd", [P, NT + NTC])
        zero = sb("zero", [P, P])
        small = sb("small", [P, 8])
        s_sb = sb("s_sb", [P, 2, NK])
        s_rep = sb("s_rep", [P, NK])
        cand = sb("cand", [P, TOPK, TOPK])
        cand_rep = sb("cand_rep", [P, TOPK, TOPK])
        q_sb = sb("q_sb", [P, 2 * P])
        qT_sb = sb("qT_sb", [P, 2, P])
        key_val = sb("key_val", [P, 2, TOPK])
        key_idx = sb("key_idx", [P, 2, TOPK], u32)
        key_idxf = sb("key_idxf", [P, 2, TOPK])
        top_val = sb("top_val", [P, TOPK])
        top_pos = sb("top_pos", [P, TOPK], u32)
        top_ab = sb("top_ab", [P, 2, TOPK], u32)
        top_abf = sb("top_abf", [P, 2, TOPK])
        picked = sb("picked", [P, 2, TOPK])
        top_exp = sb("top_exp", [P, TOPK])
        soft = sb("soft", [P, 4])
        dots = sb("dots", [P, TOPK])
        gact = sb("gact", [P, BATCH])
        wrow = sb("wrow", [P, BATCH])
        diag = sb("diag", [P, BATCH, P])
        idx_stage = sb("idx_stage", [P, TOPK], u32)
        sq_junk = sb("sq_junk", [P, D], bf16)

        pos_row = lru[:, 0:NT * H].rearrange("p (i n) -> p i n", i=NT)
        pos_col = lru[:, 4096:4608]
        dft_mid = lru[0:1, 5632:5632 + T]
        dft_chan = lru[:, 5632 + T:5632 + T + 4 * P]
        dft_fwd, dft_rev = dft_chan[:, 0:2 * P], dft_chan[:, 2 * P:4 * P]
        mod_stage = lru[:, 8192:9216].rearrange("p (b n) -> p b n", b=2)
        mod_sum = lru[:, 9216:10240].rearrange("p (b n) -> p b n", b=2)
        w_mod_ring = ybT[:, :, :].rearrange("p a n -> p (a n)").rearrange("p (b k n) -> p b k n", b=2, k=KD)
        b_mod = [wgt[0:2, u * WSLOT + 3072:(u + 1) * WSLOT] for u in range(2)]
        xhat = yT[:, 0:2, :]
        ctx_raw = yT[:, 2:2 + NTC, :]
        zfT = yT[:, 0:2, :].rearrange("p a n -> p (a n)")[:, 0:T + 1]
        PQ = lru[:, 0:NF * G * 2 * P].rearrange("p (t g n) -> p t g n", t=NF, g=G)
        pq_mid = lru[0:1, 4096:4096 + G * P]

        def wview(u, at, k):
            return wgt[:, u * WSLOT + at:u * WSLOT + at + k * P].rearrange("p (k n) -> p k n", k=k)

        w_a = [wview(u, 0, KD) for u in range(2)]
        w_b = [wview(u, 1024, KD) for u in range(2)]
        w_g = [wview(u, 2048, 4) for u in range(2)]
        w_l = [wview(u, 2048, KD) for u in range(2)]
        w_f = [wview(u, 3072, G) for u in range(2)]
        dft_t = [wgt[:, u * WSLOT + 1024:u * WSLOT + 3072].rearrange("p (c n) -> p c n", c=2) for u in range(2)]

        def larr(i):
            return lru[:, i * 1288:i * 1288 + TA]
        zpad = lru[:, 8 * 1288:8 * 1288 + TA + 6]
        ZL = TC + 3
        xc, tmp = larr(0), larr(1)
        rg, ig, ag = [larr(2), larr(3)], [larr(4), larr(5)], [larr(6), larr(7)]
        merged = lru[:, 0:KD * T].rearrange("p (k n) -> p k n", k=KD)
        sig_a, sig_b = lru[:, 8192:9216], lru[:, 9216:10240]
        merged_tile = [lru[:, 8192 + 1024 * u:9216 + 1024 * u].rearrange("p (k n) -> p k n", k=KD) for u in range(2)]
        bout_row = lru[:, 10240:11264]
        w_out_k = [yT[:, k, :] for k in range(4)] + [wgt[:, k * D:(k + 1) * D] for k in range(3)] + \
                  [wgt[:, WSLOT:WSLOT + D]]
        gate1_row, mix_tmp = wgt[:, WSLOT + D:WSLOT + 2 * D], wgt[:, WSLOT + 2 * D:WSLOT + 3 * D]

        hT_flat = hT[:, :, :].rearrange("p a n -> p (a n)")
        ybT_flat = ybT[:, :, :].rearrange("p a n -> p (a n)")
        wq_k = [hT_flat[:, k * 2048:(k + 1) * 2048] for k in range(5)] + \
               [ybT_flat[:, k * 2048:(k + 1) * 2048] for k in range(3)]
        keys_T = ybT_flat[:, 6144:8192].rearrange("p (m n) -> p m n", m=2 * PH)
        ring = [xs[:, 2 * s:2 * s + 2, :].rearrange("p a n -> p (a n)") for s in range(4)] + \
               [lru[:, s * 2 * D:(s + 1) * 2 * D] for s in range(4)]
        dot_junk = lru[:, 8192:9216].bitcast(bf16).rearrange("p (b n) -> p b n", b=2)
        eidx = lru[:, 9216:10240].bitcast(u32)
        gates = lru[:, 10240:11264]
        gain2_row, shift2_row, gate2_row, final_row = (yT[:, j, :] for j in range(4))
        h2T = wgt[:, 0:1024].rearrange("p (k n) -> p k n", k=KD)
        h2_next, h2_cur, x1_front, x1_end, acc_sb, norm2_row = (wgt[:, j * D:(j + 1) * D] for j in range(1, 7))

        bank = [ctx.enter_context(nc.psum_tensor(f"bank{i}", [P, H], f32)) for i in range(8)]

        setup_loaded = sem("setup_loaded")
        x_loaded = sem("x_loaded")
        silu_done = sem("silu_done")
        w_mod_loaded = [sem("w_mod_loaded0"), sem("w_mod_loaded1")]
        b_mod_loaded = [sem("b_mod_loaded0"), sem("b_mod_loaded1")]
        mod_matmul = sem("mod_matmul")
        mod_rows = sem("mod_rows")
        mod_stored = [sem("mod_stored0"), sem("mod_stored1")]
        mod_cols_loaded = sem("mod_cols_loaded")
        pos_added = sem("pos_added")
        pos_row_added = sem("pos_row_added")
        squares = sem("squares")
        means = sem("means")
        roots = sem("roots")
        lam_dve = sem("lam_dve")
        lam_act = sem("lam_act")
        xhat_ready = sem("xhat_ready")
        x_transposed = sem("x_transposed")
        h_act = sem("h_act")
        h_dve = sem("h_dve")
        w_loaded = [sem("w_loaded0"), sem("w_loaded1")]
        gate_w_loaded = [sem("gate_w_loaded0"), sem("gate_w_loaded1")]
        mod_summed = sem("mod_summed")
        mod_late = sem("mod_late")
        dft_loaded = [sem("dft_loaded0"), sem("dft_loaded1")]
        dft_used = sem("dft_used")
        zf_done = sem("zf_done")
        zf_copied = sem("zf_copied")
        pq_done = sem("pq_done")
        pq_copied = sem("pq_copied")
        y_done = sem("y_done")
        y_copied = sem("y_copied")
        zx_done = sem("zx_done")
        zx_copied = sem("zx_copied")
        zy_done = sem("zy_done")
        zy_read = sem("zy_read")
        conv_started = sem("conv_started")
        conv_done = sem("conv_done")
        gate_done = sem("gate_done")
        gate_read = sem("gate_read")
        gx_done = sem("gx_done")
        decay_squared = sem("decay_squared")
        norm_ready = sem("norm_ready")
        norm_root = sem("norm_root")
        yb_ready = sem("yb_ready")
        ga_done, ya_done, gb_done, yb_done = sem("ga_done"), sem("ya_done"), sem("gb_done"), sem("yb_done")
        ga_read, gb_read = sem("ga_read"), sem("gb_read")
        ya_read, yb_read = sem("ya_read"), sem("yb_read")
        merge_done = sem("merge_done")
        w_out_loaded = sem("w_out_loaded")
        bout_gated = sem("bout_gated")
        tile_staged = sem("tile_staged")
        bias_added = sem("bias_added")
        mix_done = sem("mix_done")
        x1_ready = sem("x1_ready")
        x1_stored = sem("x1_stored")
        wq_loaded = sem("wq_loaded")
        rows_loaded = sem("rows_loaded")
        x1_front_loaded = sem("x1_front_loaded")
        x1_end_loaded = sem("x1_end_loaded")
        sq2_done = sem("sq2_done")
        mean2_done = sem("mean2_done")
        root2_done = sem("root2_done")
        h2_ready = sem("h2_ready")
        h2_transposed = sem("h2_transposed")
        h2T_ready = sem("h2T_ready")
        q_done = sem("q_done")
        q_copied = sem("q_copied")
        qT_done = sem("qT_done")
        qT_copied = sem("qT_copied")
        score_done = sem("score_done")
        score_copied = sem("score_copied")
        max_ready = sem("max_ready")
        exp_done = sem("exp_done")
        picks_done = sem("picks_done")
        landed = [sem(f"landed{s}") for s in range(RING)]
        ring_free = sem("ring_free")
        idx_staged = sem("idx_staged")
        dots_done = sem("dots_done")
        diag_done = sem("diag_done")
        acc_done = sem("acc_done")
        acc_copied = sem("acc_copied")
        y_squared = sem("y_squared")
        mean3_done = sem("mean3_done")
        root3_done = sem("root3_done")
        out_ready = sem("out_ready")
        out_stored = sem("out_stored")

        SETUP = 5

        block = ctx.enter_context(nc.Block())

        @block.sync
        def _(sp):
            sp.dma_start(consts[:, :], t_in["consts"]).then_inc(setup_loaded, 16)
            sp.dma_start(c_cols[:, :, :], t_in["c_cols"]).then_inc(setup_loaded, 16)
            sp.dma_start(head_vecs[:, :, :], t_in["head_vecs"]).then_inc(setup_loaded, 16)
            sp.dma_start(dft_mid, t_in["dft_mid"]).then_inc(setup_loaded, 16)
            sp.dma_start(dft_chan, t_in["dft_chan"]).then_inc(setup_loaded, 16)

            def load_mod(c):
                sp.dma_start(w_mod_ring[:, c % 2], t_in["w_mod"][c]).then_inc(w_mod_loaded[c % 2], 16)

            def load_mod_bias(c):
                sp.dma_start(b_mod[c % 2], t_in["b_mod"][:, c * H:(c + 1) * H].to_broadcast([2, H]))\
                    .then_inc(b_mod_loaded[c % 2], 16)

            for c in range(2):
                load_mod(c)
                load_mod_bias(c)
            xv = t_in["x"].rearrange("(i p) n -> p i n", p=P)
            for j in range(2):
                sp.dma_start(xs[:, 4 * j:4 * j + 4, :], xv[:, 4 * j:4 * j + 4, :]).then_inc(x_loaded, 16)
            sp.dma_start(pos_row, t_in["pos_row"].rearrange("(i p) n -> p i n", p=P)).then_inc(x_loaded, 16)
            sp.dma_start(pos_col, t_in["pos_col"]).then_inc(x_loaded, 16)
            sp.dma_start(ctx_raw, t_in["ctx"].rearrange("(i p) n -> p i n", p=P)).then_inc(x_loaded, 16)
            for c in range(ME):
                sp.wait_ge(mod_rows, c + 1)
                sp.dma_start(mod_dram[:, c * H:(c + 1) * H], mod_stage[0:2, c % 2, :]).then_inc(mod_stored[c % 2], 16)
                load_mod(c + 2)
                load_mod_bias(c + 2)
            for u in range(2):
                sp.wait_ge(mod_stored[u], 16 * (ME // 2))
            for j in range(2):
                for r in range(2):
                    sp.dma_start(mod_cols[:, 2 * j + r, :],
                                 mod_dram[r:r + 1, j * D:(j + 1) * D].rearrange("a (k p) -> p (a k)", p=P),
                                 allow_slow_non_contiguous=True)\
                        .then_inc(mod_cols_loaded, 16)
            for u in range(2):
                sp.dma_start(w_a[u], t_in["w_in"][u]).then_inc(w_loaded[u], 16)
                sp.dma_start(dft_t[u], t_in["dft_time"][u]).then_inc(dft_loaded[u], 16)
            for g in range(G):
                if 0 < g < G - 1:
                    sp.wait_ge(zf_done, g)
                    sp.dma_start(w_a[(g + 1) % 2], t_in["w_in"][g + 1]).then_inc(w_loaded[(g + 1) % 2], 16)
                for u in range(2):
                    c = ME + 2 * g + u
                    if c + 2 < MC:
                        sp.wait_ge(mod_summed, c - ME + 1)
                        load_mod(c + 2)
                for u in range(2):
                    c = ME + 2 * g + u
                    sp.wait_ge(mod_late, c - ME + 1)
                    sp.dma_start(mod_dram[0:1, c * H:(c + 1) * H], mod_stage[0:1, u, :]).then_inc(mod_stored[u], 16)
                    if c + 2 < MC:
                        load_mod_bias(c + 2)
            for t in range(2, NF):
                sp.wait_ge(dft_used, t - 1)
                sp.dma_start(dft_t[t % 2], t_in["dft_time"][t]).then_inc(dft_loaded[t % 2], 16)
            def load_head(r, u):
                for dst, at in ((w_a[u], ZX0), (w_b[u], ZY0)):
                    sp.dma_start(dst, t_in["w_in"][ds(r + at, 1)].rearrange("a p k n -> (a p) k n")).then_inc(w_loaded[u], 16)

            def load_gates(r, u):
                sp.dma_start(w_g[u], t_in["lru_gates"][ds(r, 1)].rearrange("a p k n -> (a p) k n"))\
                    .then_inc(gate_w_loaded[u], 16)

            for u in range(2):
                sp.wait_ge(dft_used, NF - 1 + u)
                load_head(u, u)
                load_gates(u, u)
            with sp.Fori(1, R // 2) as n:
                for u in range(2):
                    r = 2 * n + u
                    sp.wait_ge(zy_done, r - 1)
                    load_head(r, u)
                    sp.wait_ge(gate_done, 12 * (r - 1))
                    load_gates(r, u)
            def load_merge(d, u):
                for dst, src, at in ((w_a[u], "w_in", ZGA0), (w_f[u], "wf", 0), (w_b[u], "w_in", ZGB0), (w_l[u], "wl", 0)):
                    sp.dma_start(dst, t_in[src][ds(d + at, 1)].rearrange("a p k n -> (a p) k n")).then_inc(w_loaded[u], 16)

            for u in range(2):
                sp.wait_ge(zy_done, R - 1 + u)
                sp.wait_ge(gate_done, 12 * (R - 1 + u))
                load_merge(u, u)
            with sp.Fori(1, KD // 2) as n:
                for u in range(2):
                    sp.wait_ge(yb_done, 2 * n + u - 1)
                    load_merge(2 * n + u, u)
            for u in range(2):
                sp.wait_ge(mod_stored[u], 16 * (MC // 2))
            sp.wait_ge(yb_ready, R + 1)
            sp.dma_start(bout_row, t_in["b_out"].to_broadcast([P, D])).then_inc(w_out_loaded, 16)

            def load_w_out(k):
                sp.dma_start(w_out_k[k], t_in["w_out"][k * P:(k + 1) * P, :]).then_inc(w_out_loaded, 16)

            sp.wait_ge(yb_done, KD - 1)
            for k in range(4, 7):
                load_w_out(k)
            sp.wait_ge(ga_done, KD)
            load_w_out(7)
            sp.wait_ge(ya_done, KD)
            for k in range(4):
                load_w_out(k)
            sp.wait_ge(gb_done, KD)
            sp.dma_start(gate1_row, mod_dram[0:1, 2 * D:3 * D].to_broadcast([P, D])).then_inc(w_out_loaded, 16)
            for k in range(5):
                sp.dma_start(wq_k[k], t_in["wq"][k * P:(k + 1) * P, :]).then_inc(wq_loaded, 16)
            sp.wait_ge(yb_done, KD)
            for k in range(5, KD):
                sp.dma_start(wq_k[k], t_in["wq"][k * P:(k + 1) * P, :]).then_inc(wq_loaded, 16)
            sp.dma_start(keys_T, t_in["keys"]).then_inc(wq_loaded, 16)
            with sp.Fori(0, NT) as i:
                sp.wait_ge(x1_ready, i + 1)
                sp.dma_start(x1_dram[ds(i * P, P), :], xs[:, ds(i, 1), :].rearrange("p a n -> p (a n)"))\
                    .then_inc(x1_stored, 16)
            sp.wait_ge(mix_done, NT + 2)
            for dst, src in ((gain2_row, mod_dram[0:1, 4 * D:5 * D]), (shift2_row, mod_dram[0:1, 3 * D:4 * D]),
                             (gate2_row, mod_dram[0:1, 5 * D:6 * D]), (final_row, t_in["final_g"]),
                             (norm2_row, t_in["norm2_g"])):
                sp.dma_start(dst, src.to_broadcast([P, D])).then_inc(rows_loaded, 16)
            sp.wait_ge(x1_stored, 16 * NT)
            sp.dma_start(x1_front, x1_dram[0:P, :]).then_inc(x1_front_loaded, 16)
            sp.wait_ge(h2_ready, 1)
            sp.dma_start(x1_front, x1_dram[P:2 * P, :]).then_inc(x1_front_loaded, 16)

            def tile_io(i, first, fetch):
                if not first:
                    sp.wait_ge(out_ready, i)
                    sp.dma_start(out[ds((i - 1) * P, P), :], x1_end).then_inc(out_stored, 16)
                    sp.wait_ge(out_stored, 16 * i)
                sp.dma_start(x1_end, x1_dram[ds(i * P, P), :]).then_inc(x1_end_loaded, 16)
                if fetch:
                    sp.wait_ge(h2_ready, i + 2)
                    sp.dma_start(x1_front, x1_dram[ds((i + 2) * P, P), :]).then_inc(x1_front_loaded, 16)

            tile_io(0, True, True)
            with sp.Fori(1, NT - 2) as i:
                tile_io(i, False, True)
            tile_io(NT - 2, False, False)
            tile_io(NT - 1, False, False)
            sp.wait_ge(out_ready, NT)
            sp.dma_start(out[(NT - 1) * P:NT * P, :], x1_end).then_inc(out_stored, 16)
            sp.wait_ge(out_stored, 16 * NT)

        @block.gpsimd
        def _(pool):
            pool.sem_inc(zx_copied, 1)
            pool.sem_inc(zy_read, 1)
            pool.sem_inc(gate_read, 3)
            pool.sem_inc(yb_ready, 1)
            pool.sem_inc(ga_read, 1)
            pool.sem_inc(gb_read, 1)
            pool.sem_inc(ya_read, 1)
            pool.sem_inc(yb_read, 1)
            pool.sem_inc(merge_done, 1)
            pool.sem_inc(mix_done, 2)
            pool.sem_inc(h2_transposed, 1)
            pool.sem_inc(h2T_ready, 1)
            pool.sem_inc(q_copied, 1)
            pool.sem_inc(qT_copied, 1)
            pool.sem_inc(score_copied, 1)
            pool.sem_inc(acc_copied, 1)
            pool.sem_inc(ring_free, RING)
            pool.wait_ge(x_loaded, 16 * 5)
            with pool.Fori(0, NT) as i:
                xt = xs[:, ds(i, 1), :].rearrange("p a n -> p (a n)")
                nc.gpsimd.tensor_tensor(xt[:, H:D], xt[:, H:D], pos_col, ALU.add).then_inc(pos_added, 1)
            pool.wait_ge(merge_done, KD + 1)
            pool.wait_ge(bout_gated, 1)
            with pool.Fori(0, NT // 2) as n:
                for u in range(2):
                    i = 2 * n + u
                    pool.wait_ge(mix_done, i + 1)
                    pool.nop(nofuse=True)
                    nc.gpsimd.tensor_copy(merged_tile[u], merged[:, :, ds(i * P, P)]).then_inc(tile_staged, 1)
                    xt = xs[:, ds(i, 1), :].rearrange("p a n -> p (a n)")
                    nc.gpsimd.tensor_tensor(xt, xt, bout_row, ALU.add).then_inc(bias_added, 1)
            pool.wait_ge(x1_stored, 16 * NT)
            pool.wait_ge(mix_done, NT + 2)
            with pool.Fori(0, NT * PH) as j:
                pool.wait_ge(picks_done, j + 1)
                pool.nop(nofuse=True)
                for k in range(TOPK):
                    if k % RING == 0:
                        nc.gpsimd.tensor_copy(idx_stage[:, k:k + RING], eidx[:, ds(j * TOPK + k, RING)])\
                            .then_inc(idx_staged, 1)
                        pool.wait_ge(idx_staged, 2 * j + k // RING + 1)
                        pool.nop(nofuse=True)
                    pool.wait_ge(ring_free, j * TOPK + k + 1)
                    pool.nop(nofuse=True)
                    pool.indirect_dma_start(
                        out=ring[k % RING], out_offset=None, in_=t_in["uv"],
                        in_offset=bass.IndirectOffsetOnAxis(ap=idx_stage[:, k:k + 1], axis=0))\
                        .then_inc(landed[k % RING], 16)

        @block.scalar
        def _(act):
            act.wait_ge(setup_loaded, 16 * SETUP)
            nc.scalar.activation(c_silu[:, :, :], c_cols[:, :, :], ACT.Silu).then_inc(silu_done, 1)
            act.wait_ge(lam_dve, 1)
            nc.scalar.activation(lam[:, 1, :], lam[:, 0, :], ACT.Exp, scale=-1.0).then_inc(lam_act, 1)
            act.wait_ge(lam_dve, 2)
            nc.scalar.activation(lam[:, 3, :], lam[:, 2, :], ACT.Ln).then_inc(lam_act, 1)
            with act.Fori(0, NT) as i:
                act.wait_ge(pos_row_added, i + 1)
                act.wait_ge(pos_added, i + 1)
                act.nop(nofuse=True)
                nc.scalar.activation(sq_junk[:, :], xs[:, ds(i, 1), :].rearrange("p a n -> p (a n)"), ACT.Square,
                                     accum_out=ssq[:, ds(i, 1)])
                act.drain()
            for i in range(NTC):
                last = nc.scalar.activation(sq_junk[:, :], ctx_raw[:, i, :], ACT.Square,
                                            accum_out=ssq[:, NT + i:NT + i + 1])
                act.drain()
            nc.scalar.activation(small[:, 7:8], ident[:, 0:1], ACT.Copy).then_inc(squares, 1)
            act.wait_ge(means, 1)
            nc.scalar.activation(rstd[:, :], ssq[:, :], ACT.Sqrt).then_inc(roots, 1)
            act.wait_ge(lam_dve, 4)

            def modulate(t, u, which, col):
                act.wait_ge(x_transposed, t + 1)
                act.nop(nofuse=True)
                for k in range(4):
                    last = nc.scalar.activation(hT[:, k, col], bank[2 * u][:, k * P:(k + 1) * P], ACT.Identity,
                                                scale=gain1[:, which, k:k + 1], bias=mod_cols[:, which, k:k + 1])
                last.then_inc(h_act, 1)

            for i in range(NTC):
                modulate(i, i, 1, slice(i * P, (i + 1) * P))
            with act.Fori(0, NT // 2) as n:
                for u in range(2):
                    modulate(NTC + 2 * n + u, u, 0, ds(TC + (2 * n + u) * P, P))
            with act.Fori(0, G) as g:
                act.wait_ge(zf_done, g + 1)
                nc.scalar.activation(zfT[:, 0:H], bank[0][:, :], ACT.Copy).then_inc(zf_copied, 1)
                act.wait_ge(pq_done, g + 1)
                act.nop(nofuse=True)
                for t in range(NF // 2):
                    last = nc.scalar.activation(PQ[:, t, ds(g, 1), :].rearrange("p a n -> p (a n)"), bank[4 + t][:, 0:2 * P],
                                                ACT.Copy)
                last.then_inc(pq_copied, 1)
            act.wait_ge(y_done, 1)
            for g in range(G):
                last = nc.scalar.activation(yT[:, g, 0:H], bank[2 * g][:, :], ACT.Copy)
            last.then_inc(y_copied, 1)
            act.wait_ge(lam_dve, 5)
            pieces = [(0, TC), (TC, TC + H), (TC + H, TA)]

            def copy_zx(r, first=False):
                act.wait_ge(zx_done, r + 1)
                if not first:
                    act.wait_ge(conv_done, r)
                nc.scalar.activation(zpad[:, 1:1 + TC], bank[2][:, 0:TC], ACT.Copy)
                for j in range(NH):
                    last = nc.scalar.activation(zpad[:, ZL + 1 + j * H:ZL + 1 + (j + 1) * H], bank[j][:, :], ACT.Copy)
                last.then_inc(zx_copied, 1)

            def start_conv(r, first=False):
                if not first:
                    act.wait_ge(gx_done, r)
                act.nop(nofuse=True)
                act.drain()
                w0, cb = head_vecs[:, 0, ds(r, 1)], head_vecs[:, 4, ds(r, 1)]
                nc.scalar.activation(xc[:, 0:TC], zpad[:, 0:TC], ACT.Identity, scale=w0, bias=cb)
                nc.scalar.activation(xc[:, TC:TA], zpad[:, ZL:ZL + T], ACT.Identity, scale=w0, bias=cb)\
                    .then_inc(conv_started, 1)

            def gelu_zy(r):
                act.wait_ge(zy_done, r + 1)
                act.nop(nofuse=True)
                yb_r = ybT[:, ds(r, 1), :].rearrange("p a n -> p (a n)")
                for j in range(NH):
                    last = nc.scalar.activation(yb_r[:, j * H:(j + 1) * H], bank[3 + j][:, :], ACT.Gelu_apprx_tanh)
                last.then_inc(zy_read, 1)

            def lru_head(r, more):
                if more:
                    copy_zx(r + 1)
                act.wait_ge(yb_ready, r + 1)
                act.nop(nofuse=True)
                for m, dst in enumerate((rg[0], ig[0], rg[1], ig[1])):
                    for p, (a, b) in enumerate(pieces):
                        act.wait_ge(gate_done, 12 * r + 3 * m + p + 1)
                        act.nop(nofuse=True)
                        nc.scalar.activation(dst[:, a:b], bank[5 + p][:, 0:b - a], ACT.Sigmoid,
                                             bias=head_vecs[:, 5 + m, ds(r, 1)]).then_inc(gate_read, 1)
                if more:
                    start_conv(r + 1)
                act.drain()
                for v in range(2):
                    nc.scalar.activation(ag[v], rg[v], ACT.Exp, scale=lam[:, 6, ds(v * R + r, 1)])
                act.drain()
                for v in range(2):
                    nc.scalar.activation(rg[v], rg[v], ACT.Tanh, scale=lam[:, 7, ds(v * R + r, 1)])
                nc.scalar.activation(tmp, ag[0], ACT.Square).then_inc(decay_squared, 1)
                if more:
                    act.wait_ge(conv_done, r + 2)
                for a, b, z in ((0, TC, 1), (TC, TA, ZL + 1)):
                    last = nc.scalar.activation(zpad[:, z:z + b - a], ag[1][:, a:b], ACT.Square)
                last.then_inc(decay_squared, 1)
                for v in range(2):
                    act.wait_ge(norm_ready, 2 * r + v + 1)
                    nc.scalar.activation(rg[v], rg[v], ACT.Sqrt).then_inc(norm_root, 1)
                if more:
                    gelu_zy(r + 1)

            copy_zx(0, True)
            start_conv(0, True)
            gelu_zy(0)
            with act.Fori(0, R - 1) as r:
                lru_head(r, True)
            lru_head(R - 1, False)
            act.wait_ge(yb_ready, R + 1)
            with act.Fori(0, KD) as d:
                for done, read, dst, b0 in ((ga_done, ga_read, sig_a, 0), (gb_done, gb_read, sig_b, 4)):
                    act.wait_ge(done, d + 1)
                    act.wait_ge(merge_done, d + 1)
                    for j in range(NH):
                        last = nc.scalar.activation(dst[:, j * H:(j + 1) * H], bank[b0 + j][:, :], ACT.Sigmoid)
                    last.then_inc(read, 1)

            def square_front(i):
                act.wait_ge(x1_front_loaded, 16 * (i + 1))
                nc.scalar.activation(sq_junk[:, :], x1_front, ACT.Square, accum_out=small[:, 0:1]).then_inc(sq2_done, 1)
                act.wait_ge(mean2_done, i + 1)
                nc.scalar.activation(small[:, 1:2], small[:, 1:2], ACT.Sqrt).then_inc(root2_done, 1)

            def copy_h2T(i):
                act.wait_ge(h2_transposed, i + 2)
                for j in range(2):
                    last = nc.scalar.activation(h2T[:, 4 * j:4 * j + 4, :].rearrange("p k n -> p (k n)"), bank[2 + j][:, :],
                                                ACT.Copy)
                last.then_inc(h2T_ready, 1)

            def copy_q(f):
                act.wait_ge(q_done, f + 1)
                nc.scalar.activation(q_sb[:, :], bank[4][:, 0:2 * P], ACT.Copy).then_inc(q_copied, 1)

            def copy_qT(f):
                act.wait_ge(qT_done, f + 1)
                nc.scalar.activation(qT_sb[:, :, :].rearrange("p a n -> p (a n)"), bank[5][:, 0:2 * P], ACT.Copy)\
                    .then_inc(qT_copied, 1)

            def soft_exp(f):
                act.wait_ge(max_ready, f + 1)
                nc.scalar.activation(top_exp[:, :], top_val[:, :], ACT.Exp, bias=soft[:, 0:1],
                                     accum_out=soft[:, 1:2]).then_inc(exp_done, 1)

            def weigh(j, b):
                act.wait_ge(dots_done, NB * j + b + 1)
                nc.scalar.activation(gact[:, :], dots[:, b * BATCH:(b + 1) * BATCH], ACT.Gelu_apprx_tanh)
                act.drain()
                for k in range(BATCH):
                    nc.scalar.activation(wrow[:, k:k + 1], gact[:, k:k + 1], ACT.Copy,
                                         scale=gates[:, ds(j * TOPK + b * BATCH + k, 1)])
                act.drain()
                for k in range(BATCH):
                    act.wait_ge(ring_free, j * TOPK + b * BATCH + k + 1 + RING - BATCH)
                    nc.scalar.activation(diag[:, k, :], ident, ACT.Copy, scale=wrow[:, k:k + 1]).then_inc(diag_done, 1)

            def copy_acc(i):
                act.wait_ge(acc_done, i + 1)
                for h in range(2):
                    last = nc.scalar.activation(acc_sb[:, h * H:(h + 1) * H], bank[h][:, :], ACT.Copy)
                last.then_inc(acc_copied, 1)

            def root_end(i):
                act.wait_ge(mean3_done, i + 1)
                nc.scalar.activation(small[:, 4:5], small[:, 4:5], ACT.Sqrt).then_inc(root3_done, 1)

            def head(j, front, very_first=False):
                f = j + AHEAD
                weigh(j, 0)
                if front:
                    copy_q(f)
                weigh(j, 1)
                if front:
                    copy_qT(f)
                if very_first:
                    soft_exp(1)
                weigh(j, 2)
                weigh(j, 3)
                if front:
                    soft_exp(f)

            def tile_body(i, first, last):
                if not first:
                    copy_acc(i - 1)
                if first:
                    head(0, True, very_first=True)
                with act.Fori(1 if first else 0, PH - AHEAD) as h:
                    head(i * PH + h, True)
                if not last:
                    square_front(i + 1)
                    copy_h2T(i + 1)
                if not first:
                    root_end(i - 1)
                with act.Fori(PH - AHEAD, PH) as h:
                    head(i * PH + h, not last)

            square_front(0)
            copy_h2T(0)
            for f in range(AHEAD):
                copy_q(f)
                copy_qT(f)
                if f == 0:
                    soft_exp(f)
            tile_body(0, True, False)
            with act.Fori(1, NT - 1) as i:
                tile_body(i, False, False)
            tile_body(NT - 1, False, True)
            copy_acc(NT - 1)
            root_end(NT - 1)

        @block.vector
        def _(dve):
            TT, TS, STT = nc.vector.tensor_tensor, nc.vector.tensor_scalar, nc.vector.scalar_tensor_tensor
            dve.wait_ge(setup_loaded, 16 * SETUP)
            nc.vector.memset(zero[:, :], 0.0)
            lam_in = head_vecs[:, 9:11, :].rearrange("p a r -> p (a r)")
            STT(lam[:, 0, :], lam_in, -1.0, lam_in, ALU.mult, ALU.max).then_inc(lam_dve, 1)
            dve.wait_ge(lam_act, 1)
            TS(lam[:, 2, :], lam[:, 1, :], 1.0, None, ALU.add).then_inc(lam_dve, 1)
            dve.wait_ge(lam_act, 2)
            TS(lam[:, 4, :], lam[:, 2, :], -1.0, None, ALU.add)
            dve.drain()
            TS(lam[:, 5, :], lam[:, 4, :], 0.0, None, ALU.is_equal)
            dve.drain()
            TT(lam[:, 4, :], lam[:, 4, :], lam[:, 5, :], ALU.add)
            TT(lam[:, 3, :], lam[:, 3, :], lam[:, 1, :], ALU.mult)
            TT(lam[:, 5, :], lam[:, 5, :], lam[:, 1, :], ALU.mult)
            dve.drain()
            nc.vector.reciprocal(lam[:, 4, :], lam[:, 4, :])
            dve.drain()
            TT(lam[:, 3, :], lam[:, 3, :], lam[:, 4, :], ALU.mult)
            TS(lam[:, 2, :], lam_in, -1.0, 0.0, ALU.mult, ALU.max)
            dve.drain()
            TT(lam[:, 3, :], lam[:, 3, :], lam[:, 5, :], ALU.add)
            dve.drain()
            TT(lam[:, 3, :], lam[:, 3, :], lam[:, 2, :], ALU.add)
            dve.drain()
            TS(lam[:, 6, :], lam[:, 3, :], -LRU_C, None, ALU.mult)
            TS(lam[:, 7, :], lam[:, 3, :], LRU_C, None, ALU.mult).then_inc(lam_dve, 1)
            def mod_row(c):
                dve.wait_ge(mod_matmul, c + 1)
                dve.wait_ge(b_mod_loaded[c % 2], 16 * (c // 2 + 1))
                if c >= 2:
                    dve.wait_ge(mod_stored[c % 2], 16)
                TT(mod_stage[0:2, c % 2, :], bank[c % 2][0:2, :], b_mod[c % 2], ALU.add).then_inc(mod_rows, 1)

            mod_row(0)
            mod_row(1)
            dve.wait_ge(x_loaded, 16 * 5)
            with dve.Fori(0, NT) as i:
                xt = xs[:, ds(i, 1), :].rearrange("p a n -> p (a n)")
                pr = pos_row[:, ds(i, 1), :].rearrange("p a n -> p (a n)")
                TT(xt[:, 0:H], xt[:, 0:H], pr, ALU.add).then_inc(pos_row_added, 1)
            mod_row(2)
            mod_row(3)
            dve.wait_ge(squares, 1)
            TS(ssq[:, :], ssq[:, :], 1.0 / D, EPS, ALU.mult, ALU.add).then_inc(means, 1)
            dve.wait_ge(roots, 1)
            nc.vector.reciprocal(rstd[:, :], rstd[:, :])
            dve.drain()

            def normalise(u, xin, col):
                TS(xhat[:, u, :], xin, rstd[:, col], None, ALU.mult).then_inc(xhat_ready, 1)

            def normalise_latent(i, u):
                normalise(u, xs[:, ds(i, 1), :].rearrange("p a n -> p (a n)"), ds(i, 1))

            def modulate(t, u, which, col):
                dve.wait_ge(x_transposed, t + 1)
                for k in range(4, KD):
                    last = TS(hT[:, k, col], bank[2 * u + 1][:, (k - 4) * P:(k - 3) * P], gain1[:, which, k:k + 1],
                              mod_cols[:, which, k:k + 1], ALU.mult, ALU.add)
                last.then_inc(h_dve, 1)

            for i in range(NTC):
                normalise(i, ctx_raw[:, i, :], slice(NT + i, NT + i + 1))
            dve.wait_ge(mod_cols_loaded, 16 * 4)
            for which in range(2):
                STT(gain1[:, which, :], mod_cols[:, 2 + which, :], 1.0, head_vecs[:, 11, :], ALU.add, ALU.mult)
            dve.drain()
            nc.vector.memset(small[:, 6:7], 0.0).then_inc(lam_dve, 1)
            for i in range(NTC):
                modulate(i, i, 1, slice(i * P, (i + 1) * P))
                normalise_latent(i, i)
            with dve.Fori(0, NT // 2 - 1) as n:
                for u in range(2):
                    i = 2 * n + u
                    modulate(NTC + i, u, 0, ds(TC + i * P, P))
                    normalise_latent(i + 2, u)
            for u in range(2):
                i = NT - 2 + u
                modulate(NTC + i, u, 0, slice(TC + i * P, TC + (i + 1) * P))
            nc.vector.memset(zfT[:, H:H + 1], 0.0)
            with dve.Fori(0, G) as g:
                for u in range(2):
                    dve.wait_ge(w_mod_loaded[u], 16 * (g + ME // 2 + 1))
                    TS(mod_sum[:, u, :], w_mod_ring[:, u, 0, :], c_silu[:, 0, 0:1], None, ALU.mult)
                    for k in range(1, KD):
                        dve.drain()
                        last = STT(mod_sum[:, u, :], w_mod_ring[:, u, k, :], c_silu[:, k, 0:1], mod_sum[:, u, :],
                                   ALU.mult, ALU.add)
                    last.then_inc(mod_summed, 1)
                dve.wait_ge(zf_done, g + 1)
                nc.vector.tensor_copy(zfT[:, T:T + 1], bank[1][:, 0:1])
                nc.vector.tensor_copy(zfT[:, T - 1:H:-1], bank[1][:, 1:H]).then_inc(zf_copied, 1)
                dve.wait_ge(pq_done, g + 1)
                nc.vector.tensor_copy(pq_mid[:, ds(g * P, P)], bank[6][0:1, 2 * P:3 * P])
                for t in range(NF // 2, NF):
                    last = nc.vector.tensor_copy(PQ[:, t, ds(g, 1), :].rearrange("p a n -> p (a n)"), bank[4 + t][:, 0:2 * P])
                last.then_inc(pq_copied, 1)
                for u in range(2):
                    dve.wait_ge(mod_stored[u], 16 * (g + ME // 2))
                    dve.wait_ge(b_mod_loaded[u], 16 * (g + ME // 2 + 1))
                    TT(mod_stage[0:1, u, :], bank[2 + u][0:1, :], b_mod[u][0:1, :], ALU.add).then_inc(mod_late, 1)
            dve.wait_ge(y_done, 1)
            for g in range(G):
                last = nc.vector.tensor_copy(yT[:, g, H:T], bank[2 * g + 1][:, :])
            last.then_inc(y_copied, 1)
            for a, b in ((0, 1), (1 + TC, ZL + 1), (ZL + 1 + T, ZL + T + 3)):
                last = nc.vector.memset(zpad[:, a:b], 0.0)
            last.then_inc(lam_dve, 1)
            def convolve(r):
                dve.wait_ge(conv_started, r + 1)
                for k in range(1, 4):
                    wk = head_vecs[:, k, ds(r, 1)]
                    STT(xc[:, 0:TC], zpad[:, k:k + TC], wk, xc[:, 0:TC], ALU.mult, ALU.add)
                    last = STT(xc[:, TC:TA], zpad[:, ZL + k:ZL + k + T], wk, xc[:, TC:TA], ALU.mult, ALU.add)
                    if k < 3:
                        dve.drain()
                last.then_inc(conv_done, 1)
                dve.drain()

            def lru_head(r, more):
                for v in range(2):
                    dve.wait_ge(gate_read, 3 + 12 * r + 6 * (v + 1))
                    last = TT(ig[v], ig[v], xc, ALU.mult)
                last.then_inc(gx_done, 1)
                if more:
                    convolve(r + 1)
                dve.wait_ge(decay_squared, 2 * r + 1)
                STT(rg[0], tmp, 1.0, rg[0], ALU.add, ALU.mult).then_inc(norm_ready, 1)
                dve.wait_ge(decay_squared, 2 * r + 2)
                for a, b, z in ((0, TC, 1), (TC, TA, ZL + 1)):
                    last = STT(rg[1][:, a:b], zpad[:, z:z + b - a], 1.0, rg[1][:, a:b], ALU.add, ALU.mult)
                last.then_inc(norm_ready, 1)
                dve.wait_ge(norm_root, 2 * r + 1)
                TT(rg[0], rg[0], ig[0], ALU.mult)
                dve.wait_ge(norm_root, 2 * r + 2)
                TT(rg[1], rg[1], ig[1], ALU.mult)
                dve.drain()
                nc.vector.tensor_tensor_scan(out=ig[0], data0=ag[0], data1=rg[0], initial=0.0, op0=ALU.mult, op1=ALU.add)
                nc.vector.tensor_tensor_scan(out=ig[1][:, TC - 1::-1], data0=ag[1][:, TC - 1::-1],
                                             data1=rg[1][:, TC - 1::-1], initial=0.0, op0=ALU.mult, op1=ALU.add)
                dve.drain()
                nc.vector.tensor_tensor_scan(out=ig[1][:, TA - 1:TC - 1:-1], data0=ag[1][:, TA - 1:TC - 1:-1],
                                             data1=rg[1][:, TA - 1:TC - 1:-1], initial=ig[1][:, 0:1],
                                             op0=ALU.mult, op1=ALU.add)
                dve.drain()
                TT(tmp[:, 0:T], ig[0][:, TC:TA], ig[1][:, TC:TA], ALU.add)
                dve.drain()
                yb_r = ybT[:, ds(r, 1), :].rearrange("p a n -> p (a n)")
                TT(yb_r, yb_r, tmp[:, 0:T], ALU.mult).then_inc(yb_ready, 1)
                dve.drain()

            convolve(0)
            with dve.Fori(0, R - 1) as r:
                lru_head(r, True)
            lru_head(R - 1, False)
            with dve.Fori(0, KD) as d:
                for sig, prod, read, dst, b0 in ((ga_read, ya_done, ya_read, sig_a, 2), (gb_read, yb_done, yb_read, sig_b, 6)):
                    dve.wait_ge(sig, d + 2)
                    dve.wait_ge(prod, d + 1)
                    for j in range(NH):
                        last = TT(dst[:, j * H:(j + 1) * H], dst[:, j * H:(j + 1) * H], bank[b0 + j][:, :], ALU.mult)
                    last.then_inc(read, 1)
                dve.drain()
                TT(merged[:, ds(d, 1), :].rearrange("p a n -> p (a n)"), sig_a, sig_b, ALU.add).then_inc(merge_done, 1)
            dve.wait_ge(w_out_loaded, 16 * (KD + 2))
            TT(bout_row, bout_row, gate1_row, ALU.mult).then_inc(bout_gated, 1)
            with dve.Fori(0, NT // 2) as n:
                for u in range(2):
                    i = 2 * n + u
                    dve.wait_ge(mix_done, i + 3)
                    for j in range(2):
                        TT(mix_tmp[:, j * H:(j + 1) * H], bank[2 * u + j][:, :], gate1_row[:, j * H:(j + 1) * H], ALU.mult)
                    dve.drain()
                    dve.wait_ge(bias_added, i + 1)
                    xt = xs[:, ds(i, 1), :].rearrange("p a n -> p (a n)")
                    TT(xt, xt, mix_tmp, ALU.add).then_inc(x1_ready, 1)
                    dve.drain()

            dve.wait_ge(rows_loaded, 16 * 5)
            STT(gain2_row, gain2_row, 1.0, norm2_row, ALU.add, ALU.mult)
            dve.drain()

            def front_norm(i):
                dve.wait_ge(sq2_done, i + 1)
                TS(small[:, 1:2], small[:, 0:1], 1.0 / D, EPS, ALU.mult, ALU.add).then_inc(mean2_done, 1)
                dve.wait_ge(root2_done, i + 1)
                nc.vector.reciprocal(small[:, 2:3], small[:, 1:2])
                dve.drain()
                dve.wait_ge(h2_transposed, i + 1)
                STT(h2_next, x1_front, small[:, 2:3], gain2_row, ALU.mult, ALU.mult)
                dve.drain()
                TT(h2_next, h2_next, shift2_row, ALU.add).then_inc(h2_ready, 1)

            def top16(vals, rep, val_out, idx_out):
                nc.vector.max(val_out[:, 0:8], vals)
                dve.drain()
                nc.vector.max_index(idx_out[:, 0:8], val_out[:, 0:8], vals)
                nc.vector.match_replace(out=rep, in_to_replace=val_out[:, 0:8], in_values=vals, imm_value=NEG)
                dve.drain()
                nc.vector.max(val_out[:, 8:16], rep)
                dve.drain()
                nc.vector.max_index(idx_out[:, 8:16], val_out[:, 8:16], rep)

            def pick_keys(f):
                dve.wait_ge(score_done, f + 1)
                nc.vector.tensor_copy(s_sb[:, :, :].rearrange("p a n -> p (a n)"), bank[6][:, 0:2 * NK])\
                    .then_inc(score_copied, 1)
                dve.drain()
                for p in range(2):
                    top16(s_sb[:, p, :], s_rep[:, :], key_val[:, p, :], key_idx[:, p, :])
                dve.drain()

            def pick_experts(f):
                nc.vector.tensor_copy(key_idxf[:, :, :], key_idx[:, :, :])
                TT(cand[:, :, :], key_val[:, 0, :].unsqueeze(2).to_broadcast([P, TOPK, TOPK]),
                   key_val[:, 1, :].unsqueeze(1).to_broadcast([P, TOPK, TOPK]), ALU.add)
                dve.drain()
                top16(cand[:, :, :].rearrange("p a b -> p (a b)"), cand_rep[:, :, :].rearrange("p a b -> p (a b)"),
                      top_val[:, :], top_pos[:, :])
                TS(soft[:, 0:1], top_val[:, 0:1], -1.0, None, ALU.mult).then_inc(max_ready, 1)
                dve.drain()
                TS(top_ab[:, 0, :], top_pos[:, :], 4, None, ALU.logical_shift_right)
                TS(top_ab[:, 1, :], top_pos[:, :], 15, None, ALU.bitwise_and)
                dve.drain()
                nc.vector.tensor_copy(top_abf[:, :, :], top_ab[:, :, :])
                dve.drain()
                for p in range(2):
                    TT(cand_rep[:, :, :], top_abf[:, p, :].unsqueeze(2).to_broadcast([P, TOPK, TOPK]),
                       iota.unsqueeze(1).to_broadcast([P, TOPK, TOPK]), ALU.is_equal)
                    dve.drain()
                    TT(cand_rep[:, :, :], cand_rep[:, :, :], key_idxf[:, p, :].unsqueeze(1).to_broadcast([P, TOPK, TOPK]),
                       ALU.mult)
                    dve.drain()
                    nc.vector.tensor_reduce(picked[:, p, :], cand_rep[:, :, :], AXX, ALU.add)
                    dve.drain()
                STT(eidx[:, ds(f * TOPK, TOPK)], picked[:, 0, :], float(NK), picked[:, 1, :], ALU.mult, ALU.add)
                dve.wait_ge(exp_done, f + 1)
                nc.vector.reciprocal(soft[:, 2:3], soft[:, 1:2])
                dve.drain()
                TS(gates[:, ds(f * TOPK, TOPK)], top_exp[:, :], soft[:, 2:3], None, ALU.mult).then_inc(picks_done, 1)
                dve.drain()

            def dot_batch(j, b):
                for k in range(b * BATCH, (b + 1) * BATCH):
                    dve.wait_ge(landed[k % RING], 16 * (TOPK // RING * j + k // RING + 1))
                    last = STT(dot_junk[:, k % 2, :], ring[k % RING][:, 0:D], 1.0, h2_cur, ALU.mult, ALU.mult,
                               accum_out=dots[:, k:k + 1])
                    if k % BATCH == BATCH - 1:
                        last.then_inc(dots_done, 1)
                    if k % 2:
                        dve.drain()

            def finish(i):
                dve.wait_ge(acc_copied, i + 2)
                TT(acc_sb, acc_sb, gate2_row, ALU.mult)
                dve.drain()
                dve.wait_ge(x1_end_loaded, 16 * (i + 1))
                TT(acc_sb, acc_sb, x1_end, ALU.add)
                dve.drain()
                STT(dot_junk[:, 0, :], acc_sb, 1.0, acc_sb, ALU.mult, ALU.mult, accum_out=small[:, 3:4])
                dve.drain()
                TS(small[:, 4:5], small[:, 3:4], 1.0 / D, EPS, ALU.mult, ALU.add).then_inc(mean3_done, 1)
                dve.wait_ge(root3_done, i + 1)
                nc.vector.reciprocal(small[:, 5:6], small[:, 4:5])
                dve.drain()
                STT(x1_end, acc_sb, small[:, 5:6], final_row, ALU.mult, ALU.mult).then_inc(out_ready, 1)
                dve.drain()

            def head(j, front, very_first=False):
                for b in range(NB - 1):
                    dot_batch(j, b)
                    if very_first and b == 1:
                        pick_keys(1)
                        pick_experts(1)
                if front:
                    pick_keys(j + AHEAD)
                dot_batch(j, NB - 1)
                if front:
                    pick_experts(j + AHEAD)

            def tile_body(i, first, last):
                nc.vector.tensor_copy(h2_cur, h2_next)
                dve.drain()
                if first:
                    head(0, True, very_first=True)
                with dve.Fori(1 if first else 0, PH - AHEAD) as h:
                    head(i * PH + h, True)
                if not last:
                    front_norm(i + 1)
                if not first:
                    finish(i - 1)
                with dve.Fori(PH - AHEAD, PH) as h:
                    head(i * PH + h, not last)

            front_norm(0)
            pick_keys(0)
            pick_experts(0)
            tile_body(0, True, False)
            with dve.Fori(1, NT - 1) as i:
                tile_body(i, False, False)
            tile_body(NT - 1, False, True)
            finish(NT - 1)

        @block.tensor
        def _(pe):
            mm = nc.tensor.matmul
            pe.wait_ge(silu_done, 1)
            for c in range(ME):
                u = c % 2
                pe.wait_ge(w_mod_loaded[u], 16 * (c // 2 + 1))
                if c >= 2:
                    pe.wait_ge(mod_rows, c - 1)
                for k in range(KD):
                    last = mm(bank[u][0:2, :], c_silu[:, k, :], w_mod_ring[:, u, k, :], start=(k == 0), stop=(k == KD - 1))
                last.then_inc(mod_matmul, 1)
            pe.wait_ge(mod_rows, ME)

            def transpose_tile(t, u):
                pe.wait_ge(xhat_ready, t + 1)
                for k in range(KD):
                    last = nc.tensor.transpose(bank[2 * u + k // 4][:, (k % 4) * P:(k % 4 + 1) * P],
                                               xhat[:, u, k * P:(k + 1) * P], ident)
                last.then_inc(x_transposed, 1)

            for u in range(2):
                transpose_tile(u, u)
            with pe.Fori(1, (NT + NTC) // 2) as n:
                for u in range(2):
                    t = 2 * n + u
                    pe.wait_ge(h_act, t - 1)
                    pe.wait_ge(h_dve, t - 1)
                    transpose_tile(t, u)
            pe.wait_ge(h_act, NT + NTC)
            pe.wait_ge(h_dve, NT + NTC)

            def project(dst, w, cols, k_n=KD, src=hT):
                for k in range(k_n):
                    last = mm(dst, w[:, k, :], src[:, k, cols], start=(k == 0), stop=(k == k_n - 1))
                return last

            with pe.Fori(0, G // 2) as n:
                for u in range(2):
                    g = 2 * n + u
                    pe.wait_ge(w_loaded[u], 16 * (n + 1))
                    for j in range(NH):
                        last = project(bank[j][:, :], w_a[u], slice(TC + j * H, TC + (j + 1) * H))
                    last.then_inc(zf_done, 1)
                    pe.wait_ge(mod_summed, 2 * g + 2)
                    for v in range(2):
                        mm(bank[2 + v][0:1, :], ones, mod_sum[:, v, :], start=True, stop=True)
                    pe.wait_ge(zf_copied, 2 * g + 2)
                    mm(bank[6][0:1, 2 * P:3 * P], zfT[:, T:T + 1], dft_fwd[:, 0:P], start=True, stop=True)
                    for t in range(NF):
                        mm(bank[4 + t][:, 0:2 * P], zfT[:, t * P:(t + 1) * P], dft_fwd, start=True, stop=False)
                        last = mm(bank[4 + t][:, 0:2 * P], zfT[:, H + t * P:H + (t + 1) * P], dft_rev,
                                  start=False, stop=True)
                    last.then_inc(pq_done, 1)
                    pe.wait_ge(pq_copied, 2 * g + 2)
            pe.wait_ge(mod_late, MC - ME)
            for t in range(NF):
                pe.wait_ge(dft_loaded[t % 2], 16 * (t // 2 + 1))
                for g in range(G):
                    for c in range(2):
                        for j in range(NH):
                            last = mm(bank[2 * g + j][:, :], PQ[:, t, g, c * P:(c + 1) * P], dft_t[t % 2][:, c, j * H:(j + 1) * H],
                                      start=(t == 0 and c == 0), stop=False)
                last.then_inc(dft_used, 1)
            for g in range(G):
                for j in range(NH):
                    last = mm(bank[2 * g + j][:, :], pq_mid[:, g * P:(g + 1) * P], dft_mid[:, j * H:(j + 1) * H],
                              start=False, stop=True)
            last.then_inc(y_done, 1)
            pe.wait_ge(y_copied, 2)
            def project_zx(r, u, loads):
                pe.wait_ge(w_loaded[u], 16 * (G // 2) + 32 * loads)
                pe.wait_ge(zx_copied, r + 1)
                project(bank[2][:, 0:TC], w_a[u], slice(0, TC))
                for j in range(NH):
                    last = project(bank[j][:, :], w_a[u], slice(TC + j * H, TC + (j + 1) * H))
                last.then_inc(zx_done, 1)

            def project_zy(r, u):
                pe.wait_ge(zy_read, r + 1)
                for j in range(NH):
                    last = project(bank[3 + j][:, :], w_b[u], slice(TC + j * H, TC + (j + 1) * H))
                last.then_inc(zy_done, 1)

            def lru_gates(r, u, loads):
                pe.wait_ge(gate_w_loaded[u], 16 * loads)
                pe.wait_ge(conv_done, r + 1)
                for m in range(4):
                    for p, (a, b) in enumerate([(0, TC), (TC, TC + H), (TC + H, TA)]):
                        pe.wait_ge(gate_read, 12 * r + 3 * m + p + 1)
                        mm(bank[5 + p][:, 0:b - a], w_g[u][:, m, :], xc[:, a:b], start=True, stop=True)\
                            .then_inc(gate_done, 1)

            project_zx(0, 0, 1)
            project_zy(0, 0)
            with pe.Fori(0, R // 2 - 1) as n:
                for u in range(2):
                    r = 2 * n + u
                    project_zx(r + 1, 1 - u, n + 1 + u)
                    lru_gates(r, u, n + 1)
                    project_zy(r + 1, 1 - u)
            project_zx(R - 1, 1, R // 2)
            lru_gates(R - 2, 0, R // 2)
            project_zy(R - 1, 1)
            lru_gates(R - 1, 1, R // 2)
            pe.wait_ge(zx_copied, R + 1)
            pe.wait_ge(zy_read, R + 1)
            pe.wait_ge(gate_read, 12 * R + 3)
            with pe.Fori(0, KD // 2) as n:
                for u in range(2):
                    d = 2 * n + u
                    pe.wait_ge(w_loaded[u], 16 * (G // 2) + 32 * (R // 2) + 64 * (n + 1))
                    pe.wait_ge(ga_read, d + 1)
                    for j in range(NH):
                        last = project(bank[j][:, :], w_a[u], slice(TC + j * H, TC + (j + 1) * H))
                    last.then_inc(ga_done, 1)
                    pe.wait_ge(ya_read, d + 1)
                    for j in range(NH):
                        last = project(bank[2 + j][:, :], w_f[u], slice(j * H, (j + 1) * H), G, yT)
                    last.then_inc(ya_done, 1)
                    pe.wait_ge(gb_read, d + 1)
                    for j in range(NH):
                        last = project(bank[4 + j][:, :], w_b[u], slice(TC + j * H, TC + (j + 1) * H))
                    last.then_inc(gb_done, 1)
                    pe.wait_ge(yb_read, d + 1)
                    pe.wait_ge(yb_ready, R + 1)
                    for j in range(NH):
                        last = project(bank[6 + j][:, :], w_l[u], slice(j * H, (j + 1) * H), R, ybT)
                    last.then_inc(yb_done, 1)
            pe.wait_ge(w_out_loaded, 16 * (KD + 2))
            pe.wait_ge(ga_read, KD + 1)
            pe.wait_ge(ya_read, KD + 1)
            for u in range(2):
                pe.wait_ge(tile_staged, u + 1)
                for j in range(2):
                    for k in range(KD):
                        last = mm(bank[2 * u + j][:, :], merged_tile[u][:, k, :], w_out_k[k][:, j * H:(j + 1) * H],
                                  start=(k == 0), stop=(k == KD - 1))
                last.then_inc(mix_done, 1)
            with pe.Fori(1, NT // 2) as n:
                for u in range(2):
                    i = 2 * n + u
                    pe.wait_ge(tile_staged, i + 1)
                    pe.wait_ge(x1_ready, i - 1)
                    for j in range(2):
                        for k in range(KD):
                            last = mm(bank[2 * u + j][:, :], merged_tile[u][:, k, :], w_out_k[k][:, j * H:(j + 1) * H],
                                      start=(k == 0), stop=(k == KD - 1))
                    last.then_inc(mix_done, 1)
            pe.wait_ge(x1_ready, NT)

            pe.wait_ge(wq_loaded, 16 * (KD + 1))

            def transpose_h2(i):
                pe.wait_ge(h2_ready, i + 1)
                pe.wait_ge(h2T_ready, i + 1)
                for k in range(KD):
                    last = nc.tensor.transpose(bank[2 + k // 4][:, (k % 4) * P:(k % 4 + 1) * P],
                                               h2_next[:, k * P:(k + 1) * P], ident)
                last.then_inc(h2_transposed, 1)

            def query(f, h):
                pe.wait_ge(q_copied, f + 1)
                for k in range(KD):
                    last = mm(bank[4][:, 0:2 * P], h2T[:, k, :], wq_k[k][:, ds(h * 2 * P, 2 * P)],
                              start=(k == 0), stop=(k == KD - 1))
                last.then_inc(q_done, 1)

            def query_T(f):
                pe.wait_ge(q_copied, f + 2)
                pe.wait_ge(qT_copied, f + 1)
                for p in range(2):
                    last = nc.tensor.transpose(bank[5][:, p * P:(p + 1) * P], q_sb[:, p * P:(p + 1) * P], ident)
                last.then_inc(qT_done, 1)

            def scores(f, h):
                pe.wait_ge(qT_copied, f + 2)
                pe.wait_ge(score_copied, f + 1)
                for p in range(2):
                    last = mm(bank[6][:, p * NK:(p + 1) * NK], qT_sb[:, p, :],
                              keys_T[:, ds(2 * h + p, 1), :].rearrange("p a n -> p (a n)"), start=True, stop=True)
                last.then_inc(score_done, 1)

            def acc_edge(start):
                for c in range(2):
                    last = mm(bank[c][:, :], zero[:, :], final_row[:, c * H:(c + 1) * H], start=start, stop=not start,
                              skip_group_check=True)
                return last

            def add_rows(j, b):
                for k in range(b * BATCH, (b + 1) * BATCH):
                    pe.wait_ge(diag_done, TOPK * j + k + 1)
                    for c in range(2):
                        last = mm(bank[c][:, :], diag[:, k % BATCH, :], ring[k % RING][:, D + c * H:D + (c + 1) * H],
                                  start=False, stop=False, skip_group_check=True)
                    last.then_inc(ring_free, 1)

            def head(j, front, h):
                f = j + AHEAD
                if front:
                    query(f, h)
                add_rows(j, 0)
                if front:
                    query_T(f)
                add_rows(j, 1)
                if front:
                    scores(f, h)
                add_rows(j, 2)
                add_rows(j, 3)

            def tile_body(i, last):
                pe.wait_ge(acc_copied, i + 1)
                acc_edge(True)
                with pe.Fori(0, PH - AHEAD) as h:
                    head(i * PH + h, True, h + AHEAD)
                if not last:
                    transpose_h2(i + 1)
                    pe.wait_ge(h2T_ready, i + 3)
                    pe.nop(nofuse=True)
                with pe.Fori(0, AHEAD) as h:
                    head(i * PH + PH - AHEAD + h, not last, h)
                acc_edge(False).then_inc(acc_done, 1)

            transpose_h2(0)
            pe.wait_ge(h2T_ready, 2)
            for h in range(AHEAD):
                query(h, h)
                query_T(h)
                scores(h, h)
            tile_body(0, False)
            with pe.Fori(1, NT - 1) as i:
                tile_body(i, False)
            tile_body(NT - 1, True)


def kernel(**inputs):
    import numpy as np
    import concourse.bacc as bacc
    from concourse import mybir as my
    from concourse.bass_utils import run_bass_kernel_spmd as run

    P, GRID_W, TOPK = 128, 64, 16
    x = inputs["x"][0]
    T, D = x.shape
    KD = D // P
    cc = np.ascontiguousarray

    def cols(a):
        a = np.asarray(a)
        return np.moveaxis(a.reshape(a.shape[:-1] + (a.shape[-1] // P, P)), -1, 0)

    def chunks(w, width):
        k, n = w.shape
        return cc(w.reshape(k // P, P, n // width, width).transpose(2, 1, 0, 3))

    nf = D // 4
    omega = 1.0 / (10000.0 ** (np.arange(nf, dtype=np.float64) / nf))
    er = np.repeat(np.arange(T // GRID_W), GRID_W)[:, None] * omega[None]
    ec = np.tile(np.arange(GRID_W), P // GRID_W)[:, None] * omega[None]
    ang = 2 * np.pi * (np.outer(np.arange(P), np.arange(P)) % P) / P
    dft_c = np.concatenate([np.cos(ang), np.sin(ang)], axis=1) / np.sqrt(P)
    ang = 2 * np.pi * (np.outer(np.arange(T), np.arange(T)) % T) / T
    dft_t = np.stack([np.cos(ang), -np.sin(ang)], axis=1) / np.sqrt(T)
    dft_rev = np.concatenate([dft_c[:, :P], -dft_c[:, P:]], axis=1)
    iota = np.tile(np.arange(TOPK), (P, 1))

    wa, wx = inputs["lru_wa"][0], inputs["lru_wx"][0]
    ba, bx, lm = inputs["lru_ba"][0], inputs["lru_bx"][0], inputs["lru_lambda"][0]
    cw, cb = inputs["conv_w"][0], inputs["conv_b"][0]
    A = {
        "x": x, "ctx": inputs["ctx"][0],
        "pos_row": np.concatenate([np.sin(er), np.cos(er)], axis=1).astype(np.float32),
        "pos_col": np.concatenate([np.sin(ec), np.cos(ec)], axis=1).astype(np.float32),
        "consts": np.concatenate([np.eye(P), iota, np.ones((P, 1))], axis=1).astype(np.float32),
        "dft_time": dft_t[:T // 2].reshape(T // 2 // P, P, 2, T).astype(np.float32),
        "dft_chan": np.concatenate([dft_c, dft_rev], axis=1).astype(np.float32),
        "dft_mid": dft_t[T // 2, 0][None].astype(np.float32),
        "c_cols": np.stack([cols(inputs["c"][0]), cols(inputs["c_ctx"])], axis=2),
        "w_mod": chunks(inputs["w_mod"][0], 512), "b_mod": inputs["b_mod"],
        "head_vecs": cols(np.stack([cw[0], cw[1], cw[2], cw[3], cb, ba[0], bx[0], ba[1], bx[1], lm[0], lm[1],
                                    inputs["norm1_g"][0]])),
        "w_in": chunks(inputs["w_in"][0], P),
        "wf": chunks(inputs["w_fourier"][0], P), "wl": chunks(inputs["w_lru_out"][0], P),
        "lru_gates": np.stack([wa[0], wx[0], wa[1], wx[1]]).transpose(1, 2, 0, 3),
        "w_out": inputs["w_out"][0], "b_out": inputs["b_out"], "norm2_g": inputs["norm2_g"],
        "final_g": np.asarray(inputs["final_g"])[None],
        "wq": inputs["peer_wq"][0],
        "keys": np.moveaxis(np.asarray(inputs["peer_keys"][0]).reshape(-1, inputs["peer_keys"].shape[3], P), 2, 0),
        "uv": np.concatenate([inputs["peer_u"][0], inputs["peer_v"][0]], axis=1),
    }
    A = {k: cc(v) for k, v in A.items()}
    nc = bacc.Bacc("TRN2", target_bir_lowering=False, num_devices=1)
    t_in = {k: nc.dram_tensor("in_" + k, v.shape, my.dt.from_np(v.dtype), kind="ExternalInput").ap() for k, v in A.items()}
    out = nc.dram_tensor("out_tokens", (T, D), my.dt.float32, kind="ExternalOutput").ap()
    mod_dram = nc.dram_tensor("modulation_rows", (2, 6 * D), my.dt.float32, kind="Internal").ap()
    x1_dram = nc.dram_tensor("x1_tokens", (T, D), my.dt.float32, kind="Internal").ap()
    build_block(nc, t_in, mod_dram, x1_dram, out)
    r = run(nc, [{"in_" + k: v for k, v in A.items()}], core_ids=[0])
    return r.results[0]["out_tokens"].reshape(1, T, D)
```

```python
import concourse.bass as bass
from concourse import mybir
from contextlib import ExitStack


def build_block(nc, t_in, mod_dram, x1_dram, out):
    f32, bf16, u32 = mybir.dt.float32, mybir.dt.bfloat16, mybir.dt.uint32
    ALU, ACT, AXX = mybir.AluOpType, mybir.ActivationFunctionType, mybir.AxisListType.X
    ds = bass.ds

    P = 128
    T, D = out.shape
    TC = t_in["ctx"].shape[0]
    KD = D // P
    NT = T // P
    NTC = TC // P
    G = t_in["wf"].shape[2]
    R = t_in["lru_gates"].shape[0]
    TA = TC + T
    H = 512
    NH = T // H
    MC = t_in["w_mod"].shape[0]
    PH = t_in["keys"].shape[1] // 2
    NK = t_in["keys"].shape[2]
    TOPK = 16
    RING = 8
    BATCH = 4
    NB = TOPK // BATCH
    END_AT = 2
    AHEAD = 2
    NF = NT // 2
    ME = 4
    EPS = 1e-6
    LRU_C = 8.0
    NEG = -3.0e38
    WSLOT = 3584
    ZX0, ZY0, ZGA0, ZGB0 = G, G + R, G + 2 * R, G + 2 * R + KD

    ctx = ExitStack()
    with ctx:
        def sb(name, shape, dt=f32):
            return ctx.enter_context(nc.sbuf_tensor(name, shape, dt))

        def sem(name):
            return ctx.enter_context(nc.semaphore(name))

        xs = sb("xs", [P, NT, D])
        lru = sb("lru", [P, 9 * 1288])
        hT = sb("hT", [P, KD, TA])
        ybT = sb("ybT", [P, KD, T])
        yT = sb("yT", [P, G, T])
        wgt = sb("wgt", [P, 2 * WSLOT])

        consts = sb("consts", [P, P + TOPK + 1])
        ident, iota, ones = consts[:, 0:P], consts[:, P:P + TOPK], consts[:, P + TOPK:P + TOPK + 1]
        head_vecs = sb("head_vecs", [P, 12, R])
        c_cols = sb("c_cols", [P, KD, 2])
        c_silu = sb("c_silu", [P, KD, 2])
        mod_cols = sb("mod_cols", [P, 4, KD])
        gain1 = sb("gain1", [P, 2, KD])
        lam = sb("lam", [P, 8, 2 * R])
        ssq = sb("ssq", [P, NT + NTC])
        rstd = sb("rstd", [P, NT + NTC])
        zero = sb("zero", [P, P])
        small = sb("small", [P, 8])
        s_sb = sb("s_sb", [P, 2, NK])
        s_rep = sb("s_rep", [P, NK])
        cand = sb("cand", [P, TOPK, TOPK])
        cand_rep = sb("cand_rep", [P, TOPK, TOPK])
        q_sb = sb("q_sb", [P, 2 * P])
        qT_sb = sb("qT_sb", [P, 2, P])
        key_val = sb("key_val", [P, 2, TOPK])
        key_idx = sb("key_idx", [P, 2, TOPK], u32)
        key_idxf = sb("key_idxf", [P, 2, TOPK])
        top_val = sb("top_val", [P, TOPK])
        top_pos = sb("top_pos", [P, TOPK], u32)
        top_ab = sb("top_ab", [P, 2, TOPK], u32)
        top_abf = sb("top_abf", [P, 2, TOPK])
        picked = sb("picked", [P, 2, TOPK])
        top_exp = sb("top_exp", [P, TOPK])
        soft = sb("soft", [P, 4])
        dots = sb("dots", [P, TOPK])
        gact = sb("gact", [P, BATCH])
        wrow = sb("wrow", [P, BATCH])
        diag = sb("diag", [P, BATCH, P])
        idx_stage = sb("idx_stage", [P, TOPK], u32)
        sq_junk = sb("sq_junk", [P, D], bf16)

        pos_row = lru[:, 0:NT * H].rearrange("p (i n) -> p i n", i=NT)
        pos_col = lru[:, 4096:4608]
        dft_mid = lru[0:1, 5632:5632 + H + 1]
        dft_chan = lru[:, 5632 + T:5632 + T + 4 * P]
        dft_fwd, dft_rev = dft_chan[:, 0:2 * P], dft_chan[:, 2 * P:4 * P]
        mod_stage = lru[:, 8192:9216].rearrange("p (b n) -> p b n", b=2)
        mod_sum = lru[:, 9216:10240].rearrange("p (b n) -> p b n", b=2)
        w_mod_ring = ybT[:, :, :].rearrange("p a n -> p (a n)").rearrange("p (b k n) -> p b k n", b=2, k=KD)
        b_mod = [wgt[0:2, u * WSLOT + 3072:(u + 1) * WSLOT] for u in range(2)]
        xhat = yT[:, 0:2, :]
        ctx_raw = yT[:, 2:2 + NTC, :]
        zfT = yT[:, 0:2, :].rearrange("p a n -> p (a n)")[:, 0:T + 1]
        PQ = lru[:, 0:NF * G * 2 * P].rearrange("p (t g n) -> p t g n", t=NF, g=G)
        pq_mid = lru[0:1, 4096:4096 + G * P]

        def wview(u, at, k):
            return wgt[:, u * WSLOT + at:u * WSLOT + at + k * P].rearrange("p (k n) -> p k n", k=k)

        w_a = [wview(u, 0, KD) for u in range(2)]
        w_b = [wview(u, 1024, KD) for u in range(2)]
        w_g = [wview(u, 2048, 4) for u in range(2)]
        w_l = [wview(u, 2048, KD) for u in range(2)]
        w_f = [wview(u, 3072, G) for u in range(2)]
        dft_t = [wgt[:, u * WSLOT + 1024:u * WSLOT + 1024 + 2 * H + 1] for u in range(2)]

        def larr(i):
            return lru[:, i * 1288:i * 1288 + TA]
        zpad = lru[:, 8 * 1288:8 * 1288 + TA + 6]
        ZL = TC + 3
        xc, tmp = larr(0), larr(1)
        rg, ig, ag = [larr(2), larr(3)], [larr(4), larr(5)], [larr(6), larr(7)]
        merged = lru[:, 0:KD * T].rearrange("p (k n) -> p k n", k=KD)
        sig_a, sig_b = lru[:, 8192:9216], lru[:, 9216:10240]

        hT_flat = hT[:, :, :].rearrange("p a n -> p (a n)")
        ybT_flat = ybT[:, :, :].rearrange("p a n -> p (a n)")
        wq_k = [hT_flat[:, k * 2048:(k + 1) * 2048] for k in range(5)] + \
               [ybT_flat[:, k * 2048:(k + 1) * 2048] for k in range(3)]
        keys_T = ybT_flat[:, 6144:8192].rearrange("p (m n) -> p m n", m=2 * PH)
        ring = [lru[:, s * 2 * D:(s + 1) * 2 * D] for s in range(4)] + \
               [xs[:, 2 * s:2 * s + 2, :].rearrange("p a n -> p (a n)") for s in range(4)]
        dot_junk = lru[:, 8192:9216].bitcast(bf16).rearrange("p (b n) -> p b n", b=2)
        eidx = lru[:, 9216:10240].bitcast(u32)
        gates = lru[:, 10240:11264]
        gain2_row, shift2_row, gate2_row, final_row = (yT[:, j, :] for j in range(4))
        h2T = wgt[:, 0:1024].rearrange("p (k n) -> p k n", k=KD)
        h2_next, h2_cur, x1_front, x1_end, acc_sb, norm2_row = (wgt[:, j * D:(j + 1) * D] for j in range(1, 7))

        bank = [ctx.enter_context(nc.psum_tensor(f"bank{i}", [P, H], f32)) for i in range(8)]

        W_LATE = 7
        w_out_k = [wq_k[k][:, D:2 * D] for k in range(5)] + [gate2_row, final_row, h2_cur]
        merged_tile = [lru[:, 8192:8192 + D].rearrange("p (k n) -> p k n", k=KD),
                       wq_k[5][:, D:2 * D].rearrange("p (k n) -> p k n", k=KD)]
        bout_row, gate1_row, mix_tmp = wq_k[6][:, D:2 * D], x1_end, acc_sb

        setup_loaded = sem("setup_loaded")
        x_loaded = sem("x_loaded")
        silu_done = sem("silu_done")
        w_mod_loaded = [sem("w_mod_loaded0"), sem("w_mod_loaded1")]
        b_mod_loaded = [sem("b_mod_loaded0"), sem("b_mod_loaded1")]
        mod_matmul = sem("mod_matmul")
        mod_rows = sem("mod_rows")
        mod_stored = [sem("mod_stored0"), sem("mod_stored1")]
        mod_cols_loaded = sem("mod_cols_loaded")
        pos_added = sem("pos_added")
        pos_row_added = sem("pos_row_added")
        squares = sem("squares")
        means = sem("means")
        roots = sem("roots")
        lam_dve = sem("lam_dve")
        lam_act = sem("lam_act")
        xhat_ready = sem("xhat_ready")
        x_transposed = sem("x_transposed")
        h_act = sem("h_act")
        h_dve = sem("h_dve")
        w_loaded = [sem("w_loaded0"), sem("w_loaded1")]
        gate_w_loaded = [sem("gate_w_loaded0"), sem("gate_w_loaded1")]
        mod_summed = sem("mod_summed")
        mod_late = sem("mod_late")
        dft_loaded = [sem("dft_loaded0"), sem("dft_loaded1")]
        dft_used = sem("dft_used")
        zf_done = sem("zf_done")
        zf_copied = sem("zf_copied")
        pq_done = sem("pq_done")
        pq_copied = sem("pq_copied")
        y_done = sem("y_done")
        y_even_copied = sem("y_even_copied")
        y_copied = sem("y_copied")
        zx_done = sem("zx_done")
        zx_copied = sem("zx_copied")
        zy_done = sem("zy_done")
        zy_read = sem("zy_read")
        conv_started = sem("conv_started")
        conv_done = sem("conv_done")
        gate_done = sem("gate_done")
        gate_read = sem("gate_read")
        gx_done = sem("gx_done")
        decay_squared = sem("decay_squared")
        norm_ready = sem("norm_ready")
        norm_root = sem("norm_root")
        yb_ready = sem("yb_ready")
        ga_done, ya_done, gb_done, yb_done = sem("ga_done"), sem("ya_done"), sem("gb_done"), sem("yb_done")
        ga_read, gb_read = sem("ga_read"), sem("gb_read")
        ya_read, yb_read = sem("ya_read"), sem("yb_read")
        merge_done = sem("merge_done")
        w_out_loaded = sem("w_out_loaded")
        gate1_loaded = sem("gate1_loaded")
        bout_gated = sem("bout_gated")
        tile_staged = sem("tile_staged")
        bias_added = sem("bias_added")
        mix_done = sem("mix_done")
        x1_ready = sem("x1_ready")
        x1_stored = sem("x1_stored")
        wq_loaded = sem("wq_loaded")
        wq_late_loaded = sem("wq_late_loaded")
        rows_loaded = sem("rows_loaded")
        late_rows_loaded = sem("late_rows_loaded")
        x1_front_loaded = sem("x1_front_loaded")
        x1_carried = sem("x1_carried")
        sq2_done = sem("sq2_done")
        mean2_done = sem("mean2_done")
        root2_done = sem("root2_done")
        h2_ready = sem("h2_ready")
        h2_transposed = sem("h2_transposed")
        h2T_ready = sem("h2T_ready")
        q_done = sem("q_done")
        q_copied = sem("q_copied")
        qT_done = sem("qT_done")
        qT_copied = sem("qT_copied")
        score_done = sem("score_done")
        score_copied = sem("score_copied")
        max_ready = sem("max_ready")
        exp_done = sem("exp_done")
        picks_done = sem("picks_done")
        landed = [sem(f"landed{s}") for s in range(RING)]
        ring_free = sem("ring_free")
        idx_staged = sem("idx_staged")
        dots_done = sem("dots_done")
        diag_done = sem("diag_done")
        acc_done = sem("acc_done")
        acc_copied = sem("acc_copied")
        y_squared = sem("y_squared")
        mean3_done = sem("mean3_done")
        root3_done = sem("root3_done")
        out_ready = sem("out_ready")
        out_stored = sem("out_stored")

        SETUP = 5

        block = ctx.enter_context(nc.Block())

        @block.sync
        def _(sp):
            sp.dma_start(consts[:, :], t_in["consts"]).then_inc(setup_loaded, 16)
            sp.dma_start(c_cols[:, :, :], t_in["c_cols"]).then_inc(setup_loaded, 16)
            sp.dma_start(head_vecs[:, :, :], t_in["head_vecs"]).then_inc(setup_loaded, 16)
            sp.dma_start(dft_mid, t_in["dft_mid"]).then_inc(setup_loaded, 16)
            sp.dma_start(dft_chan, t_in["dft_chan"]).then_inc(setup_loaded, 16)

            def load_mod(c):
                sp.dma_start(w_mod_ring[:, c % 2], t_in["w_mod"][c]).then_inc(w_mod_loaded[c % 2], 16)

            def load_mod_bias(c):
                sp.dma_start(b_mod[c % 2], t_in["b_mod"][:, c * H:(c + 1) * H].to_broadcast([2, H]))\
                    .then_inc(b_mod_loaded[c % 2], 16)

            for c in range(2):
                load_mod(c)
                load_mod_bias(c)
            xv = t_in["x"].rearrange("(i p) n -> p i n", p=P)
            for j in range(2):
                sp.dma_start(xs[:, 4 * j:4 * j + 4, :], xv[:, 4 * j:4 * j + 4, :]).then_inc(x_loaded, 16)
            sp.dma_start(pos_row, t_in["pos_row"].rearrange("(i p) n -> p i n", p=P)).then_inc(x_loaded, 16)
            sp.dma_start(pos_col, t_in["pos_col"]).then_inc(x_loaded, 16)
            sp.dma_start(ctx_raw, t_in["ctx"].rearrange("(i p) n -> p i n", p=P)).then_inc(x_loaded, 16)
            for c in range(ME):
                sp.wait_ge(mod_rows, c + 1)
                sp.dma_start(mod_dram[:, c * H:(c + 1) * H], mod_stage[0:2, c % 2, :]).then_inc(mod_stored[c % 2], 16)
                load_mod(c + 2)
                load_mod_bias(c + 2)
            for u in range(2):
                sp.wait_ge(mod_stored[u], 16 * (ME // 2))
            for j in range(2):
                for r in range(2):
                    sp.dma_start(mod_cols[:, 2 * j + r, :],
                                 mod_dram[r:r + 1, j * D:(j + 1) * D].rearrange("a (k p) -> p (a k)", p=P),
                                 allow_slow_non_contiguous=True)\
                        .then_inc(mod_cols_loaded, 16)
            for u in range(2):
                sp.dma_start(w_a[u], t_in["w_in"][u]).then_inc(w_loaded[u], 16)
                sp.dma_start(dft_t[u], t_in["dft_time"][u]).then_inc(dft_loaded[u], 16)
            for g in range(G):
                if 0 < g < G - 1:
                    sp.wait_ge(zf_done, g)
                    sp.dma_start(w_a[(g + 1) % 2], t_in["w_in"][g + 1]).then_inc(w_loaded[(g + 1) % 2], 16)
                for u in range(2):
                    c = ME + 2 * g + u
                    if c + 2 < MC:
                        sp.wait_ge(mod_summed, c - ME + 1)
                        load_mod(c + 2)
                for u in range(2):
                    c = ME + 2 * g + u
                    sp.wait_ge(mod_late, c - ME + 1)
                    sp.dma_start(mod_dram[0:1, c * H:(c + 1) * H], mod_stage[0:1, u, :]).then_inc(mod_stored[u], 16)
                    if c + 2 < MC:
                        load_mod_bias(c + 2)
            for t in range(2, NF):
                sp.wait_ge(dft_used, t - 1)
                sp.dma_start(dft_t[t % 2], t_in["dft_time"][t]).then_inc(dft_loaded[t % 2], 16)
            def load_head(r, u):
                for dst, at in ((w_a[u], ZX0), (w_b[u], ZY0)):
                    sp.dma_start(dst, t_in["w_in"][ds(r + at, 1)].rearrange("a p k n -> (a p) k n")).then_inc(w_loaded[u], 16)

            def load_gates(r, u):
                sp.dma_start(w_g[u], t_in["lru_gates"][ds(r, 1)].rearrange("a p k n -> (a p) k n"))\
                    .then_inc(gate_w_loaded[u], 16)

            for u in range(2):
                sp.wait_ge(dft_used, NF - 1)
                if u == 1:
                    sp.wait_ge(y_done, G)
                load_head(u, u)
                load_gates(u, u)
            with sp.Fori(1, R // 2) as n:
                for u in range(2):
                    r = 2 * n + u
                    sp.wait_ge(zy_done, r - 1)
                    load_head(r, u)
                    sp.wait_ge(gate_done, 12 * (r - 1))
                    load_gates(r, u)
            def load_merge(d, u):
                for dst, src, at in ((w_a[u], "w_in", ZGA0), (w_f[u], "wf", 0), (w_b[u], "w_in", ZGB0), (w_l[u], "wl", 0)):
                    sp.dma_start(dst, t_in[src][ds(d + at, 1)].rearrange("a p k n -> (a p) k n")).then_inc(w_loaded[u], 16)

            for u in range(2):
                sp.wait_ge(zy_done, R - 1 + u)
                sp.wait_ge(gate_done, 12 * (R - 1 + u))
                load_merge(u, u)
            with sp.Fori(1, KD // 2) as n:
                for u in range(2):
                    sp.wait_ge(yb_done, 2 * n + u - 1)
                    load_merge(2 * n + u, u)
            for u in range(2):
                sp.wait_ge(mod_stored[u], 16 * (MC // 2))

            def load_w_out(k):
                sp.dma_start(w_out_k[k], t_in["w_out"][k * P:(k + 1) * P, :]).then_inc(w_out_loaded, 16)

            def load_wq(k, a, b, loaded):
                sp.dma_start(wq_k[k][:, a:b], t_in["wq"][k * P:(k + 1) * P, a:b]).then_inc(loaded, 16)

            def load_row(dst, src, loaded):
                sp.dma_start(dst, src.to_broadcast([P, D])).then_inc(loaded, 16)

            sp.wait_ge(yb_done, KD - 1)
            load_w_out(7)
            sp.wait_ge(ya_done, KD)
            for k in (5, 6):
                load_w_out(k)
            load_row(gain2_row, mod_dram[0:1, 4 * D:5 * D], rows_loaded)
            load_row(shift2_row, mod_dram[0:1, 3 * D:4 * D], rows_loaded)
            sp.wait_ge(gb_done, KD)
            for k in range(5):
                load_w_out(k)
            load_row(gate1_row, mod_dram[0:1, 2 * D:3 * D], gate1_loaded)
            sp.wait_ge(yb_done, KD)
            load_row(bout_row, t_in["b_out"], gate1_loaded)
            load_row(norm2_row, t_in["norm2_g"], rows_loaded)
            for k in range(W_LATE):
                load_wq(k, 0, D, wq_loaded)
            load_wq(W_LATE, 0, 2 * D, wq_loaded)
            sp.dma_start(keys_T, t_in["keys"]).then_inc(wq_loaded, 16)

            def store_x1(i):
                sp.wait_ge(x1_ready, i + 3)
                sp.dma_start(x1_dram[i * P:(i + 1) * P, :], xs[:, i, :]).then_inc(x1_stored, 16)
                sp.wait_ge(x1_stored, 16 * (i + 1))

            store_x1(0)
            sp.dma_start(x1_front, x1_dram[0:P, :]).then_inc(x1_front_loaded, 16)
            for i in range(1, NT):
                store_x1(i)
            sp.wait_ge(mix_done, NT + 2)
            sp.wait_ge(bias_added, NT)
            for k in range(W_LATE):
                load_wq(k, D, 2 * D, wq_late_loaded)
            load_row(gate2_row, mod_dram[0:1, 5 * D:6 * D], late_rows_loaded)
            load_row(final_row, t_in["final_g"], late_rows_loaded)

            def store_out(i):
                sp.wait_ge(out_ready, i + 1)
                sp.dma_start(out[ds(i * P, P), :], acc_sb).then_inc(out_stored, 16)

            def fetch_front(i):
                sp.wait_ge(x1_carried, i)
                sp.dma_start(x1_front, x1_dram[ds(i * P, P), :]).then_inc(x1_front_loaded, 16)

            fetch_front(1)
            with sp.Fori(1, NT - 1) as i:
                store_out(i - 1)
                fetch_front(i + 1)
            for i in range(NT - 2, NT):
                store_out(i)
            sp.wait_ge(out_stored, 16 * (NT + 1))

        @block.gpsimd
        def _(pool):
            pool.sem_inc(zx_copied, 1)
            pool.sem_inc(zy_read, 1)
            pool.sem_inc(gate_read, 3)
            pool.sem_inc(yb_ready, 1)
            pool.sem_inc(ga_read, 1)
            pool.sem_inc(gb_read, 1)
            pool.sem_inc(ya_read, 1)
            pool.sem_inc(yb_read, 1)
            pool.sem_inc(merge_done, 1)
            pool.sem_inc(mix_done, 2)
            pool.sem_inc(x1_ready, 2)
            pool.sem_inc(h2_transposed, 1)
            pool.sem_inc(h2T_ready, 1)
            pool.sem_inc(q_copied, 1)
            pool.sem_inc(qT_copied, 1)
            pool.sem_inc(score_copied, 1)
            pool.sem_inc(acc_copied, 1)
            pool.sem_inc(out_stored, 16)
            pool.sem_inc(ring_free, RING)
            pool.wait_ge(x_loaded, 16 * 5)
            with pool.Fori(0, NT) as i:
                xt = xs[:, ds(i, 1), :].rearrange("p a n -> p (a n)")
                nc.gpsimd.tensor_tensor(xt[:, H:D], xt[:, H:D], pos_col, ALU.add).then_inc(pos_added, 1)
            pool.wait_ge(merge_done, KD + 1)
            with pool.Fori(0, NT // 2) as n:
                for u in range(2):
                    i = 2 * n + u
                    pool.wait_ge(mix_done, i + 1)
                    pool.nop(nofuse=True)
                    nc.gpsimd.tensor_copy(merged_tile[u], merged[:, :, ds(i * P, P)]).then_inc(tile_staged, 1)
                    pool.wait_ge(bout_gated, 1)
                    xt = xs[:, ds(i, 1), :].rearrange("p a n -> p (a n)")
                    nc.gpsimd.tensor_tensor(xt, xt, bout_row, ALU.add).then_inc(bias_added, 1)
            def gather_head(j, first=False):
                pool.wait_ge(picks_done, j + 1)
                pool.nop(nofuse=True)
                for k in range(TOPK):
                    if k % RING == 0:
                        nc.gpsimd.tensor_copy(idx_stage[:, k:k + RING], eidx[:, ds(j * TOPK + k, RING)])\
                            .then_inc(idx_staged, 1)
                        pool.wait_ge(idx_staged, 2 * j + k // RING + 1)
                        pool.nop(nofuse=True)
                    if first and k == 0:
                        pool.wait_ge(tile_staged, NT)
                    if first and 4 <= k < RING:
                        pool.wait_ge(x1_stored, 16 * 2 * (k - 3))
                    pool.wait_ge(ring_free, j * TOPK + k + 1)
                    pool.nop(nofuse=True)
                    pool.indirect_dma_start(
                        out=ring[k % RING], out_offset=None, in_=t_in["uv"],
                        in_offset=bass.IndirectOffsetOnAxis(ap=idx_stage[:, k:k + 1], axis=0))\
                        .then_inc(landed[k % RING], 16)

            gather_head(0, first=True)
            with pool.Fori(1, NT * PH) as j:
                gather_head(j)

        @block.scalar
        def _(act):
            act.wait_ge(setup_loaded, 16 * SETUP)
            nc.scalar.activation(c_silu[:, :, :], c_cols[:, :, :], ACT.Silu).then_inc(silu_done, 1)
            act.wait_ge(lam_dve, 1)
            nc.scalar.activation(lam[:, 1, :], lam[:, 0, :], ACT.Exp, scale=-1.0).then_inc(lam_act, 1)
            act.wait_ge(lam_dve, 2)
            nc.scalar.activation(lam[:, 3, :], lam[:, 2, :], ACT.Ln).then_inc(lam_act, 1)
            with act.Fori(0, NT) as i:
                act.wait_ge(pos_row_added, i + 1)
                act.wait_ge(pos_added, i + 1)
                act.nop(nofuse=True)
                nc.scalar.activation(sq_junk[:, :], xs[:, ds(i, 1), :].rearrange("p a n -> p (a n)"), ACT.Square,
                                     accum_out=ssq[:, ds(i, 1)])
                act.drain()
            for i in range(NTC):
                last = nc.scalar.activation(sq_junk[:, :], ctx_raw[:, i, :], ACT.Square,
                                            accum_out=ssq[:, NT + i:NT + i + 1])
                act.drain()
            nc.scalar.activation(small[:, 7:8], ident[:, 0:1], ACT.Copy).then_inc(squares, 1)
            act.wait_ge(means, 1)
            nc.scalar.activation(rstd[:, :], ssq[:, :], ACT.Sqrt).then_inc(roots, 1)
            act.wait_ge(lam_dve, 4)

            def modulate(t, u, which, col):
                act.wait_ge(x_transposed, t + 1)
                act.nop(nofuse=True)
                for k in range(4):
                    last = nc.scalar.activation(hT[:, k, col], bank[2 * u][:, k * P:(k + 1) * P], ACT.Identity,
                                                scale=gain1[:, which, k:k + 1], bias=mod_cols[:, which, k:k + 1])
                last.then_inc(h_act, 1)

            for i in range(NTC):
                modulate(i, i, 1, slice(i * P, (i + 1) * P))
            with act.Fori(0, NT // 2) as n:
                for u in range(2):
                    modulate(NTC + 2 * n + u, u, 0, ds(TC + (2 * n + u) * P, P))
            with act.Fori(0, G) as g:
                act.wait_ge(zf_done, g + 1)
                nc.scalar.activation(zfT[:, 0:H], bank[0][:, :], ACT.Copy).then_inc(zf_copied, 1)
                act.wait_ge(pq_done, g + 1)
                act.nop(nofuse=True)
                for t in range(NF // 2):
                    last = nc.scalar.activation(PQ[:, t, ds(g, 1), :].rearrange("p a n -> p (a n)"), bank[4 + t][:, 0:2 * P],
                                                ACT.Copy)
                last.then_inc(pq_copied, 1)
            for g in range(G):
                act.wait_ge(y_done, g + 1)
                nc.scalar.activation(yT[:, g, 0:H], bank[2 * g][:, :], ACT.Copy).then_inc(y_even_copied, 1)
            act.wait_ge(lam_dve, 5)
            pieces = [(0, TC), (TC, TC + H), (TC + H, TA)]

            def copy_zx(r, first=False):
                act.wait_ge(zx_done, r + 1)
                if not first:
                    act.wait_ge(conv_done, r)
                nc.scalar.activation(zpad[:, 1:1 + TC], bank[2][:, 0:TC], ACT.Copy)
                for j in range(NH):
                    last = nc.scalar.activation(zpad[:, ZL + 1 + j * H:ZL + 1 + (j + 1) * H], bank[j][:, :], ACT.Copy)
                last.then_inc(zx_copied, 1)

            def start_conv(r, first=False):
                if not first:
                    act.wait_ge(gx_done, r)
                act.nop(nofuse=True)
                act.drain()
                w0, cb = head_vecs[:, 0, ds(r, 1)], head_vecs[:, 4, ds(r, 1)]
                nc.scalar.activation(xc[:, 0:TC], zpad[:, 0:TC], ACT.Identity, scale=w0, bias=cb)
                nc.scalar.activation(xc[:, TC:TA], zpad[:, ZL:ZL + T], ACT.Identity, scale=w0, bias=cb)\
                    .then_inc(conv_started, 1)

            def gelu_zy(r):
                act.wait_ge(zy_done, r + 1)
                act.nop(nofuse=True)
                yb_r = ybT[:, ds(r, 1), :].rearrange("p a n -> p (a n)")
                for j in range(NH):
                    last = nc.scalar.activation(yb_r[:, j * H:(j + 1) * H], bank[3 + j][:, :], ACT.Gelu_apprx_tanh)
                last.then_inc(zy_read, 1)

            def lru_head(r, more):
                if more:
                    copy_zx(r + 1)
                act.wait_ge(yb_ready, r + 1)
                act.nop(nofuse=True)
                for m, dst in enumerate((rg[0], ig[0], rg[1], ig[1])):
                    for p, (a, b) in enumerate(pieces):
                        act.wait_ge(gate_done, 12 * r + 3 * m + p + 1)
                        act.nop(nofuse=True)
                        nc.scalar.activation(dst[:, a:b], bank[5 + p][:, 0:b - a], ACT.Sigmoid,
                                             bias=head_vecs[:, 5 + m, ds(r, 1)]).then_inc(gate_read, 1)
                if more:
                    start_conv(r + 1)
                act.drain()
                for v in range(2):
                    nc.scalar.activation(ag[v], rg[v], ACT.Exp, scale=lam[:, 6, ds(v * R + r, 1)])
                act.drain()
                for v in range(2):
                    nc.scalar.activation(rg[v], rg[v], ACT.Tanh, scale=lam[:, 7, ds(v * R + r, 1)])
                nc.scalar.activation(tmp, ag[0], ACT.Square).then_inc(decay_squared, 1)
                if more:
                    act.wait_ge(conv_done, r + 2)
                for a, b, z in ((0, TC, 1), (TC, TA, ZL + 1)):
                    last = nc.scalar.activation(zpad[:, z:z + b - a], ag[1][:, a:b], ACT.Square)
                last.then_inc(decay_squared, 1)
                for v in range(2):
                    act.wait_ge(norm_ready, 2 * r + v + 1)
                    nc.scalar.activation(rg[v], rg[v], ACT.Sqrt).then_inc(norm_root, 1)
                if more:
                    gelu_zy(r + 1)

            copy_zx(0, True)
            start_conv(0, True)
            gelu_zy(0)
            with act.Fori(0, R - 1) as r:
                lru_head(r, True)
            lru_head(R - 1, False)
            act.wait_ge(yb_ready, R + 1)
            with act.Fori(0, KD) as d:
                for done, read, dst, b0 in ((ga_done, ga_read, sig_a, 0), (gb_done, gb_read, sig_b, 4)):
                    act.wait_ge(done, d + 1)
                    act.wait_ge(merge_done, d + 1)
                    for j in range(NH):
                        last = nc.scalar.activation(dst[:, j * H:(j + 1) * H], bank[b0 + j][:, :], ACT.Sigmoid)
                    last.then_inc(read, 1)

            def square_front(i):
                act.wait_ge(x1_front_loaded, 16 * (i + 1))
                nc.scalar.activation(sq_junk[:, :], x1_front, ACT.Square, accum_out=small[:, 0:1]).then_inc(sq2_done, 1)
                act.wait_ge(mean2_done, i + 1)
                nc.scalar.activation(small[:, 1:2], small[:, 1:2], ACT.Sqrt).then_inc(root2_done, 1)

            def copy_h2T(i, b0=2):
                act.wait_ge(h2_transposed, i + 2)
                for j in range(2):
                    last = nc.scalar.activation(h2T[:, 4 * j:4 * j + 4, :].rearrange("p k n -> p (k n)"), bank[b0 + j][:, :],
                                                ACT.Copy)
                last.then_inc(h2T_ready, 1)

            def copy_q(f):
                act.wait_ge(q_done, f + 1)
                nc.scalar.activation(q_sb[:, :], bank[4][:, 0:2 * P], ACT.Copy).then_inc(q_copied, 1)

            def copy_qT(f):
                act.wait_ge(qT_done, f + 1)
                nc.scalar.activation(qT_sb[:, :, :].rearrange("p a n -> p (a n)"), bank[5][:, 0:2 * P], ACT.Copy)\
                    .then_inc(qT_copied, 1)

            def soft_exp(f):
                act.wait_ge(max_ready, f + 1)
                nc.scalar.activation(top_exp[:, :], top_val[:, :], ACT.Exp, bias=soft[:, 0:1],
                                     accum_out=soft[:, 1:2]).then_inc(exp_done, 1)

            def weigh(j, b):
                act.wait_ge(dots_done, NB * j + b + 1)
                nc.scalar.activation(gact[:, :], dots[:, b * BATCH:(b + 1) * BATCH], ACT.Gelu_apprx_tanh)
                act.drain()
                for k in range(BATCH):
                    nc.scalar.activation(wrow[:, k:k + 1], gact[:, k:k + 1], ACT.Copy,
                                         scale=gates[:, ds(j * TOPK + b * BATCH + k, 1)])
                act.drain()
                for k in range(BATCH):
                    act.wait_ge(ring_free, j * TOPK + b * BATCH + k + 1 + RING - BATCH)
                    nc.scalar.activation(diag[:, k, :], ident, ACT.Copy, scale=wrow[:, k:k + 1]).then_inc(diag_done, 1)

            def copy_acc(i):
                act.wait_ge(acc_done, i + 1)
                act.wait_ge(out_stored, 16 * (i + 1))
                act.nop(nofuse=True)
                for h in range(2):
                    last = nc.scalar.activation(acc_sb[:, h * H:(h + 1) * H], bank[h][:, :], ACT.Copy)
                last.then_inc(acc_copied, 1)

            def root_end(i):
                act.wait_ge(mean3_done, i + 1)
                nc.scalar.activation(small[:, 4:5], small[:, 4:5], ACT.Sqrt).then_inc(root3_done, 1)

            def head(j, front):
                f = j + AHEAD
                weigh(j, 0)
                if front:
                    copy_q(f)
                weigh(j, 1)
                if front:
                    copy_qT(f)
                weigh(j, 2)
                weigh(j, 3)
                if front:
                    soft_exp(f)

            def tile_body(i, first, last):
                if not first:
                    copy_acc(i - 1)
                with act.Fori(0, END_AT) as h:
                    head(i * PH + h, True)
                if not first:
                    root_end(i - 1)
                with act.Fori(END_AT, PH - AHEAD) as h:
                    head(i * PH + h, True)
                if not last:
                    square_front(i + 1)
                    copy_h2T(i + 1)
                with act.Fori(PH - AHEAD, PH) as h:
                    head(i * PH + h, not last)

            square_front(0)
            copy_h2T(0, 4)
            for f in range(AHEAD):
                copy_q(f)
                copy_qT(f)
            for f in range(AHEAD):
                soft_exp(f)
            tile_body(0, True, False)
            act.nop(nofuse=True)
            with act.Fori(1, NT - 1) as i:
                tile_body(i, False, False)
            tile_body(NT - 1, False, True)
            copy_acc(NT - 1)
            root_end(NT - 1)

        @block.vector
        def _(dve):
            TT, TS, STT = nc.vector.tensor_tensor, nc.vector.tensor_scalar, nc.vector.scalar_tensor_tensor
            dve.wait_ge(setup_loaded, 16 * SETUP)
            nc.vector.memset(zero[:, :], 0.0)
            lam_in = head_vecs[:, 9:11, :].rearrange("p a r -> p (a r)")
            STT(lam[:, 0, :], lam_in, -1.0, lam_in, ALU.mult, ALU.max).then_inc(lam_dve, 1)
            dve.wait_ge(lam_act, 1)
            TS(lam[:, 2, :], lam[:, 1, :], 1.0, None, ALU.add).then_inc(lam_dve, 1)
            dve.wait_ge(lam_act, 2)
            TS(lam[:, 4, :], lam[:, 2, :], -1.0, None, ALU.add)
            dve.drain()
            TS(lam[:, 5, :], lam[:, 4, :], 0.0, None, ALU.is_equal)
            dve.drain()
            TT(lam[:, 4, :], lam[:, 4, :], lam[:, 5, :], ALU.add)
            TT(lam[:, 3, :], lam[:, 3, :], lam[:, 1, :], ALU.mult)
            TT(lam[:, 5, :], lam[:, 5, :], lam[:, 1, :], ALU.mult)
            dve.drain()
            nc.vector.reciprocal(lam[:, 4, :], lam[:, 4, :])
            dve.drain()
            TT(lam[:, 3, :], lam[:, 3, :], lam[:, 4, :], ALU.mult)
            TS(lam[:, 2, :], lam_in, -1.0, 0.0, ALU.mult, ALU.max)
            dve.drain()
            TT(lam[:, 3, :], lam[:, 3, :], lam[:, 5, :], ALU.add)
            dve.drain()
            TT(lam[:, 3, :], lam[:, 3, :], lam[:, 2, :], ALU.add)
            dve.drain()
            TS(lam[:, 6, :], lam[:, 3, :], -LRU_C, None, ALU.mult)
            TS(lam[:, 7, :], lam[:, 3, :], LRU_C, None, ALU.mult).then_inc(lam_dve, 1)
            def mod_row(c):
                dve.wait_ge(mod_matmul, c + 1)
                dve.wait_ge(b_mod_loaded[c % 2], 16 * (c // 2 + 1))
                if c >= 2:
                    dve.wait_ge(mod_stored[c % 2], 16)
                TT(mod_stage[0:2, c % 2, :], bank[c % 2][0:2, :], b_mod[c % 2], ALU.add).then_inc(mod_rows, 1)

            mod_row(0)
            mod_row(1)
            dve.wait_ge(x_loaded, 16 * 5)
            with dve.Fori(0, NT) as i:
                xt = xs[:, ds(i, 1), :].rearrange("p a n -> p (a n)")
                pr = pos_row[:, ds(i, 1), :].rearrange("p a n -> p (a n)")
                TT(xt[:, 0:H], xt[:, 0:H], pr, ALU.add).then_inc(pos_row_added, 1)
            mod_row(2)
            mod_row(3)
            dve.wait_ge(squares, 1)
            TS(ssq[:, :], ssq[:, :], 1.0 / D, EPS, ALU.mult, ALU.add).then_inc(means, 1)
            dve.wait_ge(roots, 1)
            nc.vector.reciprocal(rstd[:, :], rstd[:, :])
            dve.drain()

            def normalise(u, xin, col):
                TS(xhat[:, u, :], xin, rstd[:, col], None, ALU.mult).then_inc(xhat_ready, 1)

            def normalise_latent(i, u):
                normalise(u, xs[:, ds(i, 1), :].rearrange("p a n -> p (a n)"), ds(i, 1))

            def modulate(t, u, which, col):
                dve.wait_ge(x_transposed, t + 1)
                for k in range(4, KD):
                    last = TS(hT[:, k, col], bank[2 * u + 1][:, (k - 4) * P:(k - 3) * P], gain1[:, which, k:k + 1],
                              mod_cols[:, which, k:k + 1], ALU.mult, ALU.add)
                last.then_inc(h_dve, 1)

            for i in range(NTC):
                normalise(i, ctx_raw[:, i, :], slice(NT + i, NT + i + 1))
            dve.wait_ge(mod_cols_loaded, 16 * 4)
            for which in range(2):
                STT(gain1[:, which, :], mod_cols[:, 2 + which, :], 1.0, head_vecs[:, 11, :], ALU.add, ALU.mult)
            dve.drain()
            nc.vector.memset(small[:, 6:7], 0.0).then_inc(lam_dve, 1)
            for i in range(NTC):
                modulate(i, i, 1, slice(i * P, (i + 1) * P))
                normalise_latent(i, i)
            with dve.Fori(0, NT // 2 - 1) as n:
                for u in range(2):
                    i = 2 * n + u
                    modulate(NTC + i, u, 0, ds(TC + i * P, P))
                    normalise_latent(i + 2, u)
            for u in range(2):
                i = NT - 2 + u
                modulate(NTC + i, u, 0, slice(TC + i * P, TC + (i + 1) * P))
            nc.vector.memset(zfT[:, H:H + 1], 0.0)
            with dve.Fori(0, G) as g:
                for u in range(2):
                    dve.wait_ge(w_mod_loaded[u], 16 * (g + ME // 2 + 1))
                    TS(mod_sum[:, u, :], w_mod_ring[:, u, 0, :], c_silu[:, 0, 0:1], None, ALU.mult)
                    for k in range(1, KD):
                        dve.drain()
                        last = STT(mod_sum[:, u, :], w_mod_ring[:, u, k, :], c_silu[:, k, 0:1], mod_sum[:, u, :],
                                   ALU.mult, ALU.add)
                    last.then_inc(mod_summed, 1)
                dve.wait_ge(zf_done, g + 1)
                nc.vector.tensor_copy(zfT[:, T:T + 1], bank[1][:, 0:1])
                nc.vector.tensor_copy(zfT[:, T - 1:H:-1], bank[1][:, 1:H]).then_inc(zf_copied, 1)
                dve.wait_ge(pq_done, g + 1)
                nc.vector.tensor_copy(pq_mid[:, ds(g * P, P)], bank[6][0:1, 2 * P:3 * P])
                for t in range(NF // 2, NF):
                    last = nc.vector.tensor_copy(PQ[:, t, ds(g, 1), :].rearrange("p a n -> p (a n)"), bank[4 + t][:, 0:2 * P])
                last.then_inc(pq_copied, 1)
                for u in range(2):
                    dve.wait_ge(mod_stored[u], 16 * (g + ME // 2))
                    dve.wait_ge(b_mod_loaded[u], 16 * (g + ME // 2 + 1))
                    TT(mod_stage[0:1, u, :], bank[2 + u][0:1, :], b_mod[u][0:1, :], ALU.add).then_inc(mod_late, 1)
            for g in range(G):
                dve.wait_ge(y_even_copied, g + 1)
                odd = bank[2 * g + 1]
                TT(yT[:, g, T - 1:H:-1], yT[:, g, 1:H], odd[:, 1:H], ALU.subtract)
                TT(yT[:, g, 1:H], yT[:, g, 1:H], odd[:, 1:H], ALU.add)
                nc.vector.tensor_copy(yT[:, g, H:H + 1], odd[:, 0:1]).then_inc(y_copied, 1)
            for a, b in ((0, 1), (1 + TC, ZL + 1), (ZL + 1 + T, ZL + T + 3)):
                last = nc.vector.memset(zpad[:, a:b], 0.0)
            last.then_inc(lam_dve, 1)
            def convolve(r):
                dve.wait_ge(conv_started, r + 1)
                for k in range(1, 4):
                    wk = head_vecs[:, k, ds(r, 1)]
                    STT(xc[:, 0:TC], zpad[:, k:k + TC], wk, xc[:, 0:TC], ALU.mult, ALU.add)
                    last = STT(xc[:, TC:TA], zpad[:, ZL + k:ZL + k + T], wk, xc[:, TC:TA], ALU.mult, ALU.add)
                    if k < 3:
                        dve.drain()
                last.then_inc(conv_done, 1)
                dve.drain()

            def lru_head(r, more):
                for v in range(2):
                    dve.wait_ge(gate_read, 3 + 12 * r + 6 * (v + 1))
                    last = TT(ig[v], ig[v], xc, ALU.mult)
                last.then_inc(gx_done, 1)
                if more:
                    convolve(r + 1)
                dve.wait_ge(decay_squared, 2 * r + 1)
                STT(rg[0], tmp, 1.0, rg[0], ALU.add, ALU.mult).then_inc(norm_ready, 1)
                dve.wait_ge(decay_squared, 2 * r + 2)
                for a, b, z in ((0, TC, 1), (TC, TA, ZL + 1)):
                    last = STT(rg[1][:, a:b], zpad[:, z:z + b - a], 1.0, rg[1][:, a:b], ALU.add, ALU.mult)
                last.then_inc(norm_ready, 1)
                dve.wait_ge(norm_root, 2 * r + 1)
                TT(rg[0], rg[0], ig[0], ALU.mult)
                dve.wait_ge(norm_root, 2 * r + 2)
                TT(rg[1], rg[1], ig[1], ALU.mult)
                dve.drain()
                nc.vector.tensor_tensor_scan(out=ig[0], data0=ag[0], data1=rg[0], initial=0.0, op0=ALU.mult, op1=ALU.add)
                nc.vector.tensor_tensor_scan(out=ig[1][:, TC - 1::-1], data0=ag[1][:, TC - 1::-1],
                                             data1=rg[1][:, TC - 1::-1], initial=0.0, op0=ALU.mult, op1=ALU.add)
                dve.drain()
                nc.vector.tensor_tensor_scan(out=ig[1][:, TA - 1:TC - 1:-1], data0=ag[1][:, TA - 1:TC - 1:-1],
                                             data1=rg[1][:, TA - 1:TC - 1:-1], initial=ig[1][:, 0:1],
                                             op0=ALU.mult, op1=ALU.add)
                dve.drain()
                TT(tmp[:, 0:T], ig[0][:, TC:TA], ig[1][:, TC:TA], ALU.add)
                dve.drain()
                yb_r = ybT[:, ds(r, 1), :].rearrange("p a n -> p (a n)")
                TT(yb_r, yb_r, tmp[:, 0:T], ALU.mult).then_inc(yb_ready, 1)
                dve.drain()

            convolve(0)
            with dve.Fori(0, R - 1) as r:
                lru_head(r, True)
            lru_head(R - 1, False)
            with dve.Fori(0, KD) as d:
                for sig, prod, read, dst, b0 in ((ga_read, ya_done, ya_read, sig_a, 2), (gb_read, yb_done, yb_read, sig_b, 6)):
                    dve.wait_ge(sig, d + 2)
                    dve.wait_ge(prod, d + 1)
                    for j in range(NH):
                        last = TT(dst[:, j * H:(j + 1) * H], dst[:, j * H:(j + 1) * H], bank[b0 + j][:, :], ALU.mult)
                    last.then_inc(read, 1)
                dve.drain()
                TT(merged[:, ds(d, 1), :].rearrange("p a n -> p (a n)"), sig_a, sig_b, ALU.add).then_inc(merge_done, 1)
            dve.wait_ge(gate1_loaded, 16 * 2)
            TT(bout_row, bout_row, gate1_row, ALU.mult).then_inc(bout_gated, 1)
            dve.wait_ge(rows_loaded, 16 * 3)
            STT(gain2_row, gain2_row, 1.0, norm2_row, ALU.add, ALU.mult)

            def residual(i):
                u = i % 2
                dve.wait_ge(mix_done, i + 3)
                for j in range(2):
                    TT(mix_tmp[:, j * H:(j + 1) * H], bank[2 * u + j][:, :], gate1_row[:, j * H:(j + 1) * H], ALU.mult)
                dve.drain()
                dve.wait_ge(bias_added, i + 1)
                TT(xs[:, i, :], xs[:, i, :], mix_tmp, ALU.add).then_inc(x1_ready, 1)
                dve.drain()

            def front_norm(i):
                dve.wait_ge(sq2_done, i + 1)
                TS(small[:, 1:2], small[:, 0:1], 1.0 / D, EPS, ALU.mult, ALU.add).then_inc(mean2_done, 1)
                dve.wait_ge(root2_done, i + 1)
                nc.vector.reciprocal(small[:, 2:3], small[:, 1:2])
                dve.drain()
                dve.wait_ge(h2_transposed, i + 1)
                STT(h2_next, x1_front, small[:, 2:3], gain2_row, ALU.mult, ALU.mult)
                dve.drain()
                TT(h2_next, h2_next, shift2_row, ALU.add).then_inc(h2_ready, 1)

            def top16(vals, rep, val_out, idx_out):
                nc.vector.max(val_out[:, 0:8], vals)
                dve.drain()
                nc.vector.max_index(idx_out[:, 0:8], val_out[:, 0:8], vals)
                nc.vector.match_replace(out=rep, in_to_replace=val_out[:, 0:8], in_values=vals, imm_value=NEG)
                dve.drain()
                nc.vector.max(val_out[:, 8:16], rep)
                dve.drain()
                nc.vector.max_index(idx_out[:, 8:16], val_out[:, 8:16], rep)

            def pick_keys(f):
                dve.wait_ge(score_done, f + 1)
                nc.vector.tensor_copy(s_sb[:, :, :].rearrange("p a n -> p (a n)"), bank[6][:, 0:2 * NK])\
                    .then_inc(score_copied, 1)
                dve.drain()
                for p in range(2):
                    top16(s_sb[:, p, :], s_rep[:, :], key_val[:, p, :], key_idx[:, p, :])
                dve.drain()

            def pick_experts(f):
                nc.vector.tensor_copy(key_idxf[:, :, :], key_idx[:, :, :])
                TT(cand[:, :, :], key_val[:, 0, :].unsqueeze(2).to_broadcast([P, TOPK, TOPK]),
                   key_val[:, 1, :].unsqueeze(1).to_broadcast([P, TOPK, TOPK]), ALU.add)
                dve.drain()
                top16(cand[:, :, :].rearrange("p a b -> p (a b)"), cand_rep[:, :, :].rearrange("p a b -> p (a b)"),
                      top_val[:, :], top_pos[:, :])
                TS(soft[:, 0:1], top_val[:, 0:1], -1.0, None, ALU.mult).then_inc(max_ready, 1)
                dve.drain()
                TS(top_ab[:, 0, :], top_pos[:, :], 4, None, ALU.logical_shift_right)
                TS(top_ab[:, 1, :], top_pos[:, :], 15, None, ALU.bitwise_and)
                dve.drain()
                nc.vector.tensor_copy(top_abf[:, :, :], top_ab[:, :, :])
                dve.drain()
                for p in range(2):
                    TT(cand_rep[:, :, :], top_abf[:, p, :].unsqueeze(2).to_broadcast([P, TOPK, TOPK]),
                       iota.unsqueeze(1).to_broadcast([P, TOPK, TOPK]), ALU.is_equal)
                    dve.drain()
                    TT(cand_rep[:, :, :], cand_rep[:, :, :], key_idxf[:, p, :].unsqueeze(1).to_broadcast([P, TOPK, TOPK]),
                       ALU.mult)
                    dve.drain()
                    nc.vector.tensor_reduce(picked[:, p, :], cand_rep[:, :, :], AXX, ALU.add)
                    dve.drain()
                STT(eidx[:, ds(f * TOPK, TOPK)], picked[:, 0, :], float(NK), picked[:, 1, :], ALU.mult, ALU.add)
                dve.wait_ge(exp_done, f + 1)
                nc.vector.reciprocal(soft[:, 2:3], soft[:, 1:2])
                dve.drain()
                TS(gates[:, ds(f * TOPK, TOPK)], top_exp[:, :], soft[:, 2:3], None, ALU.mult).then_inc(picks_done, 1)
                dve.drain()

            def dot_batch(j, b):
                for k in range(b * BATCH, (b + 1) * BATCH):
                    dve.wait_ge(landed[k % RING], 16 * (TOPK // RING * j + k // RING + 1))
                    last = STT(dot_junk[:, k % 2, :], ring[k % RING][:, 0:D], 1.0, h2_cur, ALU.mult, ALU.mult,
                               accum_out=dots[:, k:k + 1])
                    if k % BATCH == BATCH - 1:
                        last.then_inc(dots_done, 1)
                    if k % 2:
                        dve.drain()

            def finish(i):
                dve.wait_ge(acc_copied, i + 2)
                TT(acc_sb, acc_sb, gate2_row, ALU.mult)
                dve.drain()
                TT(acc_sb, acc_sb, x1_end, ALU.add)
                dve.drain()
                STT(dot_junk[:, 0, :], acc_sb, 1.0, acc_sb, ALU.mult, ALU.mult, accum_out=small[:, 3:4])
                dve.drain()
                TS(small[:, 4:5], small[:, 3:4], 1.0 / D, EPS, ALU.mult, ALU.add).then_inc(mean3_done, 1)
                dve.wait_ge(root3_done, i + 1)
                nc.vector.reciprocal(small[:, 5:6], small[:, 4:5])
                dve.drain()
                STT(acc_sb, acc_sb, small[:, 5:6], final_row, ALU.mult, ALU.mult).then_inc(out_ready, 1)

            def head(j, front):
                for b in range(NB - 1):
                    dot_batch(j, b)
                if front:
                    pick_keys(j + AHEAD)
                dot_batch(j, NB - 1)
                if front:
                    pick_experts(j + AHEAD)

            def tile_body(i, first, last):
                nc.vector.tensor_copy(h2_cur, h2_next)
                dve.drain()
                with dve.Fori(0, END_AT) as h:
                    head(i * PH + h, True)
                if not first:
                    finish(i - 1)
                nc.vector.tensor_copy(x1_end, x1_front).then_inc(x1_carried, 1)
                dve.drain()
                with dve.Fori(END_AT, PH - AHEAD) as h:
                    head(i * PH + h, True)
                if not last:
                    front_norm(i + 1)
                with dve.Fori(PH - AHEAD, PH) as h:
                    head(i * PH + h, not last)

            residual(0)
            residual(1)
            front_norm(0)
            for i in range(2, NT // 2 + 1):
                residual(i)
            for f in range(AHEAD):
                pick_keys(f)
                pick_experts(f)
                residual(NT // 2 + 1 + f)
            residual(NT - 1)
            tile_body(0, True, False)
            dve.wait_ge(late_rows_loaded, 16 * 2)
            with dve.Fori(1, NT - 1) as i:
                tile_body(i, False, False)
            tile_body(NT - 1, False, True)
            finish(NT - 1)

        @block.tensor
        def _(pe):
            mm = nc.tensor.matmul
            pe.wait_ge(silu_done, 1)
            for c in range(ME):
                u = c % 2
                pe.wait_ge(w_mod_loaded[u], 16 * (c // 2 + 1))
                if c >= 2:
                    pe.wait_ge(mod_rows, c - 1)
                for k in range(KD):
                    last = mm(bank[u][0:2, :], c_silu[:, k, :], w_mod_ring[:, u, k, :], start=(k == 0), stop=(k == KD - 1))
                last.then_inc(mod_matmul, 1)
            pe.wait_ge(mod_rows, ME)

            def transpose_tile(t, u):
                pe.wait_ge(xhat_ready, t + 1)
                for k in range(KD):
                    last = nc.tensor.transpose(bank[2 * u + k // 4][:, (k % 4) * P:(k % 4 + 1) * P],
                                               xhat[:, u, k * P:(k + 1) * P], ident)
                last.then_inc(x_transposed, 1)

            for u in range(2):
                transpose_tile(u, u)
            with pe.Fori(1, (NT + NTC) // 2) as n:
                for u in range(2):
                    t = 2 * n + u
                    pe.wait_ge(h_act, t - 1)
                    pe.wait_ge(h_dve, t - 1)
                    transpose_tile(t, u)
            pe.wait_ge(h_act, NT + NTC)
            pe.wait_ge(h_dve, NT + NTC)

            def project(dst, w, cols, k_n=KD, src=hT):
                for k in range(k_n):
                    last = mm(dst, w[:, k, :], src[:, k, cols], start=(k == 0), stop=(k == k_n - 1))
                return last

            with pe.Fori(0, G // 2) as n:
                for u in range(2):
                    g = 2 * n + u
                    pe.wait_ge(w_loaded[u], 16 * (n + 1))
                    for j in range(NH):
                        last = project(bank[j][:, :], w_a[u], slice(TC + j * H, TC + (j + 1) * H))
                    last.then_inc(zf_done, 1)
                    pe.wait_ge(mod_summed, 2 * g + 2)
                    for v in range(2):
                        mm(bank[2 + v][0:1, :], ones, mod_sum[:, v, :], start=True, stop=True)
                    pe.wait_ge(zf_copied, 2 * g + 2)
                    mm(bank[6][0:1, 2 * P:3 * P], zfT[:, T:T + 1], dft_fwd[:, 0:P], start=True, stop=True)
                    for t in range(NF):
                        mm(bank[4 + t][:, 0:2 * P], zfT[:, t * P:(t + 1) * P], dft_fwd, start=True, stop=False)
                        last = mm(bank[4 + t][:, 0:2 * P], zfT[:, H + t * P:H + (t + 1) * P], dft_rev,
                                  start=False, stop=True)
                    last.then_inc(pq_done, 1)
                    pe.wait_ge(pq_copied, 2 * g + 2)
            pe.wait_ge(mod_late, MC - ME)
            for t in range(NF):
                pe.wait_ge(dft_loaded[t % 2], 16 * (t // 2 + 1))
                dft = dft_t[t % 2]
                for g in range(G):
                    even, odd = bank[2 * g], bank[2 * g + 1]
                    p_t, q_t = PQ[:, t, g, 0:P], PQ[:, t, g, P:2 * P]
                    mid = pq_mid[:, g * P:(g + 1) * P]
                    mm(even[:, :], p_t, dft[:, 0:H], start=(t == 0), stop=False)
                    if t == NF - 1:
                        mm(even[:, :], mid, dft_mid[:, 0:H], start=False, stop=True)
                        mm(odd[:, 0:1], mid, dft_mid[:, H:H + 1], start=False, stop=False)
                    if t > 0:
                        mm(odd[:, 0:1], p_t, dft[:, H:H + 1], start=False, stop=False)
                    last = mm(odd[:, :], q_t, dft[:, H + 1:2 * H + 1], start=(t == 0), stop=(t == NF - 1))
                    if t == 0:
                        last = mm(odd[:, 0:1], p_t, dft[:, H:H + 1], start=False, stop=False)
                    if t == NF - 1:
                        last.then_inc(y_done, 1)
                if t < NF - 1:
                    last.then_inc(dft_used, 1)
            pe.wait_ge(y_copied, 2)
            def project_zx(r, u, loads):
                pe.wait_ge(w_loaded[u], 16 * (G // 2) + 32 * loads)
                pe.wait_ge(zx_copied, r + 1)
                project(bank[2][:, 0:TC], w_a[u], slice(0, TC))
                for j in range(NH):
                    last = project(bank[j][:, :], w_a[u], slice(TC + j * H, TC + (j + 1) * H))
                last.then_inc(zx_done, 1)

            def project_zy(r, u):
                pe.wait_ge(zy_read, r + 1)
                for j in range(NH):
                    last = project(bank[3 + j][:, :], w_b[u], slice(TC + j * H, TC + (j + 1) * H))
                last.then_inc(zy_done, 1)

            def lru_gates(r, u, loads):
                pe.wait_ge(gate_w_loaded[u], 16 * loads)
                pe.wait_ge(conv_done, r + 1)
                for m in range(4):
                    for p, (a, b) in enumerate([(0, TC), (TC, TC + H), (TC + H, TA)]):
                        pe.wait_ge(gate_read, 12 * r + 3 * m + p + 1)
                        mm(bank[5 + p][:, 0:b - a], w_g[u][:, m, :], xc[:, a:b], start=True, stop=True)\
                            .then_inc(gate_done, 1)

            project_zx(0, 0, 1)
            pe.wait_ge(y_copied, G)
            project_zy(0, 0)
            with pe.Fori(0, R // 2 - 1) as n:
                for u in range(2):
                    r = 2 * n + u
                    project_zx(r + 1, 1 - u, n + 1 + u)
                    lru_gates(r, u, n + 1)
                    project_zy(r + 1, 1 - u)
            project_zx(R - 1, 1, R // 2)
            lru_gates(R - 2, 0, R // 2)
            project_zy(R - 1, 1)

            def project_ga(d, u, n):
                pe.wait_ge(w_loaded[u], 16 * (G // 2) + 32 * (R // 2) + 64 * (n + 1))
                pe.wait_ge(ga_read, d + 1)
                for j in range(NH):
                    last = project(bank[j][:, :], w_a[u], slice(TC + j * H, TC + (j + 1) * H))
                last.then_inc(ga_done, 1)

            def merge_chunk(d, u, n_next=None):
                pe.wait_ge(ya_read, d + 1)
                for j in range(NH):
                    last = project(bank[2 + j][:, :], w_f[u], slice(j * H, (j + 1) * H), G, yT)
                last.then_inc(ya_done, 1)
                pe.wait_ge(gb_read, d + 1)
                for j in range(NH):
                    last = project(bank[4 + j][:, :], w_b[u], slice(TC + j * H, TC + (j + 1) * H))
                last.then_inc(gb_done, 1)
                if n_next is not None:
                    project_ga(d + 1, 1 - u, n_next)
                pe.wait_ge(yb_read, d + 1)
                pe.wait_ge(yb_ready, R + 1)
                for j in range(NH):
                    last = project(bank[6 + j][:, :], w_l[u], slice(j * H, (j + 1) * H), R, ybT)
                last.then_inc(yb_done, 1)

            pe.wait_ge(zx_copied, R + 1)
            project_ga(0, 0, 0)
            lru_gates(R - 1, 1, R // 2)
            pe.wait_ge(zy_read, R + 1)
            pe.wait_ge(gate_read, 12 * R + 3)
            pe.nop(nofuse=True)
            with pe.Fori(0, KD // 2 - 1) as n:
                for u in range(2):
                    merge_chunk(2 * n + u, u, n + u)
            merge_chunk(KD - 2, 0, KD // 2 - 1)
            merge_chunk(KD - 1, 1)
            pe.wait_ge(w_out_loaded, 16 * KD)
            pe.wait_ge(ga_read, KD + 1)
            pe.wait_ge(ya_read, KD + 1)

            def mix_half(i, u, j):
                if j == 0:
                    pe.wait_ge(tile_staged, i + 1)
                    pe.wait_ge(x1_ready, i + 1)
                for k in range(KD):
                    last = mm(bank[2 * u + j][:, :], merged_tile[u][:, k, :], w_out_k[k][:, j * H:(j + 1) * H],
                              start=(k == 0), stop=(k == KD - 1))
                if j == 1:
                    last.then_inc(mix_done, 1)

            with pe.Fori(0, NT // 4) as n:
                for u in range(2):
                    for j in range(2):
                        mix_half(2 * n + u, u, j)

            def transpose_h2(i, b0=2):
                pe.wait_ge(h2_ready, i + 1)
                pe.wait_ge(h2T_ready, i + 1)
                for k in range(KD):
                    last = nc.tensor.transpose(bank[b0 + k // 4][:, (k % 4) * P:(k % 4 + 1) * P],
                                               h2_next[:, k * P:(k + 1) * P], ident)
                last.then_inc(h2_transposed, 1)

            def query(f, h):
                pe.wait_ge(q_copied, f + 1)
                for k in range(KD):
                    last = mm(bank[4][:, 0:2 * P], h2T[:, k, :], wq_k[k][:, ds(h * 2 * P, 2 * P)],
                              start=(k == 0), stop=(k == KD - 1))
                last.then_inc(q_done, 1)

            def query_T(f):
                pe.wait_ge(q_copied, f + 2)
                pe.wait_ge(qT_copied, f + 1)
                for p in range(2):
                    last = nc.tensor.transpose(bank[5][:, p * P:(p + 1) * P], q_sb[:, p * P:(p + 1) * P], ident)
                last.then_inc(qT_done, 1)

            def scores(f, h):
                pe.wait_ge(qT_copied, f + 2)
                pe.wait_ge(score_copied, f + 1)
                for p in range(2):
                    last = mm(bank[6][:, p * NK:(p + 1) * NK], qT_sb[:, p, :],
                              keys_T[:, ds(2 * h + p, 1), :].rearrange("p a n -> p (a n)"), start=True, stop=True)
                last.then_inc(score_done, 1)

            def acc_edge(start):
                for c in range(2):
                    last = mm(bank[c][:, :], zero[:, :], shift2_row[:, c * H:(c + 1) * H], start=start, stop=not start,
                              skip_group_check=True)
                return last

            def add_rows(j, b):
                for k in range(b * BATCH, (b + 1) * BATCH):
                    pe.wait_ge(diag_done, TOPK * j + k + 1)
                    for c in range(2):
                        last = mm(bank[c][:, :], diag[:, k % BATCH, :], ring[k % RING][:, D + c * H:D + (c + 1) * H],
                                  start=False, stop=False, skip_group_check=True)
                    last.then_inc(ring_free, 1)

            def head(j, front, h):
                f = j + AHEAD
                if front:
                    query(f, h)
                add_rows(j, 0)
                if front:
                    query_T(f)
                add_rows(j, 1)
                if front:
                    scores(f, h)
                add_rows(j, 2)
                add_rows(j, 3)

            def tile_body(i, last, first=False):
                pe.wait_ge(acc_copied, i + 1)
                acc_edge(True)
                if first:
                    with pe.Fori(0, PH // 2 - AHEAD) as h:
                        head(h, True, h + AHEAD)
                    pe.wait_ge(wq_late_loaded, 16 * W_LATE)
                    pe.nop(nofuse=True)
                with pe.Fori(PH // 2 - AHEAD if first else 0, PH - AHEAD) as h:
                    head(i * PH + h, True, h + AHEAD)
                if not last:
                    transpose_h2(i + 1)
                    pe.wait_ge(h2T_ready, i + 3)
                    pe.nop(nofuse=True)
                with pe.Fori(0, AHEAD) as h:
                    head(i * PH + PH - AHEAD + h, not last, h)
                acc_edge(False).then_inc(acc_done, 1)

            pe.wait_ge(gb_read, KD + 1)
            pe.wait_ge(yb_read, KD + 1)
            transpose_h2(0, 4)
            mix_half(NT // 2, 0, 0)
            pe.wait_ge(h2T_ready, 2)
            pe.wait_ge(wq_loaded, 16 * (KD + 1))
            query(0, 0)
            mix_half(NT // 2, 0, 1)
            query_T(0)
            mix_half(NT // 2 + 1, 1, 0)
            scores(0, 0)
            query(1, 1)
            mix_half(NT // 2 + 1, 1, 1)
            query_T(1)
            mix_half(NT // 2 + 2, 0, 0)
            scores(1, 1)
            mix_half(NT // 2 + 2, 0, 1)
            for j in range(2):
                mix_half(NT - 1, 1, j)
            pe.wait_ge(x1_ready, NT + 2)
            tile_body(0, False, first=True)
            with pe.Fori(1, NT - 1) as i:
                tile_body(i, False)
            tile_body(NT - 1, True)


def kernel(**inputs):
    import numpy as np
    import concourse.bacc as bacc
    from concourse import mybir as my
    from concourse.bass_utils import run_bass_kernel_spmd as run

    P, GRID_W, TOPK = 128, 64, 16
    x = inputs["x"][0]
    T, D = x.shape
    KD = D // P
    cc = np.ascontiguousarray

    def cols(a):
        a = np.asarray(a)
        return np.moveaxis(a.reshape(a.shape[:-1] + (a.shape[-1] // P, P)), -1, 0)

    def chunks(w, width):
        k, n = w.shape
        return cc(w.reshape(k // P, P, n // width, width).transpose(2, 1, 0, 3))

    nf = D // 4
    omega = 1.0 / (10000.0 ** (np.arange(nf, dtype=np.float64) / nf))
    er = np.repeat(np.arange(T // GRID_W), GRID_W)[:, None] * omega[None]
    ec = np.tile(np.arange(GRID_W), P // GRID_W)[:, None] * omega[None]
    ang = 2 * np.pi * (np.outer(np.arange(P), np.arange(P)) % P) / P
    dft_c = np.concatenate([np.cos(ang), np.sin(ang)], axis=1) / np.sqrt(P)
    ang = 2 * np.pi * (np.outer(np.arange(T), np.arange(T)) % T) / T
    dft_t = np.stack([np.cos(ang), -np.sin(ang)], axis=1) / np.sqrt(T)
    dft_rev = np.concatenate([dft_c[:, :P], -dft_c[:, P:]], axis=1)
    iota = np.tile(np.arange(TOPK), (P, 1))

    wa, wx = inputs["lru_wa"][0], inputs["lru_wx"][0]
    ba, bx, lm = inputs["lru_ba"][0], inputs["lru_bx"][0], inputs["lru_lambda"][0]
    cw, cb = inputs["conv_w"][0], inputs["conv_b"][0]
    A = {
        "x": x, "ctx": inputs["ctx"][0],
        "pos_row": np.concatenate([np.sin(er), np.cos(er)], axis=1).astype(np.float32),
        "pos_col": np.concatenate([np.sin(ec), np.cos(ec)], axis=1).astype(np.float32),
        "consts": np.concatenate([np.eye(P), iota, np.ones((P, 1))], axis=1).astype(np.float32),
        "dft_time": np.concatenate([dft_t[:T // 2, 0, :T // 2 + 1], dft_t[:T // 2, 1, :T // 2]], axis=1)
        .reshape(T // 2 // P, P, T + 1).astype(np.float32),
        "dft_chan": np.concatenate([dft_c, dft_rev], axis=1).astype(np.float32),
        "dft_mid": dft_t[T // 2, 0, :T // 2 + 1][None].astype(np.float32),
        "c_cols": np.stack([cols(inputs["c"][0]), cols(inputs["c_ctx"])], axis=2),
        "w_mod": chunks(inputs["w_mod"][0], 512), "b_mod": inputs["b_mod"],
        "head_vecs": cols(np.stack([cw[0], cw[1], cw[2], cw[3], cb, ba[0], bx[0], ba[1], bx[1], lm[0], lm[1],
                                    inputs["norm1_g"][0]])),
        "w_in": chunks(inputs["w_in"][0], P),
        "wf": chunks(inputs["w_fourier"][0], P), "wl": chunks(inputs["w_lru_out"][0], P),
        "lru_gates": np.stack([wa[0], wx[0], wa[1], wx[1]]).transpose(1, 2, 0, 3),
        "w_out": inputs["w_out"][0], "b_out": inputs["b_out"], "norm2_g": inputs["norm2_g"],
        "final_g": np.asarray(inputs["final_g"])[None],
        "wq": inputs["peer_wq"][0],
        "keys": np.moveaxis(np.asarray(inputs["peer_keys"][0]).reshape(-1, inputs["peer_keys"].shape[3], P), 2, 0),
        "uv": np.concatenate([inputs["peer_u"][0], inputs["peer_v"][0]], axis=1),
    }
    A = {k: cc(v) for k, v in A.items()}
    nc = bacc.Bacc("TRN2", target_bir_lowering=False, num_devices=1)
    t_in = {k: nc.dram_tensor("in_" + k, v.shape, my.dt.from_np(v.dtype), kind="ExternalInput").ap() for k, v in A.items()}
    out = nc.dram_tensor("out_tokens", (T, D), my.dt.float32, kind="ExternalOutput").ap()
    mod_dram = nc.dram_tensor("modulation_rows", (2, 6 * D), my.dt.float32, kind="Internal").ap()
    x1_dram = nc.dram_tensor("x1_tokens", (T, D), my.dt.float32, kind="Internal").ap()
    build_block(nc, t_in, mod_dram, x1_dram, out)
    r = run(nc, [{"in_" + k: v for k, v in A.items()}], core_ids=[0])
    return r.results[0]["out_tokens"].reshape(1, T, D)
```
